# Optimizing a Trainium2 kernel written in Bass

```python
import math
import jax, jax.numpy as jnp
from jax import lax
import numpy as np

D_MODEL = 2048
BATCH = 1
SEQ = 256
DEPTH = 1

MLA_HEADS = 8
MLA_NOPE = 128
MLA_ROPE = 64
MLA_V = 128
KV_RANK = 512
ROPE_THETA = 10000.0
MLA_WIDTH = MLA_HEADS * MLA_V

DIFF_HEADS = 8
DIFF_QK = 64
DIFF_V = 2 * DIFF_QK
DIFF_WIDTH = DIFF_HEADS * DIFF_V

Q_BLOCK = 128
EPS = 1e-6
NEG_INF = -1e30

SPLITS = (
    MLA_HEADS * (MLA_NOPE + MLA_ROPE),
    KV_RANK,
    MLA_ROPE,
    DIFF_HEADS * 2 * DIFF_QK,
    DIFF_HEADS * 2 * DIFF_QK,
    DIFF_WIDTH,
    MLA_WIDTH,
    DIFF_WIDTH,
    D_MODEL,
    D_MODEL,
)
IN_WIDTH = sum(SPLITS)

kernel_name = "hybrid_mla_diffattn_gated_block"

def rms_norm(x, g):
    xf = x.astype(jnp.float32)
    y = xf * lax.rsqrt(jnp.mean(xf * xf, axis=-1, keepdims=True) + EPS)
    return (y * g.astype(jnp.float32)).astype(x.dtype)

def rope(x, pos):
    half = x.shape[-1] // 2
    inv = ROPE_THETA ** (-jnp.arange(half, dtype=jnp.float32) / half)
    ang = pos.astype(jnp.float32)[..., None] * inv
    cos = jnp.cos(ang)[:, :, None, :]
    sin = jnp.sin(ang)[:, :, None, :]
    x1 = x[..., :half].astype(jnp.float32)
    x2 = x[..., half:].astype(jnp.float32)
    out = jnp.concatenate([x1 * cos - x2 * sin, x2 * cos + x1 * sin], axis=-1)
    return out.astype(x.dtype)

def mla_attention(q_nope, q_rope, k_nope, k_rope, v):
    B, S, H, dv = v.shape
    scale = (MLA_NOPE + MLA_ROPE) ** -0.5
    k_idx = jnp.arange(S)

    def block(i):
        start = i * Q_BLOCK
        qn = lax.dynamic_slice_in_dim(q_nope, start, Q_BLOCK, axis=1)
        qr = lax.dynamic_slice_in_dim(q_rope, start, Q_BLOCK, axis=1)
        s = (jnp.einsum('bqhd,bkhd->bhqk', qn, k_nope).astype(jnp.float32)
             + jnp.einsum('bqhd,bkd->bhqk', qr, k_rope).astype(jnp.float32)) * scale
        q_idx = start + jnp.arange(Q_BLOCK)
        causal = k_idx[None, :] <= q_idx[:, None]
        s = jnp.where(causal[None, None], s, NEG_INF)
        p = jax.nn.softmax(s, axis=-1)
        return jnp.einsum('bhqk,bkhd->bqhd', p.astype(v.dtype), v)

    out = lax.map(block, jnp.arange(S // Q_BLOCK))
    return out.transpose(1, 0, 2, 3, 4).reshape(B, S, H, dv)

def diff_attention(q, k, v, pos, lam):
    B, S, H, dv = v.shape
    scale = DIFF_QK ** -0.5
    slopes = 2.0 ** (-8.0 * jnp.arange(1, H + 1, dtype=jnp.float32) / H)
    posf = pos.astype(jnp.float32)
    k_idx = jnp.arange(S)

    def block(i):
        start = i * Q_BLOCK
        qb = lax.dynamic_slice_in_dim(q, start, Q_BLOCK, axis=1)
        pq = lax.dynamic_slice_in_dim(posf, start, Q_BLOCK, axis=1)
        s = jnp.einsum('bqhcd,bkhcd->bchqk', qb, k).astype(jnp.float32) * scale
        dist = jnp.abs(pq[:, :, None] - posf[:, None, :])
        s = s - slopes[None, None, :, None, None] * dist[:, None, None]
        q_idx = start + jnp.arange(Q_BLOCK)
        causal = k_idx[None, :] <= q_idx[:, None]
        s = jnp.where(causal[None, None, None], s, NEG_INF)
        p = jax.nn.softmax(s, axis=-1)
        a = p[:, 0] - lam * p[:, 1]
        return jnp.einsum('bhqk,bkhd->bqhd', a.astype(v.dtype), v)

    out = lax.map(block, jnp.arange(S // Q_BLOCK))
    return out.transpose(1, 0, 2, 3, 4).reshape(B, S, H, dv)

def setup_inputs(seed: int = 0) -> dict:
    key = jax.random.key(seed)
    ks = jax.random.split(key, 20)
    f32 = jnp.float32

    def w(k, shape, fan_in, mult=1.0):
        return jax.random.normal(k, shape, f32) * (mult * fan_in ** -0.5)

    def gain(k, shape):
        return 1.0 + 0.02 * jax.random.normal(k, shape, f32)

    x = jax.random.normal(ks[0], (BATCH, SEQ, D_MODEL), f32)
    c = jax.random.normal(ks[1], (BATCH, D_MODEL), f32)
    positions = jnp.broadcast_to(jnp.arange(SEQ, dtype=jnp.int32)[None, :], (BATCH, SEQ))
    return {
        "x": x,
        "c": c,
        "positions": positions,
        "w_ada": w(ks[2], (DEPTH, D_MODEL, 3 * D_MODEL), D_MODEL, 0.2),
        "b_ada": 0.01 * jax.random.normal(ks[3], (DEPTH, 3 * D_MODEL), f32),
        "g_pre": gain(ks[4], (DEPTH, D_MODEL)),
        "w_in": w(ks[5], (DEPTH, D_MODEL, IN_WIDTH), D_MODEL),
        "g_kv": gain(ks[6], (DEPTH, KV_RANK)),
        "w_ukv": w(ks[7], (DEPTH, KV_RANK, MLA_HEADS * (MLA_NOPE + MLA_V)), KV_RANK),
        "lambda_q1": 0.1 * jax.random.normal(ks[8], (DEPTH, DIFF_QK), f32),
        "lambda_k1": 0.1 * jax.random.normal(ks[9], (DEPTH, DIFF_QK), f32),
        "lambda_q2": 0.1 * jax.random.normal(ks[10], (DEPTH, DIFF_QK), f32),
        "lambda_k2": 0.1 * jax.random.normal(ks[11], (DEPTH, DIFF_QK), f32),
        "g_subln": gain(ks[12], (DEPTH, DIFF_V)),
        "w_o_mla": w(ks[13], (DEPTH, MLA_WIDTH, D_MODEL), MLA_WIDTH),
        "w_o_diff": w(ks[14], (DEPTH, DIFF_WIDTH, D_MODEL), DIFF_WIDTH),
        "w_out": w(ks[15], (DEPTH, D_MODEL, D_MODEL), D_MODEL),
        "g_post": gain(ks[16], (DEPTH, D_MODEL)),
    }

def reference(x, c, positions, w_ada, b_ada, g_pre, w_in, g_kv, w_ukv,
              lambda_q1, lambda_k1, lambda_q2, lambda_k2, g_subln,
              w_o_mla, w_o_diff, w_out, g_post):
    B, S, _ = x.shape
    split_points = []
    acc = 0
    for n in SPLITS[:-1]:
        acc += n
        split_points.append(acc)

    for l in range(DEPTH):
        lambda_init = 0.8 - 0.6 * math.exp(-0.3 * l)

        ada = c @ w_ada[l] + b_ada[l]
        shift, scale, gate = jnp.split(ada, 3, axis=-1)
        h = rms_norm(x, g_pre[l]) * (1.0 + scale[:, None]) + shift[:, None]

        proj = h @ w_in[l]
        (q_mla, c_kv, k_rope, q_diff, k_diff, v_diff,
         gate_mla, gate_diff, mg_mla, mg_diff) = jnp.split(proj, split_points, axis=-1)

        q_mla = q_mla.reshape(B, S, MLA_HEADS, MLA_NOPE + MLA_ROPE)
        q_nope = q_mla[..., :MLA_NOPE]
        q_rope = rope(q_mla[..., MLA_NOPE:], positions)
        kv = rms_norm(c_kv, g_kv[l]) @ w_ukv[l]
        kv = kv.reshape(B, S, MLA_HEADS, MLA_NOPE + MLA_V)
        k_nope = kv[..., :MLA_NOPE]
        v_mla = kv[..., MLA_NOPE:]
        k_rope = rope(k_rope[:, :, None, :], positions)[:, :, 0]
        o_mla = mla_attention(q_nope, q_rope, k_nope, k_rope, v_mla).reshape(B, S, MLA_WIDTH)
        y_mla = (o_mla * jax.nn.silu(gate_mla)) @ w_o_mla[l]

        lam = (jnp.exp(jnp.sum(lambda_q1[l].astype(jnp.float32) * lambda_k1[l].astype(jnp.float32)))
               - jnp.exp(jnp.sum(lambda_q2[l].astype(jnp.float32) * lambda_k2[l].astype(jnp.float32)))
               + lambda_init)
        qd = q_diff.reshape(B, S, DIFF_HEADS, 2, DIFF_QK)
        kd = k_diff.reshape(B, S, DIFF_HEADS, 2, DIFF_QK)
        vd = v_diff.reshape(B, S, DIFF_HEADS, DIFF_V)
        o_diff = diff_attention(qd, kd, vd, positions, lam)
        o_diff = (rms_norm(o_diff, g_subln[l]) * (1.0 - lambda_init)).reshape(B, S, DIFF_WIDTH)
        y_diff = (o_diff * jax.nn.silu(gate_diff)) @ w_o_diff[l]

        merged = jax.nn.sigmoid(mg_mla) * y_mla + jax.nn.sigmoid(mg_diff) * y_diff
        y = merged @ w_out[l]

        x = x + gate[:, None] * rms_norm(y, g_post[l])
    return x


_drawn_inputs = setup_inputs


def setup_inputs(seed=0):
    import zlib

    import numpy as np

    out = dict(_drawn_inputs(seed))
    spreads = {}
    factors = {'b_ada': 4.638,
     'g_pre': 8.0,
     'g_kv': 8.0,
     'lambda_q1': 3.606,
     'lambda_k1': 193.784,
     'lambda_q2': 200.0,
     'g_subln': 143.095,
     'g_post': 80.458,
     'lambda_k2': 3.066}
    for name, (base, spread) in spreads.items():
        noise = np.random.default_rng([zlib.crc32(name.encode()), seed]).standard_normal(out[name].shape)
        drawn = base * np.exp(spread * noise) if base else spread * noise
        out[name] = __import__('jax').numpy.asarray(drawn.astype(out[name].dtype))
    for name, factor in factors.items():
        out[name] = (out[name] * factor).astype(out[name].dtype)
    return out
```

```python
from contextlib import ExitStack

import math

import concourse.bass as bass
from concourse import mybir

F32 = mybir.dt.float32
F32R = mybir.dt.float32r
BF16 = mybir.dt.bfloat16
I32 = mybir.dt.int32
ALU = mybir.AluOpType
ACT = mybir.ActivationFunctionType
AX_X = mybir.AxisListType.X

P = 128
D = 2048
SEQ = 256
TOK = SEQ // P
KT = D // P
CH = 512
HEADS = 8
NOPE = 128
ROPE = 64
HALF = ROPE // 2
QH = NOPE + ROPE
RANK = 512
DQK = 64
EPS = 1e-6
NEG_INF = -1e30
MLA_SCALE = (NOPE + ROPE) ** -0.5
DIFF_SCALE = DQK ** -0.5
LAMBDA_INIT = 0.8 - 0.6 * math.exp(-0.3 * 0)
SLOPES = [2.0 ** (-8.0 * (h + 1) / HEADS) for h in range(HEADS)]
ROPE_FREQ = [10000.0 ** (-i / HALF) for i in range(HALF)]

RING = 4
PIECE = 1024
KEYS = P + SEQ

C_Q, C_CKV, C_KR = 0, 1536, 2048
C_QD, C_KD, C_VD, C_GM, C_GD, C_MM, C_MD = 2112, 3136, 4160, 5184, 6208, 7232, 9280

V_SHIFT, V_SCALE, V_GPRE, V_C, V_GKV, V_GSUB = 0, 16, 32, 48, 64, 68
NVEC = 69

SQ_SCALE, SQ_CLAMP, SQ_LIMIT = 2.0 ** -40, 2.0 ** 25, 2.0 ** (128 - 80)

BIG_TURN = 2.0 * math.pi * 512
BIG_PARTS = (3216.0, 0.99072265625, 0.00015461970178876072)
TURN_PARTS = (6.283203125, -1.7814338207244873e-05, -3.4822063010864213e-09)
ROUND_MAGIC = 12582912.0


def make_jobs():
    jobs = [("ckv", 0), ("kr", 0), ("gate", 0)]
    jobs += [("ukv", i) for i in range(4)]
    jobs += [("gate", 1), ("gate", 2), ("gate", 3), ("vd", 0), ("vd", 1)]
    jobs += [("qd", 0), ("qd", 1), ("kd", 0), ("kd", 1)]
    for n in range(4):
        jobs += [("mm", n), ("wom", n)]
    for n in range(4):
        jobs += [("md", n), ("wod", n)]
    jobs += [("wout", n) for n in range(4)]
    return jobs


PIECES_OF = {"kr": 1, "ukv": 2, "wom": 4, "wod": 4}


def hybrid_block(nc, x, c, positions, w_ada, b_ada, g_pre, w_in, g_kv, w_ukv,
                 lambda_q1, lambda_k1, lambda_q2, lambda_k2, g_subln,
                 w_o_mla, w_o_diff, w_out, g_post, out):
    pieces = []
    for j in range(KT // 2):
        for ch in range(3):
            pieces.append((ch, "q", ch, j, j == 0, j == KT // 2 - 1))
    start, end = {0: 0, 1: 1, 2: 2}, {0: 21, 1: 22, 2: 23}
    acc_of = {("q", i): i for i in range(3)}
    for a, (kind, n) in enumerate(make_jobs(), start=3):
        m = PIECES_OF.get(kind, KT // 2)
        start[a], end[a] = len(pieces), len(pieces) + m - 1
        acc_of[kind, n] = a
        for i in range(m):
            pieces.append((a, kind, n, i, i == 0, i == m - 1))
    NP = len(pieces)
    first_piece = lambda kind, n: start[acc_of[kind, n]]
    last_piece = lambda kind, n: end[acc_of[kind, n]]

    def banks(a):
        return 2 * a if a < 3 else 2 * ((a + 1) % 2)

    in_cols = {"q": C_Q, "ckv": C_CKV, "gate": C_GM, "vd": C_VD, "qd": C_QD, "kd": C_KD,
               "mm": C_MM, "md": C_MD}

    def piece_source(kind, n, i):
        if kind == "kr":
            return w_in[0, :, C_KR:C_KR + ROPE].rearrange("(t p) n -> p t n", p=P)
        w, col = {"ukv": (w_ukv, n * CH), "wom": (w_o_mla, n * CH), "wod": (w_o_diff, n * CH),
                  "wout": (w_out, n * CH)}.get(kind) or (w_in, in_cols[kind] + n * CH)
        return w[0, 2 * i * P:2 * (i + 1) * P, col:col + CH].rearrange("(t p) n -> p t n", p=P)

    pe_after = {p: [] for p in range(-1, NP)}
    act_after = {p: [] for p in range(-1, NP)}
    dve_after = {p: [] for p in range(-1, NP)}

    with ExitStack() as ctx:
        KB = 1024
        at = [16512]

        def room(size):
            at[0] += size
            return at[0] - size

        def sb(name, shape, dt, offset=None):
            size = 4 if dt != BF16 else 2
            for s in shape[1:]:
                size *= s
            if offset is None:
                offset = room((size + 31) // 32 * 32)
            return nc.alloc_sbuf_tensor_at(name, shape, dt, offset=offset)

        w_raw = sb("w_raw", [P, RING, PIECE], F32)
        w_hi = sb("w_hi", [P, RING, PIECE], F32R)
        w_lo = sb("w_lo", [P, RING, PIECE], F32R)
        r_h_hi, r_h_lo, r_o_hi, r_o_lo = room(16 * KB), room(16 * KB), room(16 * KB), room(16 * KB)
        r_a, r_b, r_c = room(32 * KB), room(24 * KB), room(16 * KB)

        h_hi = sb("h_hi", [P, KT, SEQ], F32R, r_h_hi)
        h_lo = sb("h_lo", [P, KT, SEQ], F32R, r_h_lo)
        yg = sb("yg", [P, TOK, D], F32, r_h_hi)
        x_again = sb("x_again", [P, TOK, D], F32, r_h_lo)
        o_hi = sb("o_hi", [P, KT, SEQ], F32R, r_o_hi)
        o_lo = sb("o_lo", [P, KT, SEQ], F32R, r_o_lo)
        xnT = sb("xnT", [P, KT, SEQ], F32, r_o_hi)
        x_tok = sb("x_tok", [P, TOK, D], F32, r_o_lo)
        ckvT_hi = sb("ckvT_hi", [P, RANK // P, SEQ], F32R, r_o_hi + 8 * KB)
        ckvT_lo = sb("ckvT_lo", [P, RANK // P, SEQ], F32R, r_o_lo + 8 * KB)
        qnT = sb("qnT", [P, HEADS, SEQ], F32, r_a)
        qrT = sb("qrT", [P, HEADS // 2, SEQ], F32, r_a + 8 * KB)
        knT = sb("knT", [P, HEADS, SEQ], F32, r_a + 12 * KB)
        krT = sb("krT", [P, SEQ], F32, r_a + 20 * KB)
        v_mla = sb("v_mla", [P, TOK, HEADS, NOPE], F32, r_a + 21 * KB)
        merged = sb("merged", [P, TOK, D], F32, r_a)
        post_gain = sb("post_gain", [P, D], F32, r_a + 16 * KB)
        gate_ring = sb("gate_ring", [P, 2, PIECE], F32, r_a + 24 * KB)
        q_tok = sb("q_tok", [P, TOK, HEADS * QH], F32, r_b)
        qr_tok = sb("qr_tok", [P, TOK, HEADS, ROPE], F32, r_b + 12 * KB)
        kr_tok = sb("kr_tok", [P, TOK, ROPE], F32, r_b + 16 * KB)
        kr_dup = sb("kr_dup", [P, TOK, 2 * ROPE], F32, r_b + 17 * KB)
        rot_a = sb("rot_a", [P, HEADS, HALF], F32, r_b + 18 * KB)
        rot_b = sb("rot_b", [P, HEADS, HALF], F32, r_b + 19 * KB)
        lam_in = sb("lam_in", [P, 4, DQK], F32, r_b + 20 * KB)
        pos_row = sb("pos_row", [P, SEQ], I32, r_b + 21 * KB)
        angle = sb("angle", [P, 5, TOK * HALF], F32, r_b + 22 * KB)
        lam_prod = sb("lam_prod", [P, 2, DQK], F32, r_b + 23 * KB + 256)
        qdT = sb("qdT", [P, HEADS, SEQ], F32, r_b)
        kdT = sb("kdT", [P, HEADS, SEQ], F32, r_b + 8 * KB)
        v_diff = sb("v_diff", [P, TOK, HEADS * P], F32, r_b + 16 * KB)
        ada_ring = sb("ada_ring", [P, RING, 2, 2, 2 * P], F32, r_c)
        silu_gate = sb("silu_gate", [P, TOK, D], F32, r_c)
        m_hi = sb("m_hi", [P, KT, SEQ], F32R, r_b)
        m_lo = sb("m_lo", [P, KT, SEQ], F32R, r_b + 16 * KB)

        stage = sb("stage", [P, TOK, CH], F32)
        tmp = sb("tmp", [P, CH], F32)
        ada_acc = sb("ada_acc", [P, 2 * 2 * P], F32)
        r_p = room(2 * 2 * KEYS * 4)
        probs = sb("probs", [P, 2, 2, KEYS], F32, r_p)
        bias_gain = sb("bias_gain", [P, 2, CH], F32, r_p)
        probsT = sb("probsT", [P, KEYS], F32)
        o_gated = sb("o_gated", [P, TOK, P], F32)
        dist = sb("dist", [P, KEYS], F32)
        vec_rows = sb("vec_rows", [P, P], F32)
        cols = sb("cols", [P, NVEC + 3], F32)
        ident = sb("ident", [P, P], F32)
        ident_b = sb("ident_b", [P, P], BF16)
        causal_b = sb("causal_b", [P, P], BF16)
        causal_far = sb("causal_far", [P, P], F32)
        ones = sb("ones", [P, P], F32)
        freq = sb("freq", [P, HALF], F32)
        cos = sb("cos", [P, TOK, HALF], F32)
        sin = sb("sin", [P, TOK, HALF], F32)
        pos_q = sb("pos_q", [P, TOK], I32)
        pos_qf = sb("pos_qf", [P, TOK], F32)
        mod_gain = sb("mod_gain", [P, KT], F32)
        mod_shift = sb("mod_shift", [P, KT], F32)
        gain_tmp = sb("gain_tmp", [P, 2], F32)
        NR = 3 + HEADS
        R_X, R_CKV, R_HEAD, R_Y = 0, 1, 2, 2 + HEADS
        sumsq = sb("sumsq", [P, NR, TOK], F32)
        variance = sb("variance", [P, NR, TOK], F32)
        rstd = sb("rstd", [P, NR, TOK], F32)
        power = sb("power", [P, TOK], F32)
        in_range = sb("in_range", [P, TOK], F32)
        y_sq = sb("y_sq", [P, TOK, 4], F32)
        maxes = sb("maxes", [P, 2, 4], F32)
        neg_max = sb("neg_max", [P, 2, 4], F32)
        sums = sb("sums", [P, 2, 4], F32)
        recip = sb("recip", [P, 2, 4], F32)
        lam_dot = sb("lam_dot", [P, 2], F32)
        lam_exp = sb("lam_exp", [P, 2], F32)
        lam = sb("lam", [P, 1], F32)
        assert at[0] <= 229368, at[0]

        ps = ctx.enter_context(nc.psum_tensor("ps", [P, 8, CH], F32))

        def sem(name):
            return ctx.enter_context(nc.semaphore(name))

        raw_in = [sem(f"raw_in{i}") for i in range(RING)]
        ada_in = [sem(f"ada_in{i}") for i in range(RING)]
        gate_in = [sem(f"gate_in{i}") for i in range(2)]
        hi_done, lo_done, piece_used = sem("hi_done"), sem("lo_done"), sem("piece_used")
        x_in, vec_in, pos_in, lam_ld = sem("x_in"), sem("vec_in"), sem("pos_in"), sem("lam_ld")
        consts = sem("consts")
        cols_T, cols_ready = sem("cols_T"), sem("cols_ready")
        x_sq, rstd_ready, xn_ready = sem("x_sq"), sem("rstd_ready"), sem("xn_ready")
        var_ready = sem("var_ready")
        xT_made, xT_copied = sem("xT_made"), sem("xT_copied")
        ada_used, ada_acc_ready, ada_summed, mod_ready = (
            sem("ada_used"), sem("ada_acc_ready"), sem("ada_summed"), sem("mod_ready"))
        h_hi_ready, h_lo_ready = sem("h_hi_ready"), sem("h_lo_ready")
        acc_read_act, acc_read_dve = sem("acc_read_act"), sem("acc_read_dve")
        tr_made, tr_copied = sem("tr_made"), sem("tr_copied")
        angles_ready, cossin_ready = sem("angles_ready"), sem("cossin_ready")
        lam_dots, lam_exps = sem("lam_dots"), sem("lam_exps")
        ckv_scaled, ckv_hi, ckv_lo = sem("ckv_scaled"), sem("ckv_hi"), sem("ckv_lo")
        scores_ready, scores_read, max_ready, exps_done = (
            sem("scores_ready"), sem("scores_read"), sem("max_ready"), sem("exps_done"))
        weights_ready = sem("weights_ready")
        pT_made, pT_copied = sem("pT_made"), sem("pT_copied")
        pv_done, head_sq, o_gated_ready = sem("pv_done"), sem("head_sq"), sem("o_gated_ready")
        oT_made, o_hi_ready, o_lo_ready = sem("oT_made"), sem("o_hi_ready"), sem("o_lo_ready")
        sig_ready, merged_ready = sem("sig_ready"), sem("merged_ready")
        mT_made, m_hi_ready, m_lo_ready = sem("mT_made"), sem("m_hi_ready"), sem("m_lo_ready")
        gate_used, gate_acc_ready, gate_summed, gg_ready, bias_in = (
            sem("gate_used"), sem("gate_acc_ready"), sem("gate_summed"), sem("gg_ready"), sem("bias_in"))
        x_again_in, out_ready, out_done = (
            sem("x_again_in"), sem("out_ready"), sem("out_done"))
        y_sums, root_ready = sem("y_sums"), sem("root_ready")
        dve_step, pool_step = sem("dve_step"), sem("pool_step")

        block = ctx.enter_context(nc.Block())

        by_dve = [a for a in range(3, 3 + len(make_jobs())) if pieces[start[a]][1] in ("wom", "wod")]
        by_act = [a for a in range(3 + len(make_jobs())) if a not in by_dve]

        def out_bank(m):
            return ps[:, 5, 0:SEQ] if m < HEADS else ps[:, 7, SEQ:2 * SEQ]

        def wait_acc_read(eng, a):
            if a in by_dve:
                eng.wait_ge(acc_read_dve, by_dve.index(a) + 1)
            else:
                eng.wait_ge(acc_read_act, by_act.index(a) + 1)
            if pieces[start[a]][1] == "wout":
                eng.wait_ge(acc_read_dve, len(by_dve) + pieces[start[a]][2] + 1)

        MLA0 = first_piece("gate", 1) + 3
        DIFF0 = first_piece("mm", 0) + 2
        mla_at = [(MLA0 + 4 * h, MLA0 + 4 * h + 3, MLA0 + 4 * h + 5, MLA0 + 4 * h + 7) for h in range(HEADS)]
        diff_at = [(DIFF0 + 5 * h, DIFF0 + 5 * h + 6, DIFF0 + 5 * h + 8, DIFF0 + 5 * h + 11) for h in range(HEADS)]

        G_QN, G_QR, G_CKV, G_KR, G_KN, G_D = 0, 4, 6, 8, 9, 13
        N_GROUPS = G_D + 8

        @block.sync
        def _(sp):
            sp.dma_start(vec_rows[V_C:V_C + KT, :], c[0, :].rearrange("(r n) -> r n", n=P)).then_inc(vec_in, 16)
            for row, n, v in ((V_SHIFT, KT, b_ada[0, 0:D]), (V_SCALE, KT, b_ada[0, D:2 * D]),
                              (V_GPRE, KT, g_pre[0, :]), (V_GKV, RANK // P, g_kv[0, :]),
                              (V_GSUB, 1, g_subln[0, :])):
                sp.dma_start(vec_rows[row:row + n, :], v.rearrange("(r n) -> r n", n=P)).then_inc(vec_in, 16)
            for t in range(TOK):
                sp.dma_start(x_tok[:, t, :], x[0, t * P:(t + 1) * P, :]).then_inc(x_in, 16)

            def load_ada(j):
                for q in range(KT // 2):
                    n = j * (KT // 2) + q
                    if n >= RING:
                        sp.wait_ge(ada_used, n - RING + 1)
                    for s in range(2):
                        col = s * D + j * 2 * P
                        sp.dma_start(ada_ring[:, n % RING, :, s, :],
                                     w_ada[0, 2 * q * P:2 * (q + 1) * P, col:col + 2 * P]
                                     .rearrange("(t p) n -> p t n", p=P)).then_inc(ada_in[n % RING], 16)

            def load_gate(n, i):
                k = n * (KT // 2) + i
                if k >= 2:
                    sp.wait_ge(gate_used, k - 1)
                else:
                    sp.wait_ge(o_lo_ready, HEADS)
                col = 2 * D + n * CH
                sp.dma_start(gate_ring[:, k % 2, :].rearrange("p (t n) -> p t n", t=2),
                             w_ada[0, 2 * i * P:2 * (i + 1) * P, col:col + CH]
                             .rearrange("(t p) n -> p t n", p=P)).then_inc(gate_in[k % 2], 16)

            load_ada(0)
            for p, (a, kind, n, i, first, last) in enumerate(pieces):
                if kind == "q" and n == 0 and i + 1 < KT // 2:
                    load_ada(i + 1)
                if p >= RING:
                    sp.wait_ge(lo_done, p - RING + 1)
                dst = w_raw[:, p % RING, :]
                dst = dst.rearrange("p (t n) -> p t n", n=ROPE if kind == "kr" else CH)
                sp.dma_start(dst, piece_source(kind, n, i)).then_inc(raw_in[p % RING], 16)
                if p == 0:
                    sp.dma_start(pos_row[:, :], positions[0, :].partition_broadcast(P)).then_inc(pos_in, 16)
                    with nc.allow_non_contiguous_dma(reason="256 positions, once"):
                        sp.dma_start(pos_q[:, :], positions[0, :].rearrange("(t p) -> p t", p=P)).then_inc(pos_in, 16)
                    for k, v in enumerate((lambda_q1, lambda_k1, lambda_q2, lambda_k2)):
                        sp.dma_start(lam_in[:, k, :], v[0, :].partition_broadcast(P)).then_inc(lam_ld, 16)
                if kind == "md":
                    load_gate(n, i)
                    if i == 0:
                        if n == 0:
                            sp.wait_ge(pT_made, 2 * HEADS)
                        else:
                            sp.wait_ge(gg_ready, n)
                        sp.dma_start(bias_gain[:, 0, :], b_ada[0, 2 * D + n * CH:2 * D + (n + 1) * CH]
                                     .partition_broadcast(P)).then_inc(bias_in, 16)
                        sp.dma_start(bias_gain[:, 1, :], g_post[0, n * CH:(n + 1) * CH]
                                     .partition_broadcast(P)).then_inc(bias_in, 16)
                if kind == "wout" and n == 0 and i == 0:
                    sp.wait_ge(piece_used, last_piece("md", 3) + 1)
                    for t in range(TOK):
                        sp.dma_start(x_again[:, t, :], x[0, t * P:(t + 1) * P, :]).then_inc(x_again_in, 16)
            for k in range(2 * TOK):
                t, half = k // 2, k % 2
                sp.wait_ge(out_ready, k + 1)
                sp.dma_start(out[0, t * P:(t + 1) * P, half * (D // 2):(half + 1) * (D // 2)],
                             yg[:, t, half * (D // 2):(half + 1) * (D // 2)]).then_inc(out_done, 16)
            sp.wait_ge(out_done, 16 * 2 * TOK)

        @block.gpsimd
        def _(pool):
            nc.gpsimd.memset(ident[:, :], 0.0).then_inc(pool_step, 1)
            pool.wait_ge(pool_step, 1)
            nc.gpsimd.affine_select(out=ident[:, :], in_=ident[:, :], compare_op=ALU.not_equal, fill=1.0,
                                    base=0, pattern=[[-1, P]], channel_multiplier=1).then_inc(consts, 1)
            nc.gpsimd.memset(power[:, :], -0.5).then_inc(pool_step, 1)
            nc.gpsimd.memset(ones[:, :], 1.0).then_inc(consts, 1)
            nc.gpsimd.memset(ident_b[:, :], 0.0).then_inc(pool_step, 1)
            nc.gpsimd.memset(causal_b[:, :], 0.0).then_inc(pool_step, 1)
            nc.gpsimd.memset(causal_far[:, :], 0.0).then_inc(pool_step, 1)
            for i, f in enumerate(ROPE_FREQ):
                fill = nc.gpsimd.memset(freq[:, i:i + 1], f)
            fill.then_inc(consts, 1)

            def inverse_root(k, need, count, width):
                pool.wait_ge(need, count)
                nc.gpsimd.tensor_scalar(variance[:, k, :], sumsq[:, k, :], 1.0 / width, EPS,
                                        ALU.mult, ALU.add).then_inc(var_ready, 1)
                pool.wait_ge(var_ready, k + 1)
                nc.gpsimd.tensor_tensor(rstd[:, k, :], variance[:, k, :], power[:, :], ALU.pow).then_inc(rstd_ready, 1)

            pool.wait_ge(pool_step, 2)
            inverse_root(R_X, x_sq, TOK, D)
            pool.wait_ge(pool_step, 5)
            nc.gpsimd.affine_select(out=ident_b[:, :], in_=ident_b[:, :], compare_op=ALU.not_equal, fill=1.0,
                                    base=0, pattern=[[-1, P]], channel_multiplier=1).then_inc(consts, 1)
            nc.gpsimd.affine_select(out=causal_b[:, :], in_=causal_b[:, :], compare_op=ALU.is_ge,
                                    fill=NEG_INF / MLA_SCALE, base=0, pattern=[[-1, P]],
                                    channel_multiplier=1).then_inc(consts, 1)
            nc.gpsimd.affine_select(out=causal_far[:, :], in_=causal_far[:, :], compare_op=ALU.is_ge,
                                    fill=-NEG_INF / min(SLOPES), base=0, pattern=[[-1, P]],
                                    channel_multiplier=1).then_inc(consts, 1)
            inverse_root(R_CKV, acc_read_act, by_act.index(acc_of["ckv", 0]) + 1, RANK)
            for h in range(HEADS):
                k = R_HEAD + h
                pool.wait_ge(head_sq, h + 1)
                nc.gpsimd.tensor_scalar(in_range[:, :], sumsq[:, k, :], SQ_LIMIT, SQ_SCALE, ALU.is_lt, ALU.mult)
                nc.gpsimd.tensor_scalar(variance[:, k, :], sumsq[:, k, :], 1.0 / P, EPS * SQ_SCALE ** 2,
                                        ALU.mult, ALU.add).then_inc(var_ready, 1)
                pool.wait_ge(var_ready, k + 1)
                nc.gpsimd.tensor_tensor(variance[:, k, :], variance[:, k, :], power[:, :], ALU.pow).then_inc(root_ready, 1)
                pool.wait_ge(root_ready, h + 1)
                nc.gpsimd.tensor_tensor(rstd[:, k, :], variance[:, k, :], in_range[:, :], ALU.mult).then_inc(rstd_ready, 1)
                pool.wait_ge(rstd_ready, k + 1)
            inverse_root(R_Y, y_sums, 1, D)

        act = nc.scalar

        def act_copy_group(g, dst):
            def run(eng):
                eng.wait_ge(tr_made, g + 1)
                act.copy(dst, ps[:, 4 + g % 4, 0:dst_size(dst)]).then_inc(tr_copied, 1)
            return run

        def dst_size(ap):
            n = 1
            for s in ap.shape[1:]:
                n *= s
            return n

        def act_read(a, body):
            def run(eng):
                eng.wait_ge(piece_used, end[a] + 1)
                body(eng, banks(a)).then_inc(acc_read_act, 1)
            return run

        def read_q(n):
            def body(eng, b):
                for t in range(TOK):
                    ins = act.copy(q_tok[:, t, n * CH:(n + 1) * CH], ps[:, b + t, :])
                return ins
            return body

        def read_ckv(eng, b):
            for t in range(TOK):
                act.activation(act_junk[:, t, :], ps[:, b + t, :], ACT.Square, accum_out=sumsq[:, R_CKV, t:t + 1])
                ins = act.copy(stage[:, t, :], ps[:, b + t, :])
            return ins

        def read_kr(eng, b):
            for t in range(TOK):
                ins = act.copy(kr_tok[:, t, :], ps[:, b + t, 0:ROPE])
            return ins

        def read_gate(n):
            def body(eng, b):
                for t in range(TOK):
                    ins = act.activation(silu_gate[:, t, n * CH:(n + 1) * CH], ps[:, b + t, :], ACT.Silu)
                return ins
            return body

        def read_ukv(n):
            def body(eng, b):
                if n >= 2:
                    eng.wait_ge(tr_made, G_KN + n - 1)
                else:
                    eng.wait_ge(tr_made, G_CKV + 2)
                for t in range(TOK):
                    both = ps[:, b + t, :].rearrange("p (h w d) -> p h w d", h=2, w=2)
                    act.copy(stage[:, t, (n % 2) * 256:(n % 2) * 256 + 256].rearrange("p (h d) -> p h d", h=2),
                             both[:, :, 0, :])
                    ins = act.copy(v_mla[:, t, 2 * n:2 * n + 2, :], both[:, :, 1, :])
                return ins
            return body

        def read_vd(n):
            def body(eng, b):
                for t in range(TOK):
                    ins = act.copy(v_diff[:, t, n * CH:(n + 1) * CH], ps[:, b + t, :])
                return ins
            return body

        def read_qk(k):
            def body(eng, b):
                eng.wait_ge(tr_made, G_D + 2 * k)
                for t in range(TOK):
                    ins = act.copy(stage[:, t, :], ps[:, b + t, :])
                return ins
            return body

        def read_sigmoid(k):
            def body(eng, b):
                if k == 0:
                    eng.wait_ge(tr_made, N_GROUPS)
                else:
                    eng.wait_ge(acc_read_dve, k)
                for t in range(TOK):
                    ins = act.activation(stage[:, t, :], ps[:, b + t, :], ACT.Sigmoid)
                return ins
            return body

        def act_ckv_hi(eng):
            for g in range(2):
                eng.wait_ge(tr_made, G_CKV + g + 1)
                for b in range(2):
                    k = 2 * g + b
                    ins = act.activation(ckvT_hi[:, k, :], ps[:, 4 + (G_CKV + g) % 4, b * SEQ:(b + 1) * SEQ],
                                         ACT.Copy, scale=cols[:, V_GKV + k:V_GKV + k + 1])
                ins.then_inc(ckv_hi, 1)
            eng.wait_ge(ckv_lo, 2)
            act.copy(lam_dummy[:, 0:1], cols[:, 0:1]).then_inc(tr_copied, 2)

        lam_dummy = sb("lam_dummy", [P, 1], F32)

        def act_exps(m):
            def run(eng):
                eng.wait_ge(max_ready, m + 1)
                if m < HEADS:
                    if m >= 2:
                        eng.wait_ge(pT_made, m - 1)
                    for b, (lo, hi) in enumerate(((0, P), (P, KEYS))):
                        ins = act.activation(probs[:, m % 2, 0, lo:hi], ps[:, 4, lo:hi], ACT.Exp,
                                             bias=neg_max[:, m % 2, b:b + 1], scale=MLA_SCALE,
                                             accum_out=sums[:, m % 2, b:b + 1])
                else:
                    for b, (lo, hi) in enumerate(((0, P), (P, KEYS))):
                        for w in range(2):
                            s = 2 * b + w
                            ins = act.activation(probs[:, m % 2, w, lo:hi], probs[:, m % 2, w, lo:hi], ACT.Exp,
                                                 bias=neg_max[:, m % 2, s:s + 1], scale=DIFF_SCALE,
                                                 accum_out=sums[:, m % 2, s:s + 1])
                ins.then_inc(exps_done, 1)
            return run

        def act_copy_probs(m):
            def run(eng):
                eng.wait_ge(pT_made, m + 1)
                if m >= 1:
                    eng.wait_ge(pv_done, m)
                act.copy(probsT[:, :], ps[:, 6, 0:KEYS]).then_inc(pT_copied, 1)
            return run

        def act_o_hi(m):
            def run(eng):
                eng.wait_ge(oT_made, m + 1)
                scale = 1.0 if m < HEADS else cols[:, NVEC:NVEC + 1]
                act.activation(o_hi[:, m, :], out_bank(m), ACT.Copy, scale=scale).then_inc(o_hi_ready, 1)
            return run

        def act_m_hi(n):
            def run(eng):
                eng.wait_ge(mT_made, n + 1)
                act.copy(m_hi[:, 4 * n:4 * n + 4, :], ps[:, 4:6, :]).then_inc(m_hi_ready, 1)
            return run

        def read_y(n):
            def body(eng, b):
                eng.wait_ge(acc_read_act, by_act.index(acc_of["wout", n]))
                for t in range(TOK):
                    ins = act.activation(act_junk[:, t, :], ps[:, b + t, :], ACT.Square, accum_out=y_sq[:, t, n:n + 1])
                return ins
            return body

        act_junk = sb("act_junk", [P, TOK, CH], F32, r_o_hi)

        for n in range(3):
            act_after[24 + n].append(act_read(n, read_q(n)))
        e = last_piece("ckv", 0)
        act_after[e + 3].append(act_read(acc_of["ckv", 0], read_ckv))
        act_after[last_piece("kr", 0) + 3].append(act_read(acc_of["kr", 0], read_kr))
        for n in range(4):
            act_after[last_piece("gate", n) + 3].append(act_read(acc_of["gate", n], read_gate(n)))
            act_after[last_piece("ukv", n) + 3].append(act_read(acc_of["ukv", n], read_ukv(n)))
        for n in range(2):
            act_after[last_piece("vd", n) + 3].append(act_read(acc_of["vd", n], read_vd(n)))
        for k, (kind, n) in enumerate((("qd", 0), ("qd", 1), ("kd", 0), ("kd", 1))):
            act_after[last_piece(kind, n) + 3].append(act_read(acc_of[kind, n], read_qk(k)))
        for n in range(4):
            act_after[last_piece("mm", n) + 3].append(act_read(acc_of["mm", n], read_sigmoid(n)))
            act_after[last_piece("md", n) + 3].append(act_read(acc_of["md", n], read_sigmoid(4 + n)))
            act_after[min(last_piece("wout", n) + 3, NP - 1)].append(act_read(acc_of["wout", n], read_y(n)))

        q_end = 24
        group_at = {}
        for g in range(4):
            group_at[G_QN + g] = (q_end + 4 + g // 2, q_end + 8 + g // 2)
        for g in range(2):
            group_at[G_QR + g] = (q_end + 9, q_end + 13)
            group_at[G_CKV + g] = (last_piece("ckv", 0) + 6, last_piece("ckv", 0) + 9)
        group_at[G_KR] = (last_piece("kr", 0) + 7, last_piece("kr", 0) + 10)
        for n in range(4):
            group_at[G_KN + n] = (last_piece("ukv", n) + 2, last_piece("ukv", n) + 6)
        for k, (kind, n) in enumerate((("qd", 0), ("qd", 1), ("kd", 0), ("kd", 1))):
            for g in range(2):
                group_at[G_D + 2 * k + g] = (last_piece(kind, n) + 2, last_piece(kind, n) + 5)
        for g in range(N_GROUPS):
            at_pe, at_act = group_at[g]
            if g < G_QR:
                dst = qnT[:, 2 * g:2 * g + 2, :]
            elif g < G_CKV:
                dst = qrT[:, 2 * (g - G_QR):2 * (g - G_QR) + 2, :]
            elif g < G_KR:
                if g == G_CKV:
                    act_after[at_act].append(act_ckv_hi)
                continue
            elif g == G_KR:
                dst = krT[:, :]
            elif g < G_D:
                dst = knT[:, 2 * (g - G_KN):2 * (g - G_KN) + 2, :]
            else:
                k = g - G_D
                dst = (qdT if k < 4 else kdT)[:, 2 * (k % 4):2 * (k % 4) + 2, :]
            act_after[at_act].append(act_copy_group(g, dst))
        for h in range(HEADS):
            s, t, v, g = mla_at[h]
            act_after[s + 5].append(act_exps(h))
            act_after[t + 4].append(act_copy_probs(h))
            act_after[g + 4].append(act_o_hi(h))
            s, t, v, g = diff_at[h]
            act_after[s + 6].append(act_exps(HEADS + h))
            act_after[t + 4].append(act_copy_probs(HEADS + h))
            act_after[g + 4].append(act_o_hi(HEADS + h))
        merge_at = [last_piece("wod", n) + 5 for n in range(4)]
        for n in range(4):
            act_after[merge_at[n] + 4].append(act_m_hi(n))

        @block.scalar
        def _(eng):
            for t in range(TOK):
                eng.wait_ge(x_in, 16 * TOK)
                act.activation(xnT[:, 0:KT // 2, :].rearrange("p k s -> p (k s)"), x_tok[:, t, :], ACT.Square,
                               accum_out=sumsq[:, R_X, t:t + 1]).then_inc(x_sq, 1)
                eng.wait_ge(x_sq, t + 1)
            eng.wait_ge(cols_T, 1)
            act.copy(cols[:, 0:NVEC], ps[:, 7, 0:NVEC]).then_inc(cols_ready, 1)
            for g in range(KT // 2):
                eng.wait_ge(xT_made, g + 1)
                act.copy(xnT[:, 2 * g:2 * g + 2, :], ps[:, 6 + g % 2, :]).then_inc(xT_copied, 1)

            def make_h_hi(j):
                eng.wait_ge(mod_ready, j + 1)
                for k in (2 * j, 2 * j + 1):
                    ins = act.activation(h_hi[:, k, :], xnT[:, k, :], ACT.Identity,
                                         bias=mod_shift[:, k:k + 1], scale=mod_gain[:, k:k + 1])
                ins.then_inc(h_hi_ready, 1)

            eng.wait_ge(xT_copied, KT // 2)
            make_h_hi(0)
            for p, (a, kind, n, i, first, last) in enumerate(pieces):
                eng.wait_ge(raw_in[p % RING], 16 * (p // RING + 1))
                if p >= RING:
                    eng.wait_ge(piece_used, p - RING + 1)
                act.copy(w_hi[:, p % RING, :], w_raw[:, p % RING, :]).then_inc(hi_done, 1)
                if kind == "q" and n == 1 and i + 1 < KT // 2:
                    make_h_hi(i + 1)
                if p == 5:
                    eng.wait_ge(angles_ready, 1)
                    act.activation(sin[:, :, :].rearrange("p t i -> p (t i)"), angle[:, 3, :], ACT.Sin)
                    act.activation(cos[:, :, :].rearrange("p t i -> p (t i)"), angle[:, 4, :], ACT.Sin).then_inc(cossin_ready, 1)
                    eng.wait_ge(lam_dots, 1)
                    act.activation(lam_exp[:, :], lam_dot[:, :], ACT.Exp).then_inc(lam_exps, 1)
                for work in act_after[p]:
                    work(eng)

        dve = nc.vector
        steps = [0]

        def link(eng, ins):
            steps[0] += 1
            ins.then_inc(dve_step, 1)
            eng.wait_ge(dve_step, steps[0])

        def dve_rope(t, src, dst, heads):
            def run(eng):
                c_ = cos[:, t:t + 1, :].to_broadcast([P, heads, HALF])
                s_ = sin[:, t:t + 1, :].to_broadcast([P, heads, HALF])
                a, b = rot_a[:, 0:heads, :], rot_b[:, 0:heads, :]
                x1, x2 = src[:, :, 0:HALF], src[:, :, HALF:ROPE]
                dve.tensor_tensor(a, x1, c_, ALU.mult)
                link(eng, dve.tensor_tensor(b, x2, s_, ALU.mult))
                link(eng, dve.tensor_tensor(dst[:, :, 0:HALF], a, b, ALU.subtract))
                dve.tensor_tensor(a, x2, c_, ALU.mult)
                link(eng, dve.tensor_tensor(b, x1, s_, ALU.mult))
                link(eng, dve.tensor_tensor(dst[:, :, HALF:ROPE], a, b, ALU.add))
            return run

        def q_rope(t):
            def run(eng):
                if t == 0:
                    eng.wait_ge(acc_read_act, 3)
                    eng.wait_ge(cossin_ready, 1)
                src = q_tok[:, t, :].rearrange("p (h d) -> p h d", d=QH)[:, :, NOPE:QH]
                dve_rope(t, src, qr_tok[:, t, :, :], HEADS)(eng)
            return run

        def kr_rope(eng):
            eng.wait_ge(acc_read_act, by_act.index(acc_of["kr", 0]) + 1)
            for t in range(TOK):
                for copy in range(2):
                    dve_rope(t, kr_tok[:, t:t + 1, :], kr_dup[:, t:t + 1, copy * ROPE:(copy + 1) * ROPE], 1)(eng)

        def scale_ckv(eng):
            eng.wait_ge(acc_read_act, by_act.index(acc_of["ckv", 0]) + 1)
            eng.wait_ge(rstd_ready, R_CKV + 1)
            for t in range(TOK):
                ins = dve.tensor_scalar(stage[:, t, :], stage[:, t, :], rstd[:, R_CKV, t:t + 1], None, ALU.mult)
            ins.then_inc(ckv_scaled, 1)

        def dve_ckv_lo(eng):
            for g in range(2):
                eng.wait_ge(ckv_hi, g + 1)
                for b in range(2):
                    k = 2 * g + b
                    link(eng, dve.tensor_scalar(tmp[:, b * SEQ:(b + 1) * SEQ],
                                                ps[:, 4 + (G_CKV + g) % 4, b * SEQ:(b + 1) * SEQ],
                                                cols[:, V_GKV + k:V_GKV + k + 1], None, ALU.mult))
                link(eng, dve.tensor_tensor(ckvT_lo[:, 2 * g:2 * g + 2, :].rearrange("p k s -> p (k s)"), tmp[:, :],
                                            ckvT_hi[:, 2 * g:2 * g + 2, :].rearrange("p k s -> p (k s)").bitcast(F32),
                                            ALU.subtract))
            dve.memset(gain_tmp[:, 0:1], 0.0).then_inc(ckv_lo, 2)

        def mla_max(h):
            def run(eng):
                eng.wait_ge(scores_ready, h + 1)
                dve.reduce_max(maxes[:, h % 2, 0:1], ps[:, 4, 0:P], AX_X)
                link(eng, dve.reduce_max(maxes[:, h % 2, 1:2], ps[:, 4, P:KEYS], AX_X))
                if h >= 2:
                    eng.wait_ge(exps_done, h - 1)
                dve.tensor_scalar(neg_max[:, h % 2, 0:2], maxes[:, h % 2, 0:2], -MLA_SCALE, None,
                                  ALU.mult).then_inc(max_ready, 1)
            return run

        def mla_out(h):
            def run(eng):
                eng.wait_ge(pv_done, h + 1)
                link(eng, dve.reciprocal(recip[:, h % 2, 0:2], sums[:, h % 2, 0:2]))
                if h == 0:
                    eng.wait_ge(acc_read_act, by_act.index(acc_of["gate", 0]) + 1)
                if h == HEADS // 2:
                    eng.wait_ge(acc_read_act, by_act.index(acc_of["gate", 1]) + 1)
                if h >= 1:
                    eng.wait_ge(oT_made, h)
                for t in range(TOK):
                    ins = dve.scalar_tensor_tensor(
                        out=o_gated[:, t, :], in0=ps[:, 7, t * P:(t + 1) * P], scalar=recip[:, h % 2, t:t + 1],
                        in1=silu_gate[:, t, h * P:(h + 1) * P], op0=ALU.mult, op1=ALU.mult)
                ins.then_inc(o_gated_ready, 1)
            return run

        def dve_o_lo(m):
            def run(eng):
                src = out_bank(m)
                eng.wait_ge(o_hi_ready, m + 1)
                if m >= HEADS:
                    link(eng, dve.tensor_scalar(tmp[:, 0:SEQ], src, cols[:, NVEC:NVEC + 1], None, ALU.mult))
                    src = tmp[:, 0:SEQ]
                link(eng, dve.tensor_tensor(o_lo[:, m, :], src, o_hi[:, m, :].bitcast(F32), ALU.subtract))
                dve.memset(gain_tmp[:, 0:1], 0.0).then_inc(o_lo_ready, 1)
            return run

        def diff_scores(h):
            m = HEADS + h
            def run(eng):
                if m % 2 == h % 2 and m >= 2:
                    eng.wait_ge(pT_made, m - 1)
                eng.wait_ge(scores_ready, m + 1)
                dst = probs[:, m % 2, :, :]
                link(eng, dve.scalar_tensor_tensor(
                    out=dst, in0=dist[:, :].unsqueeze(1).to_broadcast([P, 2, KEYS]),
                    scalar=-SLOPES[h] / DIFF_SCALE, in1=ps[:, 4:6, 0:KEYS], op0=ALU.mult, op1=ALU.add))
                dve.tensor_reduce(maxes[:, m % 2, 0:2], dst[:, :, 0:P], AX_X, ALU.max).then_inc(scores_read, 1)
                link(eng, dve.tensor_reduce(maxes[:, m % 2, 2:4], dst[:, :, P:KEYS], AX_X, ALU.max))
                dve.tensor_scalar(neg_max[:, m % 2, :], maxes[:, m % 2, :], -DIFF_SCALE, None,
                                  ALU.mult).then_inc(max_ready, 1)
            return run

        def diff_weights(h):
            m = HEADS + h
            def run(eng):
                eng.wait_ge(exps_done, m + 1)
                link(eng, dve.reciprocal(recip[:, m % 2, :], sums[:, m % 2, :]))
                second = recip[:, m % 2, :].rearrange("p (b w) -> p b w", w=2)[:, :, 1]
                link(eng, dve.tensor_scalar(second, second, lam[:, 0:1], None, ALU.mult))
                spans = ((0, P), (P, KEYS))
                for b, (lo, hi) in enumerate(spans):
                    ins = dve.tensor_scalar(probs[:, m % 2, 1, lo:hi], probs[:, m % 2, 1, lo:hi],
                                            recip[:, m % 2, 2 * b + 1:2 * b + 2], None, ALU.mult)
                link(eng, ins)
                for b, (lo, hi) in enumerate(spans):
                    ins = dve.scalar_tensor_tensor(
                        out=probs[:, m % 2, 0, lo:hi], in0=probs[:, m % 2, 0, lo:hi],
                        scalar=recip[:, m % 2, 2 * b:2 * b + 1], in1=probs[:, m % 2, 1, lo:hi],
                        op0=ALU.mult, op1=ALU.subtract)
                ins.then_inc(weights_ready, 1)
            return run

        def head_squares(h):
            def run(eng):
                eng.wait_ge(pv_done, HEADS + h + 1)
                link(eng, dve.tensor_scalar(tmp[:, 0:SEQ], ps[:, 7, 0:SEQ], SQ_SCALE, SQ_CLAMP, ALU.mult, ALU.min))
                for t in range(TOK):
                    part = tmp[:, t * P:(t + 1) * P]
                    ins = dve.scalar_tensor_tensor(out=tmp[:, SEQ + t * P:SEQ + (t + 1) * P], in0=part, scalar=-SQ_CLAMP,
                                                   in1=part, op0=ALU.max, op1=ALU.mult,
                                                   accum_out=sumsq[:, R_HEAD + h, t:t + 1])
                ins.then_inc(head_sq, 1)
            return run

        def diff_out(h):
            def run(eng):
                eng.wait_ge(rstd_ready, R_HEAD + h + 1)
                if h == 0:
                    eng.wait_ge(acc_read_act, by_act.index(acc_of["gate", 3]) + 1)
                eng.wait_ge(oT_made, HEADS + h)
                for t in range(TOK):
                    ins = dve.scalar_tensor_tensor(
                        out=o_gated[:, t, :], in0=ps[:, 7, t * P:(t + 1) * P], scalar=rstd[:, R_HEAD + h, t:t + 1],
                        in1=silu_gate[:, t, D // 2 + h * P:D // 2 + (h + 1) * P], op0=ALU.mult, op1=ALU.mult)
                ins.then_inc(o_gated_ready, 1)
            return run

        def merge_mla(n):
            def run(eng):
                a = acc_of["wom", n]
                eng.wait_ge(piece_used, end[a] + 1)
                eng.wait_ge(acc_read_act, by_act.index(acc_of["mm", n]) + 1)
                for t in range(TOK):
                    ins = dve.tensor_tensor(merged[:, t, n * CH:(n + 1) * CH], ps[:, banks(a) + t, :],
                                            stage[:, t, :], ALU.mult)
                ins.then_inc(acc_read_dve, 1)
            return run

        def merge_diff(n):
            def run(eng):
                a = acc_of["wod", n]
                eng.wait_ge(piece_used, end[a] + 1)
                eng.wait_ge(acc_read_act, by_act.index(acc_of["md", n]) + 1)
                for t in range(TOK):
                    link(eng, dve.tensor_tensor(stage[:, t, :], ps[:, banks(a) + t, :], stage[:, t, :], ALU.mult))
                    part = merged[:, t, n * CH:(n + 1) * CH]
                    link(eng, dve.tensor_tensor(part, part, stage[:, t, :], ALU.add))
                dve.memset(gain_tmp[:, 0:1], 0.0).then_inc(acc_read_dve, 1)
            return run

        def dve_m_lo(n):
            def run(eng):
                eng.wait_ge(m_hi_ready, n + 1)
                dve.tensor_tensor(m_lo[:, 4 * n:4 * n + 4, :].rearrange("p (b k) s -> p b (k s)", b=2), ps[:, 4:6, :],
                                  m_hi[:, 4 * n:4 * n + 4, :].rearrange("p (b k) s -> p b (k s)", b=2).bitcast(F32),
                                  ALU.subtract).then_inc(m_lo_ready, 1)
            return run

        def gate_part(n, i):
            def run(eng):
                k = n * (KT // 2) + i
                eng.wait_ge(gate_in[k % 2], 16 * (k // 2 + 1))
                if i == 0 and n >= 1:
                    eng.wait_ge(gate_summed, n)
                for t in range(2):
                    src = gate_ring[:, k % 2, t * CH:(t + 1) * CH]
                    cc = cols[:, V_C + 2 * i + t:V_C + 2 * i + t + 1]
                    if i == 0 and t == 0:
                        link(eng, dve.tensor_scalar(ada_acc[:, :], src, cc, None, ALU.mult))
                    else:
                        link(eng, dve.scalar_tensor_tensor(out=ada_acc[:, :], in0=src, scalar=cc, in1=ada_acc[:, :],
                                                           op0=ALU.mult, op1=ALU.add))
                ins = dve.memset(gain_tmp[:, 0:1], 0.0)
                ins.then_inc(gate_used, 1)
            return run

        def gate_finish(n):
            def run(eng):
                eng.wait_ge(gate_summed, n + 1)
                eng.wait_ge(bias_in, 32 * (n + 1))
                link(eng, dve.tensor_tensor(tmp[:, :], ps[:, 6, :], bias_gain[:, 0, :], ALU.add))
                dve.tensor_tensor(post_gain[:, n * CH:(n + 1) * CH], tmp[:, :], bias_gain[:, 1, :],
                                  ALU.mult).then_inc(gg_ready, 1)
            return run

        def y_gain(n):
            def run(eng):
                a = acc_of["wout", n]
                eng.wait_ge(acc_read_act, by_act.index(a) + 1)
                eng.wait_ge(gg_ready, n + 1)
                if n == 0:
                    eng.wait_ge(piece_used, last_piece("md", 3) + 1)
                for t in range(TOK):
                    ins = dve.tensor_tensor(yg[:, t, n * CH:(n + 1) * CH], ps[:, banks(a) + t, :],
                                            post_gain[:, n * CH:(n + 1) * CH], ALU.mult)
                ins.then_inc(acc_read_dve, 1)
            return run

        dve_after[28].append(q_rope(0))
        dve_after[29].append(q_rope(1))
        dve_after[last_piece("ckv", 0) + 4].append(scale_ckv)
        dve_after[last_piece("kr", 0) + 4].append(kr_rope)
        dve_after[group_at[G_CKV][1]].append(dve_ckv_lo)
        for h in range(HEADS):
            s, t, v, g = mla_at[h]
            dve_after[s + 4].append(mla_max(h))
            dve_after[v + 4].append(mla_out(h))
            dve_after[g + 4].append(dve_o_lo(h))
            s, t, v, g = diff_at[h]
            dve_after[s + 4].append(diff_scores(h))
            dve_after[s + 8].append(diff_weights(h))
            dve_after[v + 4].append(head_squares(h))
            dve_after[v + 5].append(diff_out(h))
            dve_after[g + 4].append(dve_o_lo(HEADS + h))
        for n in range(4):
            dve_after[last_piece("wom", n) + 3].append(merge_mla(n))
            dve_after[last_piece("wod", n) + 3].append(merge_diff(n))
            dve_after[merge_at[n] + 4].append(dve_m_lo(n))
            for i in range(KT // 2):
                dve_after[first_piece("md", n) + i].append(gate_part(n, i))
            dve_after[last_piece("wod", n)].append(gate_finish(n))
            dve_after[min(last_piece("wout", n) + 3, NP - 1)].append(y_gain(n))

        @block.vector
        def _(eng):
            eng.wait_ge(rstd_ready, 1)
            for t in range(TOK):
                dve.tensor_scalar(x_tok[:, t, :], x_tok[:, t, :], rstd[:, R_X, t:t + 1], None,
                                  ALU.mult).then_inc(xn_ready, 1)
            eng.wait_ge(cols_ready, 1)
            link(eng, dve.tensor_scalar(cols[:, NVEC:NVEC + 1], cols[:, V_GSUB:V_GSUB + 1], 1.0 - LAMBDA_INIT, None,
                                        ALU.mult))

            def ada_products(j):
                if j >= 1:
                    eng.wait_ge(ada_summed, j)
                for q in range(KT // 2):
                    n = j * (KT // 2) + q
                    eng.wait_ge(ada_in[n % RING], 32 * (n // RING + 1))
                    for t in range(2):
                        src = ada_ring[:, n % RING, t, :, :].rearrange("p s n -> p (s n)")
                        cc = cols[:, V_C + 2 * q + t:V_C + 2 * q + t + 1]
                        if q == 0 and t == 0:
                            ins = dve.tensor_scalar(ada_acc[:, :], src, cc, None, ALU.mult)
                        else:
                            ins = dve.scalar_tensor_tensor(out=ada_acc[:, :], in0=src, scalar=cc, in1=ada_acc[:, :],
                                                           op0=ALU.mult, op1=ALU.add)
                        if t == 0:
                            link(eng, ins)
                        else:
                            ins.then_inc(ada_used, 1)
                            eng.wait_ge(ada_used, n + 1)
            def modulation(j):
                eng.wait_ge(ada_summed, j + 1)
                k = 2 * j
                dve.tensor_tensor(mod_shift[:, k:k + 2], ps[:, 6, 0:2], cols[:, V_SHIFT + k:V_SHIFT + k + 2], ALU.add)
                link(eng, dve.scalar_tensor_tensor(out=gain_tmp[:, 0:2], in0=ps[:, 6, 2:4], scalar=1.0,
                                                   in1=cols[:, V_SCALE + k:V_SCALE + k + 2],
                                                   op0=ALU.add, op1=ALU.add))
                link(eng, dve.tensor_tensor(mod_gain[:, k:k + 2], gain_tmp[:, 0:2], cols[:, V_GPRE + k:V_GPRE + k + 2],
                                            ALU.mult))
                dve.memset(gain_tmp[:, 0:1], 0.0).then_inc(mod_ready, 1)

            def make_h_lo(j):
                for t in range(2):
                    k = 2 * j + t
                    link(eng, dve.tensor_scalar(tmp[:, t * SEQ:(t + 1) * SEQ], xnT[:, k, :], mod_gain[:, k:k + 1],
                                                mod_shift[:, k:k + 1], ALU.mult, ALU.add))
                eng.wait_ge(h_hi_ready, j + 1)
                link(eng, dve.tensor_tensor(h_lo[:, 2 * j:2 * j + 2, :].rearrange("p k s -> p (k s)"), tmp[:, :],
                                            h_hi[:, 2 * j:2 * j + 2, :].rearrange("p k s -> p (k s)").bitcast(F32),
                                            ALU.subtract))
                dve.memset(gain_tmp[:, 0:1], 0.0).then_inc(h_lo_ready, 1)

            def angles():
                eng.wait_ge(pos_in, 32)
                eng.wait_ge(consts, 3)
                link(eng, dve.tensor_copy(pos_qf[:, :], pos_q[:, :]))
                ang, k_, r_, s_, c_ = (angle[:, i, :] for i in range(5))
                for t in range(TOK):
                    link(eng, dve.tensor_scalar(ang[:, t * HALF:(t + 1) * HALF], freq[:, :], pos_qf[:, t:t + 1], None,
                                                ALU.mult))

                def turns(dst, src, turn):
                    link(eng, dve.tensor_scalar(dst, src, 1.0 / turn, ROUND_MAGIC, ALU.mult, ALU.add))
                    link(eng, dve.tensor_scalar(dst, dst, ROUND_MAGIC, None, ALU.subtract))

                def less(dst, k, part, src):
                    link(eng, dve.scalar_tensor_tensor(out=dst, in0=k, scalar=-part, in1=src, op0=ALU.mult, op1=ALU.add))

                turns(k_, ang, BIG_TURN)
                less(ang, k_, BIG_PARTS[0], ang)
                less(ang, k_, BIG_PARTS[1], ang)
                link(eng, dve.tensor_scalar(r_, k_, -BIG_PARTS[2], None, ALU.mult))
                link(eng, dve.tensor_tensor(s_, ang, r_, ALU.add))
                turns(k_, s_, 2.0 * math.pi)
                less(ang, k_, TURN_PARTS[0], ang)
                less(ang, k_, TURN_PARTS[1], ang)
                link(eng, dve.tensor_tensor(ang, ang, r_, ALU.add))
                less(ang, k_, TURN_PARTS[2], ang)
                link(eng, dve.tensor_scalar(s_, ang, 3.1415925, -3.1415925, ALU.min, ALU.max))
                link(eng, dve.tensor_scalar(c_, s_, -1.0, None, ALU.mult))
                link(eng, dve.tensor_tensor(c_, c_, s_, ALU.max))
                link(eng, dve.tensor_scalar(c_, c_, -1.0, math.pi / 2, ALU.mult, ALU.add))
                dve.memset(gain_tmp[:, 0:1], 0.0).then_inc(angles_ready, 1)
                eng.wait_ge(lam_ld, 64)
                link(eng, dve.tensor_tensor(lam_prod[:, 0, :], lam_in[:, 0, :], lam_in[:, 1, :], ALU.mult))
                link(eng, dve.tensor_tensor(lam_prod[:, 1, :], lam_in[:, 2, :], lam_in[:, 3, :], ALU.mult))
                dve.tensor_reduce(lam_dot[:, :], lam_prod[:, :, :], AX_X, ALU.add).then_inc(lam_dots, 1)

            def distances():
                eng.wait_ge(consts, 6)
                link(eng, dve.tensor_copy(tmp[:, 0:SEQ], pos_row[:, :]))
                for lo, t, n in ((0, 0, P), (P, 1, SEQ)):
                    d_, n_ = dist[:, lo:lo + n], tmp[:, SEQ:SEQ + n]
                    link(eng, dve.tensor_scalar(d_, tmp[:, 0:n], pos_qf[:, t:t + 1], None, ALU.subtract))
                    link(eng, dve.tensor_scalar(n_, d_, -1.0, None, ALU.mult))
                    link(eng, dve.tensor_tensor(d_, d_, n_, ALU.max))
                for lo in (0, SEQ):
                    link(eng, dve.tensor_tensor(dist[:, lo:lo + P], dist[:, lo:lo + P], causal_far[:, :], ALU.add))
                eng.wait_ge(lam_exps, 1)
                link(eng, dve.scalar_tensor_tensor(out=lam[:, :], in0=lam_exp[:, 0:1], scalar=LAMBDA_INIT,
                                                   in1=lam_exp[:, 1:2], op0=ALU.add, op1=ALU.subtract))

            ada_products(0)
            modulation(0)
            eng.wait_ge(xT_copied, KT // 2)
            make_h_lo(0)
            for p, (a, kind, n, i, first, last) in enumerate(pieces):
                more = kind == "q" and i + 1 < KT // 2
                if more and n == 0:
                    ada_products(i + 1)
                eng.wait_ge(hi_done, p + 1)
                dve.tensor_tensor(w_lo[:, p % RING, :], w_raw[:, p % RING, :],
                                  w_hi[:, p % RING, :].bitcast(F32), ALU.subtract).then_inc(lo_done, 1)
                if more and n == 0:
                    modulation(i + 1)
                if more and n == 1:
                    make_h_lo(i + 1)
                if p == 2:
                    angles()
                if p == 8:
                    distances()
                for work in dve_after[p]:
                    work(eng)
            eng.wait_ge(acc_read_act, len(by_act))
            dve.tensor_reduce(sumsq[:, R_Y, :], y_sq[:, :, :], AX_X, ALU.add).then_inc(y_sums, 1)
            eng.wait_ge(x_again_in, 16 * TOK)
            eng.wait_ge(acc_read_dve, len(by_dve) + 4)
            eng.wait_ge(rstd_ready, NR)
            for k in range(2 * TOK):
                t, half = k // 2, k % 2
                part = slice(half * (D // 2), (half + 1) * (D // 2))
                dve.scalar_tensor_tensor(out=yg[:, t, part], in0=yg[:, t, part], scalar=rstd[:, R_Y, t:t + 1],
                                         in1=x_again[:, t, part], op0=ALU.mult, op1=ALU.add).then_inc(out_ready, 1)

        @block.tensor
        def _(pe):
            mm = nc.tensor.matmul
            tr = nc.tensor.transpose

            def ada_sum(j):
                pe.wait_ge(ada_used, (j + 1) * (KT // 2))
                if j == 0:
                    pe.wait_ge(xT_copied, KT // 2)
                else:
                    pe.wait_ge(mod_ready, j)
                for b in range(4):
                    ins = mm(ps[:, 6, b:b + 1], lhsT=ada_acc[:, b * P:(b + 1) * P], rhs=ones[:, 0:1],
                             start=True, stop=True)
                ins.then_inc(ada_summed, 1)

            def group(g):
                bank = 4 + g % 4
                if g == G_QN:
                    pe.wait_ge(acc_read_act, 3)
                    pe.wait_ge(mod_ready, KT // 2)
                    pe.wait_ge(h_hi_ready, 1)
                if g == G_QR:
                    pe.wait_ge(lo_done, 30 + 1)
                if g == G_CKV:
                    pe.wait_ge(ckv_scaled, 1)
                if g == G_KR:
                    pe.wait_ge(lo_done, last_piece("kr", 0) + 5 + 1)
                if G_KN <= g < G_D:
                    pe.wait_ge(acc_read_act, by_act.index(acc_of["ukv", g - G_KN]) + 1)
                if g == G_D:
                    pe.wait_ge(o_lo_ready, HEADS)
                    pe.wait_ge(exps_done, HEADS)
                if g >= G_D:
                    kind, n = (("qd", 0), ("qd", 1), ("kd", 0), ("kd", 1))[(g - G_D) // 2]
                    pe.wait_ge(acc_read_act, by_act.index(acc_of[kind, n]) + 1)
                if g >= 4:
                    pe.wait_ge(tr_copied, g - 3)
                for b in range(2):
                    if g == G_KR and b:
                        break
                    for t in range(TOK):
                        if g < G_QR:
                            src = q_tok[:, t, (2 * g + b) * QH:(2 * g + b) * QH + NOPE]
                        elif g < G_CKV:
                            k = 2 * (2 * (g - G_QR) + b)
                            src = qr_tok[:, t, k:k + 2, :].rearrange("p h d -> p (h d)")
                        elif g < G_KR:
                            k = 2 * (g - G_CKV) + b
                            src = stage[:, t, k * P:(k + 1) * P]
                        elif g == G_KR:
                            src = kr_dup[:, t, :]
                        elif g < G_D:
                            col = (g - G_KN) % 2 * 256 + b * P
                            src = stage[:, t, col:col + P]
                        else:
                            k = 2 * ((g - G_D) % 2) + b
                            src = stage[:, t, k * P:(k + 1) * P]
                        ins = tr(ps[:, bank, b * SEQ + t * P:b * SEQ + (t + 1) * P], src, ident[:, :])
                ins.then_inc(tr_made, 1)

            def mla_scores(h):
                pe.wait_ge(tr_copied, G_D)
                if h >= 1:
                    pe.wait_ge(exps_done, h)
                r = ROPE * (h % 2)
                for t, (lo, keys) in enumerate(((0, P), (P, SEQ))):
                    q = slice(t * P, (t + 1) * P)
                    o = ps[:, 4, lo:lo + keys]
                    mm(o, lhsT=qnT[:, h, q], rhs=knT[:, h, 0:keys], start=True, stop=False)
                    mm(o, lhsT=qrT[r:r + ROPE, h // 2, q], rhs=krT[r:r + ROPE, 0:keys], start=False, stop=False)
                    ins = mm(ps[:, 4, lo + keys - P:lo + keys], lhsT=ident_b[:, :], rhs=causal_b[:, :],
                             start=False, stop=True)
                ins.then_inc(scores_ready, 1)

            def diff_scores_pe(h):
                if h == 0:
                    pe.wait_ge(tr_copied, N_GROUPS)
                else:
                    pe.wait_ge(scores_read, h)
                for w in range(2):
                    for t, (lo, keys) in enumerate(((0, P), (P, SEQ))):
                        ins = mm(ps[:, 4 + w, lo:lo + keys], lhsT=qdT[w * DQK:(w + 1) * DQK, h, t * P:(t + 1) * P],
                                 rhs=kdT[w * DQK:(w + 1) * DQK, h, 0:keys], start=True, stop=True)
                ins.then_inc(scores_ready, 1)

            def transpose_probs(m):
                if m < HEADS:
                    pe.wait_ge(exps_done, m + 1)
                else:
                    pe.wait_ge(weights_ready, m - HEADS + 1)
                if m >= 1:
                    pe.wait_ge(pT_copied, m)
                for k in range(3):
                    ins = tr(ps[:, 6, k * P:(k + 1) * P], probs[:, m % 2, 0, k * P:(k + 1) * P], ident[:, :])
                ins.then_inc(pT_made, 1)

            def values(m):
                pe.wait_ge(pT_copied, m + 1)
                if m >= 1:
                    pe.wait_ge(o_gated_ready, m)
                if m > HEADS:
                    pe.wait_ge(o_lo_ready, m)
                if m == HEADS:
                    pe.wait_ge(acc_read_act, by_act.index(acc_of["vd", 1]) + 1)
                h = m % HEADS
                v = ((lambda t: v_mla[:, t, h, :]) if m < HEADS else (lambda t: v_diff[:, t, h * P:(h + 1) * P]))
                mm(ps[:, 7, 0:P], lhsT=probsT[:, 0:P], rhs=v(0), start=True, stop=True)
                mm(ps[:, 7, P:2 * P], lhsT=probsT[:, P:2 * P], rhs=v(0), start=True, stop=False)
                mm(ps[:, 7, P:2 * P], lhsT=probsT[:, 2 * P:3 * P], rhs=v(1), start=False, stop=True).then_inc(pv_done, 1)

            def transpose_out(m):
                pe.wait_ge(o_gated_ready, m + 1)
                if m >= 1:
                    pe.wait_ge(o_lo_ready, m)
                for t in range(TOK):
                    ins = tr(out_bank(m)[:, t * P:(t + 1) * P], o_gated[:, t, :], ident[:, :])
                ins.then_inc(oT_made, 1)

            def transpose_merged(n):
                pe.wait_ge(acc_read_dve, 4 + n + 1)
                if n >= 1:
                    pe.wait_ge(m_lo_ready, n)
                for b in range(4):
                    for t in range(TOK):
                        ins = tr(ps[:, 4 + b // 2, b % 2 * SEQ + t * P:b % 2 * SEQ + (t + 1) * P],
                                 merged[:, t, n * CH + b * P:n * CH + (b + 1) * P], ident[:, :])
                ins.then_inc(mT_made, 1)

            def gate_sum(n):
                pe.wait_ge(gate_used, (n + 1) * (KT // 2))
                if n >= 1:
                    pe.wait_ge(gg_ready, n)
                mm(ps[:, 6, :], lhsT=ones[:, :], rhs=ada_acc[:, :], start=True, stop=True).then_inc(gate_summed, 1)

            for g in range(N_GROUPS):
                pe_after[group_at[g][0]].append(lambda g=g: group(g))
            for h in range(HEADS):
                for m, place, scores in ((h, mla_at[h], mla_scores), (HEADS + h, diff_at[h], diff_scores_pe)):
                    pe_after[place[0]].append(lambda h=h, f=scores: f(h))
                    pe_after[place[1]].append(lambda m=m: transpose_probs(m))
                    pe_after[place[2]].append(lambda m=m: values(m))
                    pe_after[place[3]].append(lambda m=m: transpose_out(m))
            for n in range(4):
                pe_after[merge_at[n]].append(lambda n=n: transpose_merged(n))
                pe_after[last_piece("wod", n) - 2].append(lambda n=n: gate_sum(n))

            pe.wait_ge(consts, 2)
            pe.wait_ge(vec_in, 16 * 6)
            tr(ps[:, 7, 0:NVEC], vec_rows[0:NVEC, :], ident[0:NVEC, 0:NVEC]).then_inc(cols_T, 1)
            pe.wait_ge(xn_ready, TOK)
            for g in range(KT // 2):
                if g == 1:
                    pe.wait_ge(cols_ready, 1)
                if g >= 2:
                    pe.wait_ge(xT_copied, g - 1)
                for b in range(2):
                    for t in range(TOK):
                        k = 2 * g + b
                        ins = tr(ps[:, 6 + g % 2, b * SEQ + t * P:b * SEQ + (t + 1) * P],
                                 x_tok[:, t, k * P:(k + 1) * P], ident[:, :])
                ins.then_inc(xT_made, 1)
            ada_sum(0)
            for p, (a, kind, n, i, first, last) in enumerate(pieces):
                if kind == "q" and n == 0:
                    if i + 1 < KT // 2:
                        ada_sum(i + 1)
                    pe.wait_ge(h_lo_ready, i + 1)
                if kind == "ukv" and n == 0 and first:
                    pe.wait_ge(ckv_lo, 2)
                if kind == "wom" and n == 0 and first:
                    pe.wait_ge(o_lo_ready, HEADS)
                if kind == "wod" and n == 0 and first:
                    pe.wait_ge(o_lo_ready, 2 * HEADS)
                if kind == "wout" and n == 0:
                    pe.wait_ge(m_lo_ready, i // 2 + 1)
                if first and a >= 3:
                    wait_acc_read(pe, {3: 0, 4: 1}.get(a, a - 2))
                pe.wait_ge(lo_done, p + 1)
                b0 = banks(a)
                wide = ROPE if kind == "kr" else CH
                tiles = KT if kind == "kr" else 2
                s_hi, s_lo = {"ukv": (ckvT_hi, ckvT_lo), "wom": (o_hi, o_lo), "wod": (o_hi, o_lo),
                              "wout": (m_hi, m_lo)}.get(kind, (h_hi, h_lo))
                for r in range(tiles):
                    k = 2 * i + r + (HEADS if kind == "wod" else 0)
                    hi = w_hi[:, p % RING, r * wide:(r + 1) * wide]
                    lo = w_lo[:, p % RING, r * wide:(r + 1) * wide]
                    for t in range(TOK):
                        o = ps[:, b0 + t, 0:wide]
                        q = slice(t * P, (t + 1) * P)
                        mm(o, lhsT=s_hi[:, k, q], rhs=hi, start=first and r == 0, stop=False)
                        mm(o, lhsT=s_hi[:, k, q], rhs=lo, start=False, stop=False)
                        ins = mm(o, lhsT=s_lo[:, k, q], rhs=hi, start=False, stop=last and r == tiles - 1)
                ins.then_inc(piece_used, 1)
                for work in pe_after[p]:
                    work()


_INS = ["x", "c", "positions", "w_ada", "b_ada", "g_pre", "w_in", "g_kv", "w_ukv",
        "lambda_q1", "lambda_k1", "lambda_q2", "lambda_k2", "g_subln",
        "w_o_mla", "w_o_diff", "w_out", "g_post"]


def kernel(**inputs):
    import numpy as _np
    import concourse.bacc as _bacc
    from concourse import mybir as _mybir
    from concourse.bass_utils import run_bass_kernel_spmd as _run

    nc = _bacc.Bacc("TRN2", target_bir_lowering=False, num_devices=1)
    arrays, args = {}, []
    for name in _INS:
        a = _np.ascontiguousarray(inputs[name])
        arrays[f"in_{name}"] = a
        args.append(nc.dram_tensor(f"in_{name}", a.shape, _mybir.dt.from_np(a.dtype), kind="ExternalInput").ap())
    shape = (1, 256, 2048)
    args.append(nc.dram_tensor("out", shape, _mybir.dt.float32, kind="ExternalOutput").ap())
    hybrid_block(nc, *args)
    r = _run(nc, [arrays], core_ids=[0])
    return r.results[0]["out"]
```

```python
from contextlib import ExitStack

import math

import concourse.bass as bass
from concourse import mybir

F32 = mybir.dt.float32
F32R = mybir.dt.float32r
BF16 = mybir.dt.bfloat16
I32 = mybir.dt.int32
ALU = mybir.AluOpType
ACT = mybir.ActivationFunctionType
AX_X = mybir.AxisListType.X

P = 128
D = 2048
SEQ = 256
TOK = SEQ // P
KT = D // P
CH = 512
HEADS = 8
NOPE = 128
ROPE = 64
HALF = ROPE // 2
QH = NOPE + ROPE
RANK = 512
DQK = 64
EPS = 1e-6
NEG_INF = -1e30
MLA_SCALE = (NOPE + ROPE) ** -0.5
DIFF_SCALE = DQK ** -0.5
LAMBDA_INIT = 0.8 - 0.6 * math.exp(-0.3 * 0)
SLOPES = [2.0 ** (-8.0 * (h + 1) / HEADS) for h in range(HEADS)]
ROPE_FREQ = [10000.0 ** (-i / HALF) for i in range(HALF)]

RING = 4
PIECE = 1024
KEYS = P + SEQ

C_Q, C_CKV, C_KR = 0, 1536, 2048
C_QD, C_KD, C_VD, C_GM, C_GD, C_MM, C_MD = 2112, 3136, 4160, 5184, 6208, 7232, 9280

V_SHIFT, V_SCALE, V_GPRE, V_C, V_GKV, V_GSUB = 0, 16, 32, 48, 64, 68
NVEC = 69

SQ_SCALE, SQ_CLAMP, SQ_LIMIT = 2.0 ** -40, 2.0 ** 25, 2.0 ** (128 - 80)

BIG_TURN = 2.0 * math.pi * 512
BIG_PARTS = (3216.0, 0.99072265625, 0.00015461970178876072)
TURN_PARTS = (6.283203125, -1.7814338207244873e-05, -3.4822063010864213e-09)
ROUND_MAGIC = 12582912.0


def make_jobs():
    jobs = [("ckv", 0), ("kr", 0)]
    jobs += [("gate", i) for i in range(4)]
    jobs += [("ukv", i) for i in range(4)]
    jobs += [("vd", 0), ("vd", 1)]
    jobs += [("qd", 0), ("qd", 1), ("kd", 0), ("kd", 1)]
    for n in range(4):
        jobs += [("mm", n), ("wom", n)]
    for n in range(4):
        jobs += [("md", n), ("wod", n)]
    jobs += [("wout", n) for n in range(4)]
    return jobs


EARLY = KT // 4
PIECES_OF = {"kr": 1, "gate": KT // 2 - EARLY, "ukv": 2, "wom": 4, "wod": 4}


def hybrid_block(nc, x, c, positions, w_ada, b_ada, g_pre, w_in, g_kv, w_ukv,
                 lambda_q1, lambda_k1, lambda_q2, lambda_k2, g_subln,
                 w_o_mla, w_o_diff, w_out, g_post, out):
    pieces = []
    start, end = {}, {}
    first_part = []
    for j in range(KT // 2):
        first_part.append([])
        if EARLY - 1 <= j < EARLY + 3:
            for i in range(EARLY):
                first_part[j].append(len(pieces))
                pieces.append((None, "early", j - EARLY + 1, i, i == 0, i == EARLY - 1))
        for ch in range(3):
            first_part[j].append(len(pieces))
            start.setdefault(ch, len(pieces))
            end[ch] = len(pieces)
            pieces.append((ch, "q", ch, j, j == 0, j == KT // 2 - 1))
    early_end = [first_part[EARLY - 1 + n][EARLY - 1] for n in range(4)]
    PH1 = len(pieces)
    acc_of = {("q", i): i for i in range(3)}
    for a, (kind, n) in enumerate(make_jobs(), start=3):
        m = PIECES_OF.get(kind, KT // 2)
        start[a], end[a] = len(pieces), len(pieces) + m - 1
        acc_of[kind, n] = a
        for i in range(m):
            pieces.append((a, kind, n, i + (EARLY if kind == "gate" else 0), i == 0, i == m - 1))
    NP = len(pieces)
    first_piece = lambda kind, n: start[acc_of[kind, n]]
    last_piece = lambda kind, n: end[acc_of[kind, n]]

    def banks(a):
        return 6 if a is None else 2 * a if a < 3 else 2 * ((a + 1) % 2)

    in_cols = {"q": C_Q, "ckv": C_CKV, "gate": C_GM, "early": C_GM, "vd": C_VD, "qd": C_QD, "kd": C_KD,
               "mm": C_MM, "md": C_MD}

    def piece_source(kind, n, i):
        if kind == "kr":
            return w_in[0, :, C_KR:C_KR + ROPE].rearrange("(t p) n -> p t n", p=P)
        w, col = {"ukv": (w_ukv, n * CH), "wom": (w_o_mla, n * CH), "wod": (w_o_diff, n * CH),
                  "wout": (w_out, n * CH)}.get(kind) or (w_in, in_cols[kind] + n * CH)
        return w[0, 2 * i * P:2 * (i + 1) * P, col:col + CH].rearrange("(t p) n -> p t n", p=P)

    pe_after = {p: [] for p in range(-1, NP)}
    act_after = {p: [] for p in range(-1, NP)}
    dve_after = {p: [] for p in range(-1, NP)}

    with ExitStack() as ctx:
        KB = 1024
        at = [16512]

        def room(size):
            at[0] += size
            return at[0] - size

        def sb(name, shape, dt, offset=None):
            size = 4 if dt != BF16 else 2
            for s in shape[1:]:
                size *= s
            if offset is None:
                offset = room((size + 31) // 32 * 32)
            return nc.alloc_sbuf_tensor_at(name, shape, dt, offset=offset)

        w_raw = sb("w_raw", [P, RING, PIECE], F32)
        w_hi = sb("w_hi", [P, RING, PIECE], F32R)
        w_lo = sb("w_lo", [P, RING, PIECE], F32R)
        r_h_hi, r_h_lo, r_o_hi, r_o_lo = room(16 * KB), room(16 * KB), room(16 * KB), room(16 * KB)
        r_a, r_b, r_c = room(32 * KB), room(24 * KB), room(16 * KB)

        h_hi = sb("h_hi", [P, KT, SEQ], F32R, r_h_hi)
        h_lo = sb("h_lo", [P, KT, SEQ], F32R, r_h_lo)
        yg = sb("yg", [P, TOK, D], F32, r_h_hi)
        x_again = sb("x_again", [P, TOK, D], F32, r_h_lo)
        o_hi = sb("o_hi", [P, KT, SEQ], F32R, r_o_hi)
        o_lo = sb("o_lo", [P, KT, SEQ], F32R, r_o_lo)
        xnT = sb("xnT", [P, KT, SEQ], F32, r_o_hi)
        x_tok = sb("x_tok", [P, TOK, D], F32, r_o_lo)
        ckvT_hi = sb("ckvT_hi", [P, RANK // P, SEQ], F32R, r_o_hi + 8 * KB)
        ckvT_lo = sb("ckvT_lo", [P, RANK // P, SEQ], F32R, r_o_hi + 12 * KB)
        gate_part_sum = sb("gate_part_sum", [P, 4, TOK, CH], F32, r_o_lo)
        qnT = sb("qnT", [P, HEADS, SEQ], F32, r_a)
        qrT = sb("qrT", [P, HEADS // 2, SEQ], F32, r_a + 8 * KB)
        knT = sb("knT", [P, HEADS, SEQ], F32, r_a + 12 * KB)
        krT = sb("krT", [P, SEQ], F32, r_a + 20 * KB)
        v_mla = sb("v_mla", [P, TOK, HEADS, NOPE], F32, r_a + 21 * KB)
        merged = sb("merged", [P, TOK, D], F32, r_a)
        post_gain = sb("post_gain", [P, D], F32, r_a + 16 * KB)
        gate_ring = sb("gate_ring", [P, 2, PIECE], F32, r_a + 24 * KB)
        q_tok = sb("q_tok", [P, TOK, HEADS * QH], F32, r_b)
        qr_tok = sb("qr_tok", [P, TOK, HEADS, ROPE], F32, r_b + 12 * KB)
        kr_tok = sb("kr_tok", [P, TOK, ROPE], F32, r_b + 16 * KB)
        kr_dup = sb("kr_dup", [P, TOK, 2 * ROPE], F32, r_b + 17 * KB)
        rot_a = sb("rot_a", [P, HEADS, HALF], F32, r_b + 18 * KB)
        rot_b = sb("rot_b", [P, HEADS, HALF], F32, r_b + 19 * KB)
        lam_in = sb("lam_in", [P, 4, DQK], F32, r_b + 20 * KB)
        pos_row = sb("pos_row", [P, SEQ], I32, r_b + 21 * KB)
        angle = sb("angle", [P, 5, TOK * HALF], F32, r_b + 22 * KB)
        lam_prod = sb("lam_prod", [P, 2, DQK], F32, r_b + 23 * KB + 256)
        qdT = sb("qdT", [P, HEADS, SEQ], F32, r_b)
        kdT = sb("kdT", [P, HEADS, SEQ], F32, r_b + 8 * KB)
        v_diff = sb("v_diff", [P, TOK, HEADS * P], F32, r_b + 16 * KB)
        ada_ring = sb("ada_ring", [P, RING, 2, 2, 2 * P], F32, r_c)
        silu_gate = sb("silu_gate", [P, 2, TOK, D // 2], F32, r_c)
        bias_gain = sb("bias_gain", [P, 2, CH], F32, r_c + 4 * KB)
        m_hi = sb("m_hi", [P, KT, SEQ], F32R, r_b)
        m_lo = sb("m_lo", [P, KT, SEQ], F32R, r_b + 16 * KB)

        stage = sb("stage", [P, TOK, CH], F32)
        tmp = sb("tmp", [P, CH], F32)
        ada_acc = sb("ada_acc", [P, 2, CH], F32)
        r_p = room(2 * 2 * KEYS * 4)
        probs = sb("probs", [P, 2, 2, KEYS], F32, r_p)
        probsT = sb("probsT", [P, KEYS], F32)
        o_gated = sb("o_gated", [P, TOK, P], F32)
        dist = sb("dist", [P, KEYS], F32)
        vec_rows = sb("vec_rows", [P, P], F32, r_a)
        cols = sb("cols", [P, NVEC + 3], F32)
        ident = sb("ident", [P, P], F32)
        ident_b = sb("ident_b", [P, P], BF16)
        causal_b = sb("causal_b", [P, P], BF16)
        causal_far = sb("causal_far", [P, P], F32)
        ones = sb("ones", [P, P], F32)
        freq = sb("freq", [P, HALF], F32)
        cos = sb("cos", [P, TOK, HALF], F32)
        sin = sb("sin", [P, TOK, HALF], F32)
        pos_q = sb("pos_q", [P, TOK], I32)
        pos_qf = sb("pos_qf", [P, TOK], F32)
        mod_gain = sb("mod_gain", [P, KT], F32)
        mod_shift = sb("mod_shift", [P, KT], F32)
        gain_tmp = sb("gain_tmp", [P, 2], F32)
        NR = 3 + HEADS
        R_X, R_CKV, R_HEAD, R_Y = 0, 1, 2, 2 + HEADS
        sumsq = sb("sumsq", [P, NR, TOK], F32)
        variance = sb("variance", [P, NR, TOK], F32)
        rstd = sb("rstd", [P, NR, TOK], F32)
        power = sb("power", [P, TOK], F32)
        in_range = sb("in_range", [P, TOK], F32)
        y_sq = sb("y_sq", [P, TOK, 4], F32)
        maxes = sb("maxes", [P, 2, 4], F32)
        neg_max = sb("neg_max", [P, 2, 4], F32)
        sums = sb("sums", [P, 2, 4], F32)
        recip = sb("recip", [P, 2, 4], F32)
        lam_dot = sb("lam_dot", [P, 2], F32)
        lam_exp = sb("lam_exp", [P, 2], F32)
        lam = sb("lam", [P, 1], F32)
        assert at[0] <= 229368, at[0]

        ps = ctx.enter_context(nc.psum_tensor("ps", [P, 8, CH], F32))

        def sem(name):
            return ctx.enter_context(nc.semaphore(name))

        raw_in = [sem(f"raw_in{i}") for i in range(RING)]
        ada_in = [sem(f"ada_in{i}") for i in range(RING)]
        gate_in = [sem(f"gate_in{i}") for i in range(2)]
        hi_done, lo_done, piece_used = sem("hi_done"), sem("lo_done"), sem("piece_used")
        x_in, vec_in, pos_in, lam_ld = sem("x_in"), sem("vec_in"), sem("pos_in"), sem("lam_ld")
        consts = sem("consts")
        cols_T, cols_ready = sem("cols_T"), sem("cols_ready")
        x_sq, rstd_ready, xn_ready = sem("x_sq"), sem("rstd_ready"), sem("xn_ready")
        var_ready = sem("var_ready")
        xT_made, xT_copied = sem("xT_made"), sem("xT_copied")
        ada_used, ada_acc_ready, ada_summed, mod_ready = (
            sem("ada_used"), sem("ada_acc_ready"), sem("ada_summed"), sem("mod_ready"))
        h_hi_ready, h_lo_ready = sem("h_hi_ready"), sem("h_lo_ready")
        acc_read_act, acc_read_dve = sem("acc_read_act"), sem("acc_read_dve")
        tr_made, tr_copied = sem("tr_made"), sem("tr_copied")
        angles_ready, cossin_ready = sem("angles_ready"), sem("cossin_ready")
        lam_dots, lam_exps = sem("lam_dots"), sem("lam_exps")
        ckv_scaled, ckv_hi, ckv_lo = sem("ckv_scaled"), sem("ckv_hi"), sem("ckv_lo")
        scores_ready, scores_read, max_ready, exps_done = (
            sem("scores_ready"), sem("scores_read"), sem("max_ready"), sem("exps_done"))
        weights_ready = sem("weights_ready")
        pT_made, pT_copied = sem("pT_made"), sem("pT_copied")
        pv_done, head_sq, o_gated_ready = sem("pv_done"), sem("head_sq"), sem("o_gated_ready")
        oT_made, o_hi_ready, o_lo_ready = sem("oT_made"), sem("o_hi_ready"), sem("o_lo_ready")
        sig_ready, merged_ready = sem("sig_ready"), sem("merged_ready")
        mT_made, m_hi_ready, m_lo_ready = sem("mT_made"), sem("m_hi_ready"), sem("m_lo_ready")
        gate_used, gate_acc_ready, gate_summed, gg_ready, bias_in = (
            sem("gate_used"), sem("gate_acc_ready"), sem("gate_summed"), sem("gg_ready"), sem("bias_in"))
        x_again_in, out_ready, out_done = (
            sem("x_again_in"), sem("out_ready"), sem("out_done"))
        y_sums, root_ready = sem("y_sums"), sem("root_ready")
        dve_step, pool_step = sem("dve_step"), sem("pool_step")

        block = ctx.enter_context(nc.Block())

        by_dve = [a for a in range(3, 3 + len(make_jobs())) if pieces[start[a]][1] in ("gate", "wom", "wod")]
        by_act = [a for a in range(3 + len(make_jobs())) if a not in by_dve]

        def dve_reads(kind, n):
            return by_dve.index(acc_of[kind, n]) + 1

        def wait_acc_read(eng, a):
            if a in by_dve:
                eng.wait_ge(acc_read_dve, by_dve.index(a) + 1)
            else:
                eng.wait_ge(acc_read_act, by_act.index(a) + 1)
            if pieces[start[a]][1] == "wout":
                eng.wait_ge(acc_read_dve, len(by_dve) + pieces[start[a]][2] + 1)

        MLA0 = first_piece("vd", 0) + 3
        DIFF0 = first_piece("mm", 0) + 4
        mla_at = [(MLA0 + 5 * h, MLA0 + 5 * h + 3, MLA0 + 5 * h + 5, MLA0 + 5 * h + 7) for h in range(HEADS)]
        diff_at = [(DIFF0 + 5 * h, DIFF0 + 5 * h + 6, DIFF0 + 5 * h + 8, DIFF0 + 5 * h + 11) for h in range(HEADS)]

        G_QN, G_QR, G_CKV, G_KR, G_KN, G_D = 0, 4, 6, 8, 9, 13
        N_GROUPS = G_D + 8

        def group_bank(g):
            return 4 + g % 4 if g < G_D else 5

        ada_before = {}
        for j in range(KT // 2 - 1):
            own = first_part[j]
            for q in range(KT // 2):
                ada_before.setdefault(own[min((q + 1) * len(own) // (KT // 2 + 1), len(own) - 1)], []).append((j + 1, q))
        pair_end = {first_part[j][-1]: j for j in range(KT // 2 - 1)}
        GATE0, GATE_STEP = first_piece("mm", 0) + 5, 3
        gate_parts_at = {GATE0 + GATE_STEP * k: (k,) for k in range(4 * (KT // 2))}
        gate_end = [GATE0 + GATE_STEP * (8 * n + 7) for n in range(4)]

        @block.sync
        def _(sp):
            sp.dma_start(vec_rows[V_C:V_C + KT, :], c[0, :].rearrange("(r n) -> r n", n=P)).then_inc(vec_in, 16)
            for row, n, v in ((V_SHIFT, KT, b_ada[0, 0:D]), (V_SCALE, KT, b_ada[0, D:2 * D]),
                              (V_GPRE, KT, g_pre[0, :]), (V_GKV, RANK // P, g_kv[0, :]),
                              (V_GSUB, 1, g_subln[0, :])):
                sp.dma_start(vec_rows[row:row + n, :], v.rearrange("(r n) -> r n", n=P)).then_inc(vec_in, 16)
            for t in range(TOK):
                sp.dma_start(x_tok[:, t, :], x[0, t * P:(t + 1) * P, :]).then_inc(x_in, 16)

            def load_ada(j, q):
                n = j * (KT // 2) + q
                if n >= RING:
                    sp.wait_ge(ada_used, n - RING + 1)
                for s in range(2):
                    col = s * D + j * 2 * P
                    sp.dma_start(ada_ring[:, n % RING, :, s, :],
                                 w_ada[0, 2 * q * P:2 * (q + 1) * P, col:col + 2 * P]
                                 .rearrange("(t p) n -> p t n", p=P)).then_inc(ada_in[n % RING], 16)

            def load_gate(n, i):
                k = n * (KT // 2) + i
                if k >= 2:
                    sp.wait_ge(gate_used, k - 1)
                else:
                    sp.wait_ge(pv_done, HEADS)
                col = 2 * D + n * CH
                sp.dma_start(gate_ring[:, k % 2, :].rearrange("p (t n) -> p t n", t=2),
                             w_ada[0, 2 * i * P:2 * (i + 1) * P, col:col + CH]
                             .rearrange("(t p) n -> p t n", p=P)).then_inc(gate_in[k % 2], 16)

            def load_bias_gain(n):
                if n == 0:
                    sp.wait_ge(o_gated_ready, HEADS)
                else:
                    sp.wait_ge(gg_ready, n)
                sp.dma_start(bias_gain[:, 0, :], b_ada[0, 2 * D + n * CH:2 * D + (n + 1) * CH]
                             .partition_broadcast(P)).then_inc(bias_in, 16)
                sp.dma_start(bias_gain[:, 1, :], g_post[0, n * CH:(n + 1) * CH]
                             .partition_broadcast(P)).then_inc(bias_in, 16)

            for q in range(KT // 2):
                load_ada(0, q)
            for p, (a, kind, n, i, first, last) in enumerate(pieces):
                for j, q in ada_before.get(p, ()):
                    load_ada(j, q)
                if p >= RING:
                    sp.wait_ge(lo_done, p - RING + 1)
                dst = w_raw[:, p % RING, :]
                dst = dst.rearrange("p (t n) -> p t n", n=ROPE if kind == "kr" else CH)
                sp.dma_start(dst, piece_source(kind, n, i)).then_inc(raw_in[p % RING], 16)
                if p == 0:
                    sp.dma_start(pos_row[:, :], positions[0, :].partition_broadcast(P)).then_inc(pos_in, 16)
                    with nc.allow_non_contiguous_dma(reason="256 positions, once"):
                        sp.dma_start(pos_q[:, :], positions[0, :].rearrange("(t p) -> p t", p=P)).then_inc(pos_in, 16)
                    for k, v in enumerate((lambda_q1, lambda_k1, lambda_q2, lambda_k2)):
                        sp.dma_start(lam_in[:, k, :], v[0, :].partition_broadcast(P)).then_inc(lam_ld, 16)
                for k in gate_parts_at.get(p + 1, ()):
                    load_gate(k // (KT // 2), k % (KT // 2))
                    if k % (KT // 2) == 4:
                        load_bias_gain(k // (KT // 2))
                if kind == "wout" and n == 0 and i == 0:
                    sp.wait_ge(piece_used, last_piece("md", 3) + 1)
                    for t in range(TOK):
                        sp.dma_start(x_again[:, t, :], x[0, t * P:(t + 1) * P, :]).then_inc(x_again_in, 16)
            for k in range(2 * TOK):
                t, half = k // 2, k % 2
                sp.wait_ge(out_ready, k + 1)
                sp.dma_start(out[0, t * P:(t + 1) * P, half * (D // 2):(half + 1) * (D // 2)],
                             yg[:, t, half * (D // 2):(half + 1) * (D // 2)]).then_inc(out_done, 16)
            sp.wait_ge(out_done, 16 * 2 * TOK)

        @block.gpsimd
        def _(pool):
            nc.gpsimd.memset(ident[:, :], 0.0).then_inc(pool_step, 1)
            pool.wait_ge(pool_step, 1)
            nc.gpsimd.affine_select(out=ident[:, :], in_=ident[:, :], compare_op=ALU.not_equal, fill=1.0,
                                    base=0, pattern=[[-1, P]], channel_multiplier=1).then_inc(consts, 1)
            nc.gpsimd.memset(power[:, :], -0.5).then_inc(pool_step, 1)
            nc.gpsimd.memset(ones[:, :], 1.0).then_inc(consts, 1)
            nc.gpsimd.memset(ident_b[:, :], 0.0).then_inc(pool_step, 1)
            nc.gpsimd.memset(causal_b[:, :], 0.0).then_inc(pool_step, 1)
            nc.gpsimd.memset(causal_far[:, :], 0.0).then_inc(pool_step, 1)
            for i, f in enumerate(ROPE_FREQ):
                fill = nc.gpsimd.memset(freq[:, i:i + 1], f)
            fill.then_inc(consts, 1)

            def inverse_root(k, need, count, width):
                pool.wait_ge(need, count)
                nc.gpsimd.tensor_scalar(variance[:, k, :], sumsq[:, k, :], 1.0 / width, EPS,
                                        ALU.mult, ALU.add).then_inc(var_ready, 1)
                pool.wait_ge(var_ready, k + 1)
                nc.gpsimd.tensor_tensor(rstd[:, k, :], variance[:, k, :], power[:, :], ALU.pow).then_inc(rstd_ready, 1)

            pool.wait_ge(pool_step, 2)
            inverse_root(R_X, x_sq, TOK, D)
            pool.wait_ge(pool_step, 5)
            nc.gpsimd.affine_select(out=ident_b[:, :], in_=ident_b[:, :], compare_op=ALU.not_equal, fill=1.0,
                                    base=0, pattern=[[-1, P]], channel_multiplier=1).then_inc(consts, 1)
            nc.gpsimd.affine_select(out=causal_b[:, :], in_=causal_b[:, :], compare_op=ALU.is_ge,
                                    fill=NEG_INF / MLA_SCALE, base=0, pattern=[[-1, P]],
                                    channel_multiplier=1).then_inc(consts, 1)
            nc.gpsimd.affine_select(out=causal_far[:, :], in_=causal_far[:, :], compare_op=ALU.is_ge,
                                    fill=-NEG_INF / min(SLOPES), base=0, pattern=[[-1, P]],
                                    channel_multiplier=1).then_inc(consts, 1)
            inverse_root(R_CKV, acc_read_act, by_act.index(acc_of["ckv", 0]) + 1, RANK)
            for h in range(HEADS):
                k = R_HEAD + h
                pool.wait_ge(head_sq, h + 1)
                nc.gpsimd.tensor_scalar(in_range[:, :], sumsq[:, k, :], SQ_LIMIT, SQ_SCALE, ALU.is_lt, ALU.mult)
                nc.gpsimd.tensor_scalar(variance[:, k, :], sumsq[:, k, :], 1.0 / P, EPS * SQ_SCALE ** 2,
                                        ALU.mult, ALU.add).then_inc(var_ready, 1)
                pool.wait_ge(var_ready, k + 1)
                nc.gpsimd.tensor_tensor(variance[:, k, :], variance[:, k, :], power[:, :], ALU.pow).then_inc(root_ready, 1)
                pool.wait_ge(root_ready, h + 1)
                nc.gpsimd.tensor_tensor(rstd[:, k, :], variance[:, k, :], in_range[:, :], ALU.mult).then_inc(rstd_ready, 1)
                pool.wait_ge(rstd_ready, k + 1)
            inverse_root(R_Y, y_sums, 1, D)

        act = nc.scalar

        def act_copy_group(g, dst):
            def run(eng):
                eng.wait_ge(tr_made, g + 1)
                act.copy(dst, ps[:, group_bank(g), 0:dst_size(dst)]).then_inc(tr_copied, 1)
            return run

        def dst_size(ap):
            n = 1
            for s in ap.shape[1:]:
                n *= s
            return n

        def act_read(a, body):
            def run(eng):
                eng.wait_ge(piece_used, end[a] + 1)
                body(eng, banks(a)).then_inc(acc_read_act, 1)
            return run

        def read_q(n):
            def body(eng, b):
                for t in range(TOK):
                    ins = act.copy(q_tok[:, t, n * CH:(n + 1) * CH], ps[:, b + t, :])
                return ins
            return body

        def read_ckv(eng, b):
            for t in range(TOK):
                act.activation(act_junk[:, t, :], ps[:, b + t, :], ACT.Square, accum_out=sumsq[:, R_CKV, t:t + 1])
                ins = act.copy(stage[:, t, :], ps[:, b + t, :])
            return ins

        def read_kr(eng, b):
            for t in range(TOK):
                ins = act.copy(kr_tok[:, t, :], ps[:, b + t, 0:ROPE])
            return ins

        def act_silu(n):
            def run(eng):
                eng.wait_ge(acc_read_dve, dve_reads("gate", n))
                if n == 0:
                    eng.wait_ge(ada_used, (KT // 2) ** 2)
                act.activation(silu_gate[:, n // 2, :, n % 2 * CH:(n % 2 + 1) * CH], gate_part_sum[:, n, :, :],
                               ACT.Silu).then_inc(silu_ready, 1)
            return run

        def act_early(n):
            def run(eng):
                eng.wait_ge(piece_used, early_end[n] + 1)
                act.copy(gate_part_sum[:, n, :, :], ps[:, 6:8, :]).then_inc(early_read, 1)
            return run

        silu_ready, early_read = sem("silu_ready"), sem("early_read")

        def read_ukv(n):
            def body(eng, b):
                if n >= 2:
                    eng.wait_ge(tr_made, G_KN + n - 1)
                else:
                    eng.wait_ge(tr_made, G_CKV + 2)
                for t in range(TOK):
                    both = ps[:, b + t, :].rearrange("p (h w d) -> p h w d", h=2, w=2)
                    act.copy(stage[:, t, (n % 2) * 256:(n % 2) * 256 + 256].rearrange("p (h d) -> p h d", h=2),
                             both[:, :, 0, :])
                    ins = act.copy(v_mla[:, t, 2 * n:2 * n + 2, :], both[:, :, 1, :])
                return ins
            return body

        def read_vd(n):
            def body(eng, b):
                for t in range(TOK):
                    ins = act.copy(v_diff[:, t, n * CH:(n + 1) * CH], ps[:, b + t, :])
                return ins
            return body

        def read_qk(k):
            def body(eng, b):
                eng.wait_ge(tr_made, G_D + 2 * k)
                for t in range(TOK):
                    ins = act.copy(stage[:, t, :], ps[:, b + t, :])
                return ins
            return body

        def read_sigmoid(k):
            def body(eng, b):
                if k == 0:
                    eng.wait_ge(tr_made, N_GROUPS)
                else:
                    eng.wait_ge(acc_read_dve, 4 + k)
                for t in range(TOK):
                    ins = act.activation(stage[:, t, :], ps[:, b + t, :], ACT.Sigmoid)
                return ins
            return body

        def act_ckv_hi(eng):
            for g in range(2):
                eng.wait_ge(tr_made, G_CKV + g + 1)
                for b in range(2):
                    k = 2 * g + b
                    ins = act.activation(ckvT_hi[:, k, :], ps[:, 4 + (G_CKV + g) % 4, b * SEQ:(b + 1) * SEQ],
                                         ACT.Copy, scale=cols[:, V_GKV + k:V_GKV + k + 1])
                ins.then_inc(ckv_hi, 1)
            eng.wait_ge(ckv_lo, 2)
            act.copy(lam_dummy[:, 0:1], cols[:, 0:1]).then_inc(tr_copied, 2)

        lam_dummy = sb("lam_dummy", [P, 1], F32)

        def act_exps(m):
            def run(eng):
                eng.wait_ge(max_ready, m + 1)
                if m < HEADS:
                    if m >= 2:
                        eng.wait_ge(pT_made, m - 1)
                    for b, (lo, hi) in enumerate(((0, P), (P, KEYS))):
                        ins = act.activation(probs[:, m % 2, 0, lo:hi], ps[:, 4, lo:hi], ACT.Exp,
                                             bias=neg_max[:, m % 2, b:b + 1], scale=MLA_SCALE,
                                             accum_out=sums[:, m % 2, b:b + 1])
                else:
                    for b, (lo, hi) in enumerate(((0, P), (P, KEYS))):
                        for w in range(2):
                            s = 2 * b + w
                            ins = act.activation(probs[:, m % 2, w, lo:hi], probs[:, m % 2, w, lo:hi], ACT.Exp,
                                                 bias=neg_max[:, m % 2, s:s + 1], scale=DIFF_SCALE,
                                                 accum_out=sums[:, m % 2, s:s + 1])
                ins.then_inc(exps_done, 1)
            return run

        def act_copy_probs(m):
            def run(eng):
                eng.wait_ge(pT_made, m + 1)
                if m >= 1:
                    eng.wait_ge(pv_done, m)
                act.copy(probsT[:, :], ps[:, 6, 0:KEYS]).then_inc(pT_copied, 1)
            return run

        def act_o_hi(m):
            def run(eng):
                eng.wait_ge(oT_made, m + 1)
                scale = 1.0 if m < HEADS else cols[:, NVEC:NVEC + 1]
                act.activation(o_hi[:, m, :], ps[:, 7, SEQ:2 * SEQ], ACT.Copy, scale=scale).then_inc(o_hi_ready, 1)
            return run

        def act_m_hi(n):
            def run(eng):
                eng.wait_ge(mT_made, n + 1)
                act.copy(m_hi[:, 4 * n:4 * n + 4, :], ps[:, 4:6, :]).then_inc(m_hi_ready, 1)
            return run

        def read_y(n):
            def body(eng, b):
                eng.wait_ge(acc_read_act, by_act.index(acc_of["wout", n]))
                for t in range(TOK):
                    ins = act.activation(act_junk[:, t, :], ps[:, b + t, :], ACT.Square, accum_out=y_sq[:, t, n:n + 1])
                return ins
            return body

        act_junk = sb("act_junk", [P, TOK, CH], F32, r_o_hi)

        for n in range(3):
            act_after[PH1 + n].append(act_read(n, read_q(n)))
        e = last_piece("ckv", 0)
        act_after[e + 3].append(act_read(acc_of["ckv", 0], read_ckv))
        act_after[last_piece("kr", 0) + 3].append(act_read(acc_of["kr", 0], read_kr))
        for n in range(4):
            act_after[early_end[n] + 2].append(act_early(n))
            act_after[last_piece("gate", n) + 4].append(act_silu(n))
            act_after[last_piece("ukv", n) + 3].append(act_read(acc_of["ukv", n], read_ukv(n)))
        for n in range(2):
            act_after[last_piece("vd", n) + 3].append(act_read(acc_of["vd", n], read_vd(n)))
        for k, (kind, n) in enumerate((("qd", 0), ("qd", 1), ("kd", 0), ("kd", 1))):
            act_after[last_piece(kind, n) + 3].append(act_read(acc_of[kind, n], read_qk(k)))
        for n in range(4):
            act_after[last_piece("mm", n) + 3].append(act_read(acc_of["mm", n], read_sigmoid(n)))
            act_after[last_piece("md", n) + 3].append(act_read(acc_of["md", n], read_sigmoid(4 + n)))
            act_after[min(last_piece("wout", n) + 3, NP - 1)].append(act_read(acc_of["wout", n], read_y(n)))

        q_end = PH1
        group_at = {}
        for g in range(4):
            group_at[G_QN + g] = (q_end + 4 + g // 2, q_end + 8 + g // 2)
        for g in range(2):
            group_at[G_QR + g] = (q_end + 9, q_end + 13)
            group_at[G_CKV + g] = (last_piece("ckv", 0) + 6, last_piece("ckv", 0) + 9)
        group_at[G_KR] = (last_piece("kr", 0) + 7, last_piece("kr", 0) + 10)
        for n in range(4):
            group_at[G_KN + n] = (last_piece("ukv", n) + 2, last_piece("ukv", n) + 6)
        for k, (kind, n) in enumerate((("qd", 0), ("qd", 1), ("kd", 0), ("kd", 1))):
            for g in range(2):
                group_at[G_D + 2 * k + g] = (last_piece(kind, n) + 2 + 2 * g, last_piece(kind, n) + 5 + 2 * g)
        for g in range(N_GROUPS):
            at_pe, at_act = group_at[g]
            if g < G_QR:
                dst = qnT[:, 2 * g:2 * g + 2, :]
            elif g < G_CKV:
                dst = qrT[:, 2 * (g - G_QR):2 * (g - G_QR) + 2, :]
            elif g < G_KR:
                if g == G_CKV:
                    act_after[at_act].append(act_ckv_hi)
                continue
            elif g == G_KR:
                dst = krT[:, :]
            elif g < G_D:
                dst = knT[:, 2 * (g - G_KN):2 * (g - G_KN) + 2, :]
            else:
                k = g - G_D
                dst = (qdT if k < 4 else kdT)[:, 2 * (k % 4):2 * (k % 4) + 2, :]
            act_after[at_act].append(act_copy_group(g, dst))
        for h in range(HEADS):
            s, t, v, g = mla_at[h]
            act_after[s + 5].append(act_exps(h))
            act_after[t + 4].append(act_copy_probs(h))
            act_after[g + 4].append(act_o_hi(h))
            s, t, v, g = diff_at[h]
            act_after[s + 6].append(act_exps(HEADS + h))
            act_after[t + 4].append(act_copy_probs(HEADS + h))
            act_after[g + 4].append(act_o_hi(HEADS + h))
        merge_at = [last_piece("wod", n) + 5 for n in range(4)]
        for n in range(4):
            act_after[merge_at[n] + 4].append(act_m_hi(n))

        @block.scalar
        def _(eng):
            for t in range(TOK):
                eng.wait_ge(x_in, 16 * TOK)
                act.activation(xnT[:, 0:KT // 2, :].rearrange("p k s -> p (k s)"), x_tok[:, t, :], ACT.Square,
                               accum_out=sumsq[:, R_X, t:t + 1]).then_inc(x_sq, 1)
                eng.wait_ge(x_sq, t + 1)
            eng.wait_ge(cols_T, 1)
            act.copy(cols[:, 0:NVEC], ps[:, 7, 0:NVEC]).then_inc(cols_ready, 1)
            for g in range(KT // 2):
                eng.wait_ge(xT_made, g + 1)
                act.copy(xnT[:, 2 * g:2 * g + 2, :], ps[:, 6 + g % 2, :]).then_inc(xT_copied, 1)

            def make_h_hi(j):
                eng.wait_ge(mod_ready, j + 1)
                if j >= 1:
                    eng.wait_ge(h_lo_ready, j)
                for b in range(2):
                    k = 2 * j + b
                    act.activation(stage[:, 0, b * SEQ:(b + 1) * SEQ], xnT[:, k, :], ACT.Identity,
                                   bias=mod_shift[:, k:k + 1], scale=mod_gain[:, k:k + 1])
                    ins = act.activation(h_hi[:, k, :], xnT[:, k, :], ACT.Identity,
                                         bias=mod_shift[:, k:k + 1], scale=mod_gain[:, k:k + 1])
                ins.then_inc(h_hi_ready, 1)

            eng.wait_ge(xT_copied, KT // 2)
            make_h_hi(0)
            for p, (a, kind, n, i, first, last) in enumerate(pieces):
                eng.wait_ge(raw_in[p % RING], 16 * (p // RING + 1))
                if p >= RING:
                    eng.wait_ge(piece_used, p - RING + 1)
                act.copy(w_hi[:, p % RING, :], w_raw[:, p % RING, :]).then_inc(hi_done, 1)
                if p in pair_end:
                    make_h_hi(pair_end[p] + 1)
                if p == 5:
                    eng.wait_ge(angles_ready, 1)
                    act.activation(sin[:, :, :].rearrange("p t i -> p (t i)"), angle[:, 3, :], ACT.Sin)
                    act.activation(cos[:, :, :].rearrange("p t i -> p (t i)"), angle[:, 4, :], ACT.Sin).then_inc(cossin_ready, 1)
                    eng.wait_ge(lam_dots, 1)
                    act.activation(lam_exp[:, :], lam_dot[:, :], ACT.Exp).then_inc(lam_exps, 1)
                for work in act_after[p]:
                    work(eng)

        dve = nc.vector
        steps = [0]

        def link(eng, ins):
            steps[0] += 1
            ins.then_inc(dve_step, 1)
            eng.wait_ge(dve_step, steps[0])

        def dve_rope(t, src, dst, heads):
            def run(eng):
                c_ = cos[:, t:t + 1, :].to_broadcast([P, heads, HALF])
                s_ = sin[:, t:t + 1, :].to_broadcast([P, heads, HALF])
                a, b = rot_a[:, 0:heads, :], rot_b[:, 0:heads, :]
                x1, x2 = src[:, :, 0:HALF], src[:, :, HALF:ROPE]
                dve.tensor_tensor(a, x1, c_, ALU.mult)
                link(eng, dve.tensor_tensor(b, x2, s_, ALU.mult))
                link(eng, dve.tensor_tensor(dst[:, :, 0:HALF], a, b, ALU.subtract))
                dve.tensor_tensor(a, x2, c_, ALU.mult)
                link(eng, dve.tensor_tensor(b, x1, s_, ALU.mult))
                link(eng, dve.tensor_tensor(dst[:, :, HALF:ROPE], a, b, ALU.add))
            return run

        def q_rope(t):
            def run(eng):
                if t == 0:
                    eng.wait_ge(acc_read_act, 3)
                    eng.wait_ge(cossin_ready, 1)
                src = q_tok[:, t, :].rearrange("p (h d) -> p h d", d=QH)[:, :, NOPE:QH]
                dve_rope(t, src, qr_tok[:, t, :, :], HEADS)(eng)
            return run

        def kr_rope(eng):
            eng.wait_ge(acc_read_act, by_act.index(acc_of["kr", 0]) + 1)
            for t in range(TOK):
                for copy in range(2):
                    dve_rope(t, kr_tok[:, t:t + 1, :], kr_dup[:, t:t + 1, copy * ROPE:(copy + 1) * ROPE], 1)(eng)

        def scale_ckv(eng):
            eng.wait_ge(acc_read_act, by_act.index(acc_of["ckv", 0]) + 1)
            eng.wait_ge(rstd_ready, R_CKV + 1)
            for t in range(TOK):
                ins = dve.tensor_scalar(stage[:, t, :], stage[:, t, :], rstd[:, R_CKV, t:t + 1], None, ALU.mult)
            ins.then_inc(ckv_scaled, 1)

        def dve_ckv_lo(eng):
            for g in range(2):
                eng.wait_ge(ckv_hi, g + 1)
                for b in range(2):
                    k = 2 * g + b
                    link(eng, dve.tensor_scalar(tmp[:, b * SEQ:(b + 1) * SEQ],
                                                ps[:, 4 + (G_CKV + g) % 4, b * SEQ:(b + 1) * SEQ],
                                                cols[:, V_GKV + k:V_GKV + k + 1], None, ALU.mult))
                link(eng, dve.tensor_tensor(ckvT_lo[:, 2 * g:2 * g + 2, :].rearrange("p k s -> p (k s)"), tmp[:, :],
                                            ckvT_hi[:, 2 * g:2 * g + 2, :].rearrange("p k s -> p (k s)").bitcast(F32),
                                            ALU.subtract))
            dve.memset(gain_tmp[:, 0:1], 0.0).then_inc(ckv_lo, 2)

        def mla_max(h):
            def run(eng):
                eng.wait_ge(scores_ready, h + 1)
                dve.reduce_max(maxes[:, h % 2, 0:1], ps[:, 4, 0:P], AX_X)
                link(eng, dve.reduce_max(maxes[:, h % 2, 1:2], ps[:, 4, P:KEYS], AX_X))
                if h >= 2:
                    eng.wait_ge(exps_done, h - 1)
                dve.tensor_scalar(neg_max[:, h % 2, 0:2], maxes[:, h % 2, 0:2], -MLA_SCALE, None,
                                  ALU.mult).then_inc(max_ready, 1)
            return run

        def add_gate(n):
            def run(eng):
                a = acc_of["gate", n]
                eng.wait_ge(piece_used, end[a] + 1)
                eng.wait_ge(early_read, n + 1)
                part = gate_part_sum[:, n, :, :]
                dve.tensor_tensor(part, part, ps[:, banks(a):banks(a) + TOK, :], ALU.add).then_inc(acc_read_dve, 1)
            return run

        def mla_out(h):
            def run(eng):
                eng.wait_ge(pv_done, h + 1)
                link(eng, dve.reciprocal(recip[:, h % 2, 0:2], sums[:, h % 2, 0:2]))
                if h == 0:
                    eng.wait_ge(silu_ready, 4)
                if h >= 1:
                    eng.wait_ge(oT_made, h)
                for t in range(TOK):
                    ins = dve.scalar_tensor_tensor(
                        out=o_gated[:, t, :], in0=ps[:, 7, t * P:(t + 1) * P], scalar=recip[:, h % 2, t:t + 1],
                        in1=silu_gate[:, 0, t, h * P:(h + 1) * P], op0=ALU.mult, op1=ALU.mult)
                ins.then_inc(o_gated_ready, 1)
            return run

        def dve_o_lo(m):
            def run(eng):
                src = ps[:, 7, SEQ:2 * SEQ]
                eng.wait_ge(o_hi_ready, m + 1)
                if m >= HEADS:
                    link(eng, dve.tensor_scalar(tmp[:, 0:SEQ], src, cols[:, NVEC:NVEC + 1], None, ALU.mult))
                    src = tmp[:, 0:SEQ]
                link(eng, dve.tensor_tensor(o_lo[:, m, :], src, o_hi[:, m, :].bitcast(F32), ALU.subtract))
                dve.memset(gain_tmp[:, 0:1], 0.0).then_inc(o_lo_ready, 1)
            return run

        def diff_scores(h):
            m = HEADS + h
            def run(eng):
                if m % 2 == h % 2 and m >= 2:
                    eng.wait_ge(pT_made, m - 1)
                eng.wait_ge(scores_ready, m + 1)
                dst = probs[:, m % 2, :, :]
                link(eng, dve.scalar_tensor_tensor(
                    out=dst, in0=dist[:, :].unsqueeze(1).to_broadcast([P, 2, KEYS]),
                    scalar=-SLOPES[h] / DIFF_SCALE, in1=ps[:, 4:6, 0:KEYS], op0=ALU.mult, op1=ALU.add))
                dve.tensor_reduce(maxes[:, m % 2, 0:2], dst[:, :, 0:P], AX_X, ALU.max).then_inc(scores_read, 1)
                link(eng, dve.tensor_reduce(maxes[:, m % 2, 2:4], dst[:, :, P:KEYS], AX_X, ALU.max))
                dve.tensor_scalar(neg_max[:, m % 2, :], maxes[:, m % 2, :], -DIFF_SCALE, None,
                                  ALU.mult).then_inc(max_ready, 1)
            return run

        def diff_weights(h):
            m = HEADS + h
            def run(eng):
                eng.wait_ge(exps_done, m + 1)
                link(eng, dve.reciprocal(recip[:, m % 2, :], sums[:, m % 2, :]))
                second = recip[:, m % 2, :].rearrange("p (b w) -> p b w", w=2)[:, :, 1]
                link(eng, dve.tensor_scalar(second, second, lam[:, 0:1], None, ALU.mult))
                spans = ((0, P), (P, KEYS))
                for b, (lo, hi) in enumerate(spans):
                    ins = dve.tensor_scalar(probs[:, m % 2, 1, lo:hi], probs[:, m % 2, 1, lo:hi],
                                            recip[:, m % 2, 2 * b + 1:2 * b + 2], None, ALU.mult)
                link(eng, ins)
                for b, (lo, hi) in enumerate(spans):
                    ins = dve.scalar_tensor_tensor(
                        out=probs[:, m % 2, 0, lo:hi], in0=probs[:, m % 2, 0, lo:hi],
                        scalar=recip[:, m % 2, 2 * b:2 * b + 1], in1=probs[:, m % 2, 1, lo:hi],
                        op0=ALU.mult, op1=ALU.subtract)
                ins.then_inc(weights_ready, 1)
            return run

        def head_squares(h):
            def run(eng):
                eng.wait_ge(pv_done, HEADS + h + 1)
                link(eng, dve.tensor_scalar(tmp[:, 0:SEQ], ps[:, 7, 0:SEQ], SQ_SCALE, SQ_CLAMP, ALU.mult, ALU.min))
                for t in range(TOK):
                    part = tmp[:, t * P:(t + 1) * P]
                    ins = dve.scalar_tensor_tensor(out=tmp[:, SEQ + t * P:SEQ + (t + 1) * P], in0=part, scalar=-SQ_CLAMP,
                                                   in1=part, op0=ALU.max, op1=ALU.mult,
                                                   accum_out=sumsq[:, R_HEAD + h, t:t + 1])
                ins.then_inc(head_sq, 1)
            return run

        def diff_out(h):
            def run(eng):
                eng.wait_ge(rstd_ready, R_HEAD + h + 1)
                eng.wait_ge(oT_made, HEADS + h)
                for t in range(TOK):
                    ins = dve.scalar_tensor_tensor(
                        out=o_gated[:, t, :], in0=ps[:, 7, t * P:(t + 1) * P], scalar=rstd[:, R_HEAD + h, t:t + 1],
                        in1=silu_gate[:, 1, t, h * P:(h + 1) * P], op0=ALU.mult, op1=ALU.mult)
                ins.then_inc(o_gated_ready, 1)
            return run

        def merge_mla(n):
            def run(eng):
                a = acc_of["wom", n]
                eng.wait_ge(piece_used, end[a] + 1)
                eng.wait_ge(acc_read_act, by_act.index(acc_of["mm", n]) + 1)
                for t in range(TOK):
                    ins = dve.tensor_tensor(merged[:, t, n * CH:(n + 1) * CH], ps[:, banks(a) + t, :],
                                            stage[:, t, :], ALU.mult)
                ins.then_inc(acc_read_dve, 1)
            return run

        def merge_diff(n):
            def run(eng):
                a = acc_of["wod", n]
                eng.wait_ge(piece_used, end[a] + 1)
                eng.wait_ge(acc_read_act, by_act.index(acc_of["md", n]) + 1)
                for t in range(TOK):
                    link(eng, dve.tensor_tensor(stage[:, t, :], ps[:, banks(a) + t, :], stage[:, t, :], ALU.mult))
                    part = merged[:, t, n * CH:(n + 1) * CH]
                    link(eng, dve.tensor_tensor(part, part, stage[:, t, :], ALU.add))
                dve.memset(gain_tmp[:, 0:1], 0.0).then_inc(acc_read_dve, 1)
            return run

        def dve_m_lo(n):
            def run(eng):
                eng.wait_ge(m_hi_ready, n + 1)
                dve.tensor_tensor(m_lo[:, 4 * n:4 * n + 4, :].rearrange("p (b k) s -> p b (k s)", b=2), ps[:, 4:6, :],
                                  m_hi[:, 4 * n:4 * n + 4, :].rearrange("p (b k) s -> p b (k s)", b=2).bitcast(F32),
                                  ALU.subtract).then_inc(m_lo_ready, 1)
            return run

        acc_steps = [0, 0]

        def add_rows(eng, src, cc, t, fresh, signal):
            if fresh:
                ins = dve.tensor_scalar(ada_acc[:, t, :], src, cc, None, ALU.mult)
            else:
                eng.wait_ge(*acc_steps[t])
                ins = dve.scalar_tensor_tensor(out=ada_acc[:, t, :], in0=src, scalar=cc, in1=ada_acc[:, t, :],
                                               op0=ALU.mult, op1=ALU.add)
            if signal:
                sem_, value = signal
                ins.then_inc(sem_, 1)
                acc_steps[t] = (sem_, value)
            else:
                steps[0] += 1
                ins.then_inc(dve_step, 1)
                acc_steps[t] = (dve_step, steps[0])

        def gate_part(k):
            def run(eng):
                n, i = k // (KT // 2), k % (KT // 2)
                eng.wait_ge(gate_in[k % 2], 16 * (k // 2 + 1))
                if i == 0 and n >= 1:
                    eng.wait_ge(gate_summed, n)
                for t in range(2):
                    add_rows(eng, gate_ring[:, k % 2, t * CH:(t + 1) * CH],
                             cols[:, V_C + 2 * i + t:V_C + 2 * i + t + 1], t, i == 0,
                             (gate_used, k + 1) if t else None)
            return run

        def gate_finish(n):
            def run(eng):
                eng.wait_ge(gate_summed, n + 1)
                eng.wait_ge(bias_in, 32 * (n + 1))
                link(eng, dve.tensor_tensor(tmp[:, :], ps[:, 6, :], bias_gain[:, 0, :], ALU.add))
                dve.tensor_tensor(post_gain[:, n * CH:(n + 1) * CH], tmp[:, :], bias_gain[:, 1, :],
                                  ALU.mult).then_inc(gg_ready, 1)
                eng.wait_ge(gg_ready, n + 1)
            return run

        def y_gain(n):
            def run(eng):
                a = acc_of["wout", n]
                eng.wait_ge(acc_read_act, by_act.index(a) + 1)
                eng.wait_ge(gg_ready, n + 1)
                if n == 0:
                    eng.wait_ge(piece_used, last_piece("md", 3) + 1)
                for t in range(TOK):
                    ins = dve.tensor_tensor(yg[:, t, n * CH:(n + 1) * CH], ps[:, banks(a) + t, :],
                                            post_gain[:, n * CH:(n + 1) * CH], ALU.mult)
                ins.then_inc(acc_read_dve, 1)
            return run

        dve_after[PH1 + 4].append(q_rope(0))
        dve_after[PH1 + 5].append(q_rope(1))
        dve_after[last_piece("ckv", 0) + 4].append(scale_ckv)
        dve_after[last_piece("kr", 0) + 4].append(kr_rope)
        dve_after[group_at[G_CKV][1]].append(dve_ckv_lo)
        for h in range(HEADS):
            s, t, v, g = mla_at[h]
            dve_after[s + 4].append(mla_max(h))
            dve_after[v + 4].append(mla_out(h))
            dve_after[g + 4].append(dve_o_lo(h))
            s, t, v, g = diff_at[h]
            dve_after[s + 4].append(diff_scores(h))
            dve_after[s + 8].append(diff_weights(h))
            dve_after[v + 4].append(head_squares(h))
            dve_after[v + 5].append(diff_out(h))
            dve_after[g + 4].append(dve_o_lo(HEADS + h))
        for n in range(4):
            dve_after[last_piece("wom", n) + 3].append(merge_mla(n))
            dve_after[last_piece("wod", n) + 3].append(merge_diff(n))
            dve_after[merge_at[n] + 4].append(dve_m_lo(n))
            dve_after[last_piece("gate", n) + 3].append(add_gate(n))
            dve_after[gate_end[n] + 4].append(gate_finish(n))
            dve_after[min(last_piece("wout", n) + 3, NP - 1)].append(y_gain(n))

        for p, parts in gate_parts_at.items():
            for k in parts:
                dve_after[p].append(gate_part(k))

        @block.vector
        def _(eng):
            eng.wait_ge(cols_ready, 1)
            link(eng, dve.tensor_scalar(cols[:, NVEC:NVEC + 1], cols[:, V_GSUB:V_GSUB + 1], 1.0 - LAMBDA_INIT, None,
                                        ALU.mult))

            def ada_part(j, q):
                n = j * (KT // 2) + q
                if q == 0 and j >= 1:
                    eng.wait_ge(ada_summed, j)
                eng.wait_ge(ada_in[n % RING], 32 * (n // RING + 1))
                for t in range(2):
                    add_rows(eng, ada_ring[:, n % RING, t, :, :].rearrange("p s n -> p (s n)"),
                             cols[:, V_C + 2 * q + t:V_C + 2 * q + t + 1], t, q == 0,
                             (ada_used, n + 1) if t else None)

            def modulation(j):
                eng.wait_ge(ada_summed, j + 1)
                k = 2 * j
                dve.tensor_tensor(mod_shift[:, k:k + 2], ps[:, 6, 0:2], cols[:, V_SHIFT + k:V_SHIFT + k + 2], ALU.add)
                link(eng, dve.scalar_tensor_tensor(out=gain_tmp[:, 0:2], in0=ps[:, 6, 2:4], scalar=1.0,
                                                   in1=cols[:, V_SCALE + k:V_SCALE + k + 2],
                                                   op0=ALU.add, op1=ALU.add))
                dve.tensor_tensor(mod_gain[:, k:k + 2], gain_tmp[:, 0:2], cols[:, V_GPRE + k:V_GPRE + k + 2],
                                  ALU.mult).then_inc(mod_ready, 1)

            def make_h_lo(j):
                eng.wait_ge(h_hi_ready, j + 1)
                dve.tensor_tensor(h_lo[:, 2 * j:2 * j + 2, :].rearrange("p k s -> p (k s)"), stage[:, 0, :],
                                  h_hi[:, 2 * j:2 * j + 2, :].rearrange("p k s -> p (k s)").bitcast(F32),
                                  ALU.subtract).then_inc(h_lo_ready, 1)

            def angles():
                eng.wait_ge(pos_in, 32)
                eng.wait_ge(consts, 3)
                link(eng, dve.tensor_copy(pos_qf[:, :], pos_q[:, :]))
                ang, k_, r_, s_, c_ = (angle[:, i, :] for i in range(5))
                for t in range(TOK):
                    link(eng, dve.tensor_scalar(ang[:, t * HALF:(t + 1) * HALF], freq[:, :], pos_qf[:, t:t + 1], None,
                                                ALU.mult))

                def turns(dst, src, turn):
                    link(eng, dve.tensor_scalar(dst, src, 1.0 / turn, ROUND_MAGIC, ALU.mult, ALU.add))
                    link(eng, dve.tensor_scalar(dst, dst, ROUND_MAGIC, None, ALU.subtract))

                def less(dst, k, part, src):
                    link(eng, dve.scalar_tensor_tensor(out=dst, in0=k, scalar=-part, in1=src, op0=ALU.mult, op1=ALU.add))

                turns(k_, ang, BIG_TURN)
                less(ang, k_, BIG_PARTS[0], ang)
                less(ang, k_, BIG_PARTS[1], ang)
                link(eng, dve.tensor_scalar(r_, k_, -BIG_PARTS[2], None, ALU.mult))
                link(eng, dve.tensor_tensor(s_, ang, r_, ALU.add))
                turns(k_, s_, 2.0 * math.pi)
                less(ang, k_, TURN_PARTS[0], ang)
                less(ang, k_, TURN_PARTS[1], ang)
                link(eng, dve.tensor_tensor(ang, ang, r_, ALU.add))
                less(ang, k_, TURN_PARTS[2], ang)
                link(eng, dve.tensor_scalar(s_, ang, 3.1415925, -3.1415925, ALU.min, ALU.max))
                link(eng, dve.tensor_scalar(c_, s_, -1.0, None, ALU.mult))
                link(eng, dve.tensor_tensor(c_, c_, s_, ALU.max))
                link(eng, dve.tensor_scalar(c_, c_, -1.0, math.pi / 2, ALU.mult, ALU.add))
                dve.memset(gain_tmp[:, 0:1], 0.0).then_inc(angles_ready, 1)
                eng.wait_ge(lam_ld, 64)
                link(eng, dve.tensor_tensor(lam_prod[:, 0, :], lam_in[:, 0, :], lam_in[:, 1, :], ALU.mult))
                link(eng, dve.tensor_tensor(lam_prod[:, 1, :], lam_in[:, 2, :], lam_in[:, 3, :], ALU.mult))
                dve.tensor_reduce(lam_dot[:, :], lam_prod[:, :, :], AX_X, ALU.add).then_inc(lam_dots, 1)

            def distances():
                eng.wait_ge(consts, 6)
                link(eng, dve.tensor_copy(tmp[:, 0:SEQ], pos_row[:, :]))
                for lo, t, n in ((0, 0, P), (P, 1, SEQ)):
                    d_, n_ = dist[:, lo:lo + n], tmp[:, SEQ:SEQ + n]
                    link(eng, dve.tensor_scalar(d_, tmp[:, 0:n], pos_qf[:, t:t + 1], None, ALU.subtract))
                    link(eng, dve.tensor_scalar(n_, d_, -1.0, None, ALU.mult))
                    link(eng, dve.tensor_tensor(d_, d_, n_, ALU.max))
                for lo in (0, SEQ):
                    link(eng, dve.tensor_tensor(dist[:, lo:lo + P], dist[:, lo:lo + P], causal_far[:, :], ALU.add))
                eng.wait_ge(lam_exps, 1)
                link(eng, dve.scalar_tensor_tensor(out=lam[:, :], in0=lam_exp[:, 0:1], scalar=LAMBDA_INIT,
                                                   in1=lam_exp[:, 1:2], op0=ALU.add, op1=ALU.subtract))

            for q in range(KT // 2):
                ada_part(0, q)
                if q == 2:
                    eng.wait_ge(rstd_ready, 1)
                    for t in range(TOK):
                        dve.tensor_scalar(x_tok[:, t, :], x_tok[:, t, :], rstd[:, R_X, t:t + 1], None,
                                          ALU.mult).then_inc(xn_ready, 1)
            modulation(0)
            make_h_lo(0)
            for p, (a, kind, n, i, first, last) in enumerate(pieces):
                for j, q in ada_before.get(p, ()):
                    ada_part(j, q)
                    if q == 0 and j >= 2:
                        make_h_lo(j - 1)
                eng.wait_ge(hi_done, p + 1)
                dve.tensor_tensor(w_lo[:, p % RING, :], w_raw[:, p % RING, :],
                                  w_hi[:, p % RING, :].bitcast(F32), ALU.subtract).then_inc(lo_done, 1)
                if p in pair_end:
                    modulation(pair_end[p] + 1)
                    if pair_end[p] + 2 == KT // 2:
                        make_h_lo(pair_end[p] + 1)
                if p == 1:
                    angles()
                if p == first_part[2][0]:
                    distances()
                for work in dve_after[p]:
                    work(eng)
            eng.wait_ge(acc_read_act, len(by_act))
            dve.tensor_reduce(sumsq[:, R_Y, :], y_sq[:, :, :], AX_X, ALU.add).then_inc(y_sums, 1)
            eng.wait_ge(x_again_in, 16 * TOK)
            eng.wait_ge(acc_read_dve, len(by_dve) + 4)
            eng.wait_ge(rstd_ready, NR)
            for k in range(2 * TOK):
                t, half = k // 2, k % 2
                part = slice(half * (D // 2), (half + 1) * (D // 2))
                dve.scalar_tensor_tensor(out=yg[:, t, part], in0=yg[:, t, part], scalar=rstd[:, R_Y, t:t + 1],
                                         in1=x_again[:, t, part], op0=ALU.mult, op1=ALU.add).then_inc(out_ready, 1)

        @block.tensor
        def _(pe):
            mm = nc.tensor.matmul
            tr = nc.tensor.transpose

            sum_before = {first_part[j][-1]: j + 1 for j in range(KT // 2 - 1)}

            def ada_sum(j):
                pe.wait_ge(ada_used, (j + 1) * (KT // 2))
                if j == 0:
                    pe.wait_ge(xT_copied, KT // 2)
                else:
                    pe.wait_ge(mod_ready, j)
                if j >= EARLY:
                    pe.wait_ge(early_read, j - EARLY + 1)
                for b in range(4):
                    for t in range(2):
                        ins = mm(ps[:, 6, b:b + 1], lhsT=ada_acc[:, t, b * P:(b + 1) * P], rhs=ones[:, 0:1],
                                 start=t == 0, stop=t == 1)
                ins.then_inc(ada_summed, 1)

            def group(g):
                bank = group_bank(g)
                if g == G_QN:
                    pe.wait_ge(acc_read_act, 3)
                    pe.wait_ge(mod_ready, KT // 2)
                if g == G_QR:
                    pe.wait_ge(lo_done, PH1 + 6 + 1)
                if g == G_CKV:
                    pe.wait_ge(ckv_scaled, 1)
                if g == G_KR:
                    pe.wait_ge(lo_done, last_piece("kr", 0) + 5 + 1)
                if G_KN <= g < G_D:
                    pe.wait_ge(acc_read_act, by_act.index(acc_of["ukv", g - G_KN]) + 1)
                if g >= G_D:
                    kind, n = (("qd", 0), ("qd", 1), ("kd", 0), ("kd", 1))[(g - G_D) // 2]
                    pe.wait_ge(acc_read_act, by_act.index(acc_of[kind, n]) + 1)
                if g >= 4:
                    pe.wait_ge(tr_copied, g - 3 if g < G_D else g)
                for b in range(2):
                    if g == G_KR and b:
                        break
                    for t in range(TOK):
                        if g < G_QR:
                            src = q_tok[:, t, (2 * g + b) * QH:(2 * g + b) * QH + NOPE]
                        elif g < G_CKV:
                            k = 2 * (2 * (g - G_QR) + b)
                            src = qr_tok[:, t, k:k + 2, :].rearrange("p h d -> p (h d)")
                        elif g < G_KR:
                            k = 2 * (g - G_CKV) + b
                            src = stage[:, t, k * P:(k + 1) * P]
                        elif g == G_KR:
                            src = kr_dup[:, t, :]
                        elif g < G_D:
                            col = (g - G_KN) % 2 * 256 + b * P
                            src = stage[:, t, col:col + P]
                        else:
                            k = 2 * ((g - G_D) % 2) + b
                            src = stage[:, t, k * P:(k + 1) * P]
                        ins = tr(ps[:, bank, b * SEQ + t * P:b * SEQ + (t + 1) * P], src, ident[:, :])
                ins.then_inc(tr_made, 1)

            def mla_scores(h):
                pe.wait_ge(tr_copied, G_D)
                if h >= 1:
                    pe.wait_ge(exps_done, h)
                r = ROPE * (h % 2)
                for t, (lo, keys) in enumerate(((0, P), (P, SEQ))):
                    q = slice(t * P, (t + 1) * P)
                    o = ps[:, 4, lo:lo + keys]
                    mm(o, lhsT=qnT[:, h, q], rhs=knT[:, h, 0:keys], start=True, stop=False)
                    mm(o, lhsT=qrT[r:r + ROPE, h // 2, q], rhs=krT[r:r + ROPE, 0:keys], start=False, stop=False)
                    ins = mm(ps[:, 4, lo + keys - P:lo + keys], lhsT=ident_b[:, :], rhs=causal_b[:, :],
                             start=False, stop=True)
                ins.then_inc(scores_ready, 1)

            def diff_scores_pe(h):
                if h == 0:
                    pe.wait_ge(tr_copied, N_GROUPS)
                else:
                    pe.wait_ge(scores_read, h)
                for w in range(2):
                    for t, (lo, keys) in enumerate(((0, P), (P, SEQ))):
                        ins = mm(ps[:, 4 + w, lo:lo + keys], lhsT=qdT[w * DQK:(w + 1) * DQK, h, t * P:(t + 1) * P],
                                 rhs=kdT[w * DQK:(w + 1) * DQK, h, 0:keys], start=True, stop=True)
                ins.then_inc(scores_ready, 1)

            def transpose_probs(m):
                if m < HEADS:
                    pe.wait_ge(exps_done, m + 1)
                else:
                    pe.wait_ge(weights_ready, m - HEADS + 1)
                if m >= 1:
                    pe.wait_ge(pT_copied, m)
                sums = sum(place < (mla_at + diff_at)[m][1] for place in gate_end)
                if sums:
                    pe.wait_ge(gg_ready, sums)
                for k in range(3):
                    ins = tr(ps[:, 6, k * P:(k + 1) * P], probs[:, m % 2, 0, k * P:(k + 1) * P], ident[:, :])
                ins.then_inc(pT_made, 1)

            def values(m):
                pe.wait_ge(pT_copied, m + 1)
                if m >= 1:
                    pe.wait_ge(o_gated_ready, m)
                    pe.wait_ge(o_lo_ready, m)
                if m == HEADS:
                    pe.wait_ge(acc_read_act, by_act.index(acc_of["vd", 1]) + 1)
                h = m % HEADS
                v = ((lambda t: v_mla[:, t, h, :]) if m < HEADS else (lambda t: v_diff[:, t, h * P:(h + 1) * P]))
                mm(ps[:, 7, 0:P], lhsT=probsT[:, 0:P], rhs=v(0), start=True, stop=True)
                mm(ps[:, 7, P:2 * P], lhsT=probsT[:, P:2 * P], rhs=v(0), start=True, stop=False)
                mm(ps[:, 7, P:2 * P], lhsT=probsT[:, 2 * P:3 * P], rhs=v(1), start=False, stop=True).then_inc(pv_done, 1)

            def transpose_out(m):
                pe.wait_ge(o_gated_ready, m + 1)
                if m >= 1:
                    pe.wait_ge(o_lo_ready, m)
                for t in range(TOK):
                    ins = tr(ps[:, 7, SEQ + t * P:SEQ + (t + 1) * P], o_gated[:, t, :], ident[:, :])
                ins.then_inc(oT_made, 1)

            def transpose_merged(n):
                pe.wait_ge(acc_read_dve, dve_reads("wod", n))
                if n >= 1:
                    pe.wait_ge(m_lo_ready, n)
                for b in range(4):
                    for t in range(TOK):
                        ins = tr(ps[:, 4 + b // 2, b % 2 * SEQ + t * P:b % 2 * SEQ + (t + 1) * P],
                                 merged[:, t, n * CH + b * P:n * CH + (b + 1) * P], ident[:, :])
                ins.then_inc(mT_made, 1)

            def gate_sum(n):
                pe.wait_ge(gate_used, (n + 1) * (KT // 2))
                if n >= 1:
                    pe.wait_ge(gg_ready, n)
                pe.wait_ge(pT_copied, HEADS + sum(gate_end[n] > at[1] for at in diff_at))
                mm(ps[:, 6, :], lhsT=ones[:, :], rhs=ada_acc[:, 0, :], start=True, stop=False)
                mm(ps[:, 6, :], lhsT=ones[:, :], rhs=ada_acc[:, 1, :], start=False, stop=True).then_inc(gate_summed, 1)

            for g in range(N_GROUPS):
                pe_after[group_at[g][0]].append(lambda g=g: group(g))
            for h in range(HEADS):
                for m, place, scores in ((h, mla_at[h], mla_scores), (HEADS + h, diff_at[h], diff_scores_pe)):
                    pe_after[place[0]].append(lambda h=h, f=scores: f(h))
                    pe_after[place[1]].append(lambda m=m: transpose_probs(m))
                    pe_after[place[2]].append(lambda m=m: values(m))
                    pe_after[place[3]].append(lambda m=m: transpose_out(m))
            for n in range(4):
                pe_after[merge_at[n]].append(lambda n=n: transpose_merged(n))
                pe_after[gate_end[n]].append(lambda n=n: gate_sum(n))

            pe.wait_ge(consts, 2)
            pe.wait_ge(vec_in, 16 * 6)
            tr(ps[:, 7, 0:NVEC], vec_rows[0:NVEC, :], ident[0:NVEC, 0:NVEC]).then_inc(cols_T, 1)
            pe.wait_ge(xn_ready, TOK)
            for g in range(KT // 2):
                if g == 1:
                    pe.wait_ge(cols_ready, 1)
                if g >= 2:
                    pe.wait_ge(xT_copied, g - 1)
                for b in range(2):
                    for t in range(TOK):
                        k = 2 * g + b
                        ins = tr(ps[:, 6 + g % 2, b * SEQ + t * P:b * SEQ + (t + 1) * P],
                                 x_tok[:, t, k * P:(k + 1) * P], ident[:, :])
                ins.then_inc(xT_made, 1)
            ada_sum(0)
            for p, (a, kind, n, i, first, last) in enumerate(pieces):
                if p in sum_before:
                    ada_sum(sum_before[p])
                if kind == "q" and n == 0:
                    pe.wait_ge(h_lo_ready, i + 1)
                if kind == "early" and i == EARLY - 1:
                    pe.wait_ge(h_lo_ready, EARLY)
                if kind == "early" and first:
                    pe.wait_ge(mod_ready, EARLY + n)
                if kind == "ukv" and n == 0 and first:
                    pe.wait_ge(ckv_lo, 2)
                if kind == "wom" and n == 0 and first:
                    pe.wait_ge(o_lo_ready, HEADS)
                if kind == "wod" and n == 0 and first:
                    pe.wait_ge(o_lo_ready, 2 * HEADS)
                if kind == "wout" and n == 0:
                    pe.wait_ge(m_lo_ready, i // 2 + 1)
                if first and a is not None and a >= 3:
                    wait_acc_read(pe, {3: 0, 4: 1}.get(a, a - 2))
                pe.wait_ge(lo_done, p + 1)
                b0 = banks(a)
                wide = ROPE if kind == "kr" else CH
                tiles = KT if kind == "kr" else 2
                s_hi, s_lo = {"ukv": (ckvT_hi, ckvT_lo), "wom": (o_hi, o_lo), "wod": (o_hi, o_lo),
                              "wout": (m_hi, m_lo)}.get(kind, (h_hi, h_lo))
                for r in range(tiles):
                    k = 2 * i + r + (HEADS if kind == "wod" else 0)
                    hi = w_hi[:, p % RING, r * wide:(r + 1) * wide]
                    lo = w_lo[:, p % RING, r * wide:(r + 1) * wide]
                    for t in range(TOK):
                        o = ps[:, b0 + t, 0:wide]
                        q = slice(t * P, (t + 1) * P)
                        mm(o, lhsT=s_hi[:, k, q], rhs=hi, start=first and r == 0, stop=False)
                        mm(o, lhsT=s_hi[:, k, q], rhs=lo, start=False, stop=False)
                        ins = mm(o, lhsT=s_lo[:, k, q], rhs=hi, start=False, stop=last and r == tiles - 1)
                ins.then_inc(piece_used, 1)
                for work in pe_after[p]:
                    work()


_INS = ["x", "c", "positions", "w_ada", "b_ada", "g_pre", "w_in", "g_kv", "w_ukv",
        "lambda_q1", "lambda_k1", "lambda_q2", "lambda_k2", "g_subln",
        "w_o_mla", "w_o_diff", "w_out", "g_post"]


def kernel(**inputs):
    import numpy as _np
    import concourse.bacc as _bacc
    from concourse import mybir as _mybir
    from concourse.bass_utils import run_bass_kernel_spmd as _run

    nc = _bacc.Bacc("TRN2", target_bir_lowering=False, num_devices=1)
    arrays, args = {}, []
    for name in _INS:
        a = _np.ascontiguousarray(inputs[name])
        arrays[f"in_{name}"] = a
        args.append(nc.dram_tensor(f"in_{name}", a.shape, _mybir.dt.from_np(a.dtype), kind="ExternalInput").ap())
    shape = (1, 256, 2048)
    args.append(nc.dram_tensor("out", shape, _mybir.dt.float32, kind="ExternalOutput").ap())
    hybrid_block(nc, *args)
    r = _run(nc, [arrays], core_ids=[0])
    return r.results[0]["out"]
```

```python
from contextlib import ExitStack

import math

import concourse.bass as bass
from concourse import mybir

F32 = mybir.dt.float32
F32R = mybir.dt.float32r
BF16 = mybir.dt.bfloat16
I32 = mybir.dt.int32
ALU = mybir.AluOpType
ACT = mybir.ActivationFunctionType
AX_X = mybir.AxisListType.X

P = 128
D = 2048
SEQ = 256
TOK = SEQ // P
KT = D // P
CH = 512
HEADS = 8
NOPE = 128
ROPE = 64
HALF = ROPE // 2
QH = NOPE + ROPE
RANK = 512
DQK = 64
EPS = 1e-6
NEG_INF = -1e30
MLA_SCALE = (NOPE + ROPE) ** -0.5
DIFF_SCALE = DQK ** -0.5
LAMBDA_INIT = 0.8 - 0.6 * math.exp(-0.3 * 0)
SLOPES = [2.0 ** (-8.0 * (h + 1) / HEADS) for h in range(HEADS)]
ROPE_FREQ = [10000.0 ** (-i / HALF) for i in range(HALF)]

RING = 4
PIECE = 1024
KEYS = P + SEQ

C_Q, C_CKV, C_KR = 0, 1536, 2048
C_QD, C_KD, C_VD, C_GM, C_GD, C_MM, C_MD = 2112, 3136, 4160, 5184, 6208, 7232, 9280

V_SHIFT, V_SCALE, V_GPRE, V_C, V_GKV, V_GSUB = 0, 16, 32, 48, 64, 68
NVEC = 69

SQ_SCALE, SQ_CLAMP, SQ_LIMIT = 2.0 ** -40, 2.0 ** 25, 2.0 ** (128 - 80)

BIG_TURN = 2.0 * math.pi * 512
BIG_PARTS = (3216.0, 0.99072265625, 0.00015461970178876072)
TURN_PARTS = (6.283203125, -1.7814338207244873e-05, -3.4822063010864213e-09)
ROUND_MAGIC = 12582912.0


def make_jobs():
    jobs = [("kr", 0), ("vd", 0), ("vd", 1)]
    jobs += [("gate", i) for i in (1, 2, 3)]
    jobs += [("ukv", i) for i in range(4)]
    jobs += [("qd", 0), ("qd", 1), ("kd", 0), ("kd", 1)]
    for n in range(4):
        jobs += [("mm", n), ("wom", n)]
    for n in range(4):
        jobs += [("md", n), ("wod", n)]
    jobs += [("wout", n) for n in range(4)]
    return jobs


VISITS = [
    (1, ("vd", 0), (0, 1)), (1, ("vd", 1), (0, 1)),
    (2, ("gate", 3), (0, 1, 2)), (2, ("gate", 1), (0, 1, 2)),
    (3, ("gate", 2), (0, 1, 2, 3)), (3, ("ckv", 0), (0, 1, 2, 3)),
    (4, ("gate", 0), (0, 1, 2, 3, 4)), (4, ("vd", 0), (2, 3, 4)),
    (5, ("vd", 1), (2, 3, 4, 5)), (5, ("gate", 3), (3, 4, 5)),
    (6, ("gate", 1), (3, 4, 5, 6)), (6, ("gate", 2), (4, 5, 6)),
    (7, ("ckv", 0), (4, 5, 6, 7)), (7, ("gate", 0), (5, 6, 7)),
]
EARLY_PAIRS = {}
for _, job, pairs in VISITS:
    EARLY_PAIRS[job] = EARLY_PAIRS.get(job, 0) + len(pairs)
OUT_PARTS = [(t, part) for t in range(TOK) for part in (slice(0, D // 4), slice(D // 4, D // 2), slice(D // 2, D))]
LAST_GROUP = 3
PIECES_OF = {"kr": 1, "ukv": 2, "wom": 4, "wod": 4}


def hybrid_block(nc, x, c, positions, w_ada, b_ada, g_pre, w_in, g_kv, w_ukv,
                 lambda_q1, lambda_k1, lambda_q2, lambda_k2, g_subln,
                 w_o_mla, w_o_diff, w_out, g_post, out):
    pieces = []
    start, end = {}, {}
    visit_end = []
    first_part = []
    for j in range(KT // 2):
        first_part.append([])
        here = [v for v, visit in enumerate(VISITS) if visit[0] == j]
        for ch in range(3):
            if ch < len(here):
                pairs = VISITS[here[ch]][2]
                for i in pairs:
                    first_part[j].append(len(pieces))
                    pieces.append((None, "early", here[ch], i, i == pairs[0], i == pairs[-1]))
                visit_end.append(len(pieces) - 1)
            first_part[j].append(len(pieces))
            start.setdefault(ch, len(pieces))
            end[ch] = len(pieces)
            pieces.append((ch, "q", ch, j, j == 0, j == KT // 2 - 1))
    PH1 = len(pieces)
    acc_of = {("q", i): i for i in range(3)}
    for a, (kind, n) in enumerate(make_jobs(), start=3):
        done = EARLY_PAIRS.get((kind, n), 0)
        m = PIECES_OF.get(kind, KT // 2) - done
        start[a], end[a] = len(pieces), len(pieces) + m - 1
        acc_of[kind, n] = a
        for i in range(m):
            pieces.append((a, kind, n, i + done, i == 0, i == m - 1))
    NP = len(pieces)
    first_piece = lambda kind, n: start[acc_of[kind, n]]
    last_piece = lambda kind, n: end[acc_of[kind, n]]

    def banks(a):
        return 6 if a is None else 2 * a if a < 3 else 2 * ((a + 1) % 2)

    in_cols = {"q": C_Q, "ckv": C_CKV, "gate": C_GM, "vd": C_VD, "qd": C_QD, "kd": C_KD,
               "mm": C_MM, "md": C_MD}

    def piece_source(kind, n, i):
        if kind == "early":
            kind, n = VISITS[n][1]
        if kind == "kr":
            return w_in[0, :, C_KR:C_KR + ROPE].rearrange("(t p) n -> p t n", p=P)
        w, col = {"ukv": (w_ukv, n * CH), "wom": (w_o_mla, n * CH), "wod": (w_o_diff, n * CH),
                  "wout": (w_out, n * CH)}.get(kind) or (w_in, in_cols[kind] + n * CH)
        return w[0, 2 * i * P:2 * (i + 1) * P, col:col + CH].rearrange("(t p) n -> p t n", p=P)

    pe_after = {p: [] for p in range(-1, NP)}
    act_after = {p: [] for p in range(-1, NP)}
    dve_after = {p: [] for p in range(-1, NP)}

    with ExitStack() as ctx:
        KB = 1024
        at = [16512]

        def room(size):
            at[0] += size
            return at[0] - size

        def sb(name, shape, dt, offset=None):
            size = 4 if dt != BF16 else 2
            for s in shape[1:]:
                size *= s
            if offset is None:
                offset = room((size + 31) // 32 * 32)
            return nc.alloc_sbuf_tensor_at(name, shape, dt, offset=offset)

        w_raw = sb("w_raw", [P, RING, PIECE], F32)
        w_hi = sb("w_hi", [P, RING, PIECE], F32R)
        w_lo = sb("w_lo", [P, RING, PIECE], F32R)
        r_h_hi, r_h_lo, r_o_hi, r_o_lo = room(16 * KB), room(16 * KB), room(16 * KB), room(16 * KB)
        r_a, r_b, r_c = room(32 * KB), room(24 * KB), room(16 * KB)

        h_hi = sb("h_hi", [P, KT, SEQ], F32R, r_h_hi)
        h_lo = sb("h_lo", [P, KT, SEQ], F32R, r_h_lo)
        yg = sb("yg", [P, TOK, D], F32, r_h_hi)
        x_again = sb("x_again", [P, TOK, D], F32, r_h_lo)
        o_hi = sb("o_hi", [P, KT, SEQ], F32R, r_o_hi)
        o_lo = sb("o_lo", [P, KT, SEQ], F32R, r_o_lo)
        xnT = sb("xnT", [P, KT, SEQ], F32, r_o_hi)
        x_tok = sb("x_tok", [P, TOK, D], F32, r_o_lo)
        kr_tok = sb("kr_tok", [P, TOK, ROPE], F32, r_o_hi + 4 * KB)
        kr_dup = sb("kr_dup", [P, TOK, 2 * ROPE], F32, r_o_hi + 5 * KB)
        rot_a = sb("rot_a", [P, HEADS, HALF], F32, r_o_hi + 6 * KB)
        rot_b = sb("rot_b", [P, HEADS, HALF], F32, r_o_hi + 7 * KB)
        ckvT_hi = sb("ckvT_hi", [P, RANK // P, SEQ], F32R, r_o_hi + 8 * KB)
        ckvT_lo = sb("ckvT_lo", [P, RANK // P, SEQ], F32R, r_o_hi + 12 * KB)
        gate_part_sum = sb("gate_part_sum", [P, 4, TOK, CH], F32, r_o_lo)
        qnT = sb("qnT", [P, HEADS, SEQ], F32, r_a)
        qrT = sb("qrT", [P, HEADS // 2, SEQ], F32, r_a + 8 * KB)
        knT = sb("knT", [P, HEADS, SEQ], F32, r_a + 12 * KB)
        krT = sb("krT", [P, SEQ], F32, r_a + 20 * KB)
        v_mla = sb("v_mla", [P, TOK, HEADS, NOPE], F32, r_a + 21 * KB)
        merged = sb("merged", [P, TOK, D], F32, r_a)
        post_gain = sb("post_gain", [P, D], F32, r_a + 16 * KB)
        ckv_part = sb("ckv_part", [P, TOK, CH], F32, r_a + 24 * KB)
        x_diag = sb("x_diag", [P, TOK, P], F32, r_a + KB)
        kr_raw = sb("kr_raw", [P, SEQ], F32, r_a + 29 * KB)
        gate_ring = sb("gate_ring", [P, 2, PIECE], F32, r_a + 24 * KB)
        q_tok = sb("q_tok", [P, TOK, HEADS * QH], F32, r_b)
        qr_tok = sb("qr_tok", [P, TOK, HEADS, ROPE], F32, r_b + 12 * KB)
        lam_in = sb("lam_in", [P, 4, DQK], F32, r_b + 20 * KB)
        pos_row = sb("pos_row", [P, SEQ], I32, r_b + 21 * KB)
        angle = sb("angle", [P, 5, TOK * HALF], F32, r_b + 22 * KB)
        lam_prod = sb("lam_prod", [P, 2, DQK], F32, r_b + 23 * KB + 256)
        qdT = sb("qdT", [P, HEADS, SEQ], F32, r_b)
        kdT = sb("kdT", [P, HEADS, SEQ], F32, r_b + 8 * KB)
        v_diff = sb("v_diff", [P, TOK, HEADS * P], F32, r_b + 16 * KB)
        ada_ring = sb("ada_ring", [P, RING, 2, 2, 2 * P], F32, r_c)
        silu_gate = sb("silu_gate", [P, 2, TOK, D // 2], F32, r_c)
        bias_gain = sb("bias_gain", [P, 2, CH], F32, r_c + 4 * KB)
        m_hi = sb("m_hi", [P, KT, SEQ], F32R, r_b)
        m_lo = sb("m_lo", [P, KT, SEQ], F32R, r_b + 16 * KB)

        stage = sb("stage", [P, TOK, CH], F32)
        tmp = sb("tmp", [P, CH], F32)
        ada_acc = sb("ada_acc", [P, 2, CH], F32)
        r_p = room(2 * 2 * KEYS * 4 + KEYS * 4 + TOK * P * 4)
        probs = sb("probs", [P, 2, 2, KEYS], F32, r_p)
        probsT = sb("probsT", [P, KEYS], F32, r_p + 4 * KEYS * 4)
        o_gated = sb("o_gated", [P, TOK, P], F32, r_p + 5 * KEYS * 4)
        vd_part = sb("vd_part", [P, 2, TOK, CH], F32, r_p)
        dist = sb("dist", [P, KEYS], F32)
        vec_rows = sb("vec_rows", [P, P], F32, r_a)
        cols = sb("cols", [P, NVEC + 3], F32)
        ident = sb("ident", [P, P], F32)
        ident_b = sb("ident_b", [P, P], BF16)
        causal_b = sb("causal_b", [P, P], BF16)
        causal_far = sb("causal_far", [P, P], F32)
        ones = sb("ones", [P, P], F32)
        freq = sb("freq", [P, HALF], F32)
        cos = sb("cos", [P, TOK, HALF], F32)
        sin = sb("sin", [P, TOK, HALF], F32)
        pos_q = sb("pos_q", [P, TOK], I32)
        pos_qf = sb("pos_qf", [P, TOK], F32)
        mod_gain = sb("mod_gain", [P, KT], F32)
        mod_shift = sb("mod_shift", [P, KT], F32)
        gain_tmp = sb("gain_tmp", [P, 2], F32)
        NR = 3 + HEADS
        R_X, R_CKV, R_HEAD, R_Y = 0, 1, 2, 2 + HEADS
        sumsq = sb("sumsq", [P, NR, TOK], F32)
        variance = sb("variance", [P, NR, TOK], F32)
        rstd = sb("rstd", [P, NR, TOK], F32)
        power = sb("power", [P, TOK], F32)
        in_range = sb("in_range", [P, TOK], F32)
        y_sq = sb("y_sq", [P, TOK, 4], F32)
        maxes = sb("maxes", [P, 2, 4], F32)
        neg_max = sb("neg_max", [P, 2, 4], F32)
        sums = sb("sums", [P, 2, 4], F32)
        recip = sb("recip", [P, 2, 4], F32)
        lam_dot = sb("lam_dot", [P, 2], F32)
        lam_exp = sb("lam_exp", [P, 2], F32)
        lam = sb("lam", [P, 1], F32)
        assert at[0] <= 229368, at[0]

        ps = ctx.enter_context(nc.psum_tensor("ps", [P, 8, CH], F32))

        def sem(name):
            return ctx.enter_context(nc.semaphore(name))

        raw_in = [sem(f"raw_in{i}") for i in range(RING)]
        ada_in = [sem(f"ada_in{i}") for i in range(RING)]
        gate_in = [sem(f"gate_in{i}") for i in range(2)]
        hi_done, lo_done, piece_used = sem("hi_done"), sem("lo_done"), sem("piece_used")
        x_in = [sem(f"x_in{t}") for t in range(TOK)]
        vec_in, pos_in, lam_ld = sem("vec_in"), sem("pos_in"), sem("lam_ld")
        consts = sem("consts")
        cols_T, cols_ready = sem("cols_T"), sem("cols_ready")
        x_sq, rstd_ready, xn_ready = sem("x_sq"), sem("rstd_ready"), sem("xn_ready")
        var_ready = sem("var_ready")
        xT_made, xT_copied = sem("xT_made"), sem("xT_copied")
        ada_used, ada_acc_ready, ada_summed, mod_ready = (
            sem("ada_used"), sem("ada_acc_ready"), sem("ada_summed"), sem("mod_ready"))
        h_hi_ready, h_lo_ready = sem("h_hi_ready"), sem("h_lo_ready")
        acc_read_act, acc_read_dve = sem("acc_read_act"), sem("acc_read_dve")
        tr_made, tr_copied = sem("tr_made"), sem("tr_copied")
        angles_ready, cossin_ready = sem("angles_ready"), sem("cossin_ready")
        lam_dots, lam_exps = sem("lam_dots"), sem("lam_exps")
        ckv_sq, ckv_scaled, ckv_hi, ckv_lo = sem("ckv_sq"), sem("ckv_scaled"), sem("ckv_hi"), sem("ckv_lo")
        scores_ready, scores_read, max_ready, exps_done = (
            sem("scores_ready"), sem("scores_read"), sem("max_ready"), sem("exps_done"))
        weights_ready = sem("weights_ready")
        pT_made, pT_copied = sem("pT_made"), sem("pT_copied")
        pv_done, head_sq, o_gated_ready = sem("pv_done"), sem("head_sq"), sem("o_gated_ready")
        oT_made, o_hi_ready, o_lo_ready = sem("oT_made"), sem("o_hi_ready"), sem("o_lo_ready")
        sig_ready, merged_ready = sem("sig_ready"), sem("merged_ready")
        mT_made, m_hi_ready, m_lo_ready = sem("mT_made"), sem("m_hi_ready"), sem("m_lo_ready")
        gate_used, gate_acc_ready, gate_summed, gg_ready, bias_in = (
            sem("gate_used"), sem("gate_acc_ready"), sem("gate_summed"), sem("gg_ready"), sem("bias_in"))
        x_again_in, out_ready, out_done = (
            sem("x_again_in"), sem("out_ready"), sem("out_done"))
        y_made = sem("y_made")
        y_squared = [sem(f"y_squared{t}") for t in range(TOK)]
        yg_ready = sem("yg_ready")
        y_root = sem("y_root")
        y_sums, root_ready = sem("y_sums"), sem("root_ready")
        silu_ready = sem("silu_ready")
        early_read = sem("early_read")
        kr_turned, kr_ready = sem("kr_turned"), sem("kr_ready")
        ada_used_pool, gate_used_pool = sem("ada_used_pool"), sem("gate_used_pool")
        gate_joined = sem("gate_joined")
        ada_odd = sem("ada_odd")
        odd_products = sem("odd_products")
        dve_step, pool_step = sem("dve_step"), sem("pool_step")

        block = ctx.enter_context(nc.Block())

        by_dve = [a for a in range(3, 3 + len(make_jobs())) if pieces[start[a]][1] in ("vd", "gate", "wom", "wod")]
        by_act = [a for a in range(3 + len(make_jobs())) if a not in by_dve]

        def dve_reads(kind, n):
            return by_dve.index(acc_of[kind, n]) + 1

        def wait_acc_read(eng, a):
            if a in by_dve:
                eng.wait_ge(acc_read_dve, by_dve.index(a) + 1)
            elif pieces[start[a]][1] == "wout":
                eng.wait_ge(yg_ready, TOK * (pieces[start[a]][2] + 1))
            else:
                eng.wait_ge(acc_read_act, by_act.index(a) + 1)

        MLA0 = last_piece("ukv", 0) + 6
        DIFF0 = first_piece("mm", 0) + 4
        mla_at = [(MLA0 + 4 * h, MLA0 + 4 * h + 3, MLA0 + 4 * h + 5, MLA0 + 4 * h + 7) for h in range(HEADS)]
        diff_at = [(DIFF0 + 5 * h, DIFF0 + 5 * h + 6, DIFF0 + 5 * h + 8, DIFF0 + 5 * h + 11) for h in range(HEADS)]

        G_QN, G_CKV, G_QR, G_KR, G_KN, G_D = 0, 4, 6, 8, 9, 13
        N_GROUPS = G_D + 8

        def group_bank(g):
            return 4 + g % 4 if g < G_KN else 5

        POOL_FROM = 3
        pool_parts = lambda j: max(0, j + 1 - POOL_FROM) * (KT // 2)
        ada_before = {}
        for j in range(KT // 2 - 1):
            own = first_part[j]
            for q in range(KT // 2):
                ada_before.setdefault(own[1 + q * (len(own) - 1) // (KT // 2)], []).append((j + 1, q))
        mod_after = {first_part[j][0]: j for j in range(KT // 2)}
        h_after = {}
        for j in range(KT // 2):
            reads_h = min(k for k, p in enumerate(first_part[j])
                          if pieces[p][1] == "q" or pieces[p][3] == j)
            h_after[first_part[j][max(0, reads_h - 2)]] = j
        GATE0, GATE_STEP = first_piece("mm", 0) + 5, 3
        gate_parts_at = {GATE0 + GATE_STEP * k: (k,) for k in range(4 * (KT // 2))}
        gate_end = [GATE0 + GATE_STEP * (8 * n + 7) for n in range(4)]
        gate_sum_at = [gate_end[n] + (n > 0) for n in range(4)]

        @block.sync
        def _(sp):
            for t in range(TOK):
                sp.dma_start(x_tok[:, t, :], x[0, t * P:(t + 1) * P, :]).then_inc(x_in[t], 16)
            sp.dma_start(vec_rows[V_C:V_C + KT, :], c[0, :].rearrange("(r n) -> r n", n=P)).then_inc(vec_in, 16)
            for row, n, v in ((V_SHIFT, KT, b_ada[0, 0:D]), (V_SCALE, KT, b_ada[0, D:2 * D]),
                              (V_GPRE, KT, g_pre[0, :]), (V_GKV, RANK // P, g_kv[0, :]),
                              (V_GSUB, 1, g_subln[0, :])):
                sp.dma_start(vec_rows[row:row + n, :], v.rearrange("(r n) -> r n", n=P)).then_inc(vec_in, 16)

            def load_ada(j, q):
                n = j * (KT // 2) + q
                if n >= RING:
                    sp.wait_ge(ada_used, n - RING + 1)
                    if n - RING >= POOL_FROM * (KT // 2):
                        sp.wait_ge(ada_used_pool, n - RING + 1 - POOL_FROM * (KT // 2))
                for s in range(2):
                    col = s * D + j * 2 * P
                    sp.dma_start(ada_ring[:, n % RING, :, s, :],
                                 w_ada[0, 2 * q * P:2 * (q + 1) * P, col:col + 2 * P]
                                 .rearrange("(t p) n -> p t n", p=P)).then_inc(ada_in[n % RING], 16)

            def load_gate(n, i):
                k = n * (KT // 2) + i
                if k >= 2:
                    sp.wait_ge(gate_used, k - 1)
                    sp.wait_ge(gate_used_pool, k - 1)
                else:
                    sp.wait_ge(pv_done, HEADS)
                col = 2 * D + n * CH
                sp.dma_start(gate_ring[:, k % 2, :].rearrange("p (t n) -> p t n", t=2),
                             w_ada[0, 2 * i * P:2 * (i + 1) * P, col:col + CH]
                             .rearrange("(t p) n -> p t n", p=P)).then_inc(gate_in[k % 2], 16)

            def load_bias_gain(n):
                if n == 0:
                    sp.wait_ge(o_gated_ready, HEADS)
                else:
                    sp.wait_ge(gg_ready, n)
                sp.dma_start(bias_gain[:, 0, :], b_ada[0, 2 * D + n * CH:2 * D + (n + 1) * CH]
                             .partition_broadcast(P)).then_inc(bias_in, 16)
                sp.dma_start(bias_gain[:, 1, :], g_post[0, n * CH:(n + 1) * CH]
                             .partition_broadcast(P)).then_inc(bias_in, 16)

            for q in range(KT // 2):
                load_ada(0, q)
            for p, (a, kind, n, i, first, last) in enumerate(pieces):
                for j, q in ada_before.get(p, ()):
                    load_ada(j, q)
                if p >= RING:
                    sp.wait_ge(lo_done, p - RING + 1)
                dst = w_raw[:, p % RING, :]
                dst = dst.rearrange("p (t n) -> p t n", n=ROPE if kind == "kr" else CH)
                sp.dma_start(dst, piece_source(kind, n, i)).then_inc(raw_in[p % RING], 16)
                if p == 0:
                    sp.dma_start(pos_row[:, :], positions[0, :].partition_broadcast(P)).then_inc(pos_in, 16)
                    with nc.allow_non_contiguous_dma(reason="256 positions, once"):
                        sp.dma_start(pos_q[:, :], positions[0, :].rearrange("(t p) -> p t", p=P)).then_inc(pos_in, 16)
                    for k, v in enumerate((lambda_q1, lambda_k1, lambda_q2, lambda_k2)):
                        sp.dma_start(lam_in[:, k, :], v[0, :].partition_broadcast(P)).then_inc(lam_ld, 16)
                for k in gate_parts_at.get(p + 1, ()):
                    load_gate(k // (KT // 2), k % (KT // 2))
                    if k % (KT // 2) == 4:
                        load_bias_gain(k // (KT // 2))
                if kind == "wout" and n == 0 and i == 0:
                    sp.wait_ge(piece_used, last_piece("md", 3) + 1)
                    for t in range(TOK):
                        sp.dma_start(x_again[:, t, :], x[0, t * P:(t + 1) * P, :]).then_inc(x_again_in, 16)
            for k, (t, part) in enumerate(OUT_PARTS):
                sp.wait_ge(out_ready, k + 1)
                sp.dma_start(out[0, t * P:(t + 1) * P, part], yg[:, t, part]).then_inc(out_done, 16)
            sp.wait_ge(out_done, 16 * len(OUT_PARTS))

        @block.gpsimd
        def _(pool):
            nc.gpsimd.memset(ident[:, :], 0.0).then_inc(pool_step, 1)
            pool.wait_ge(pool_step, 1)
            nc.gpsimd.affine_select(out=ident[:, :], in_=ident[:, :], compare_op=ALU.not_equal, fill=1.0,
                                    base=0, pattern=[[-1, P]], channel_multiplier=1).then_inc(consts, 1)
            nc.gpsimd.memset(power[:, :], -0.5).then_inc(pool_step, 1)
            nc.gpsimd.memset(ones[:, :], 1.0).then_inc(consts, 1)
            nc.gpsimd.memset(ident_b[:, :], 0.0).then_inc(pool_step, 1)
            nc.gpsimd.memset(causal_b[:, :], 0.0).then_inc(pool_step, 1)
            nc.gpsimd.memset(causal_far[:, :], 0.0).then_inc(pool_step, 1)
            for i, f in enumerate(ROPE_FREQ):
                fill = nc.gpsimd.memset(freq[:, i:i + 1], f)
            fill.then_inc(consts, 1)

            def inverse_root(k, need, count, width):
                pool.wait_ge(need, count)
                nc.gpsimd.tensor_scalar(variance[:, k, :], sumsq[:, k, :], 1.0 / width, EPS,
                                        ALU.mult, ALU.add).then_inc(var_ready, 1)
                pool.wait_ge(var_ready, k + 1)
                nc.gpsimd.tensor_tensor(rstd[:, k, :], variance[:, k, :], power[:, :], ALU.pow).then_inc(rstd_ready, 1)

            pool.wait_ge(pool_step, 2)
            inverse_root(R_X, x_sq, TOK, D)
            pool.wait_ge(pool_step, 5)
            nc.gpsimd.affine_select(out=ident_b[:, :], in_=ident_b[:, :], compare_op=ALU.not_equal, fill=1.0,
                                    base=0, pattern=[[-1, P]], channel_multiplier=1).then_inc(consts, 1)
            nc.gpsimd.affine_select(out=causal_b[:, :], in_=causal_b[:, :], compare_op=ALU.is_ge,
                                    fill=NEG_INF / MLA_SCALE, base=0, pattern=[[-1, P]],
                                    channel_multiplier=1).then_inc(consts, 1)
            nc.gpsimd.affine_select(out=causal_far[:, :], in_=causal_far[:, :], compare_op=ALU.is_ge,
                                    fill=-NEG_INF / min(SLOPES), base=0, pattern=[[-1, P]],
                                    channel_multiplier=1).then_inc(consts, 1)

            products = [0]

            def add_odd_rows(ring, cc, fresh, used, count):
                if fresh:
                    nc.gpsimd.tensor_scalar(ada_acc[:, 1, :], ring, cc, None, ALU.mult).then_inc(used, 1)
                else:
                    products[0] += 1
                    nc.gpsimd.tensor_scalar(ring, ring, cc, None, ALU.mult).then_inc(odd_products, 1)
                    pool.wait_ge(odd_products, products[0])
                    pool.wait_ge(used, count - 1)
                    nc.gpsimd.tensor_tensor(ada_acc[:, 1, :], ada_acc[:, 1, :], ring, ALU.add).then_inc(used, 1)

            pool.wait_ge(cols_ready, 1)
            for n in range(POOL_FROM * (KT // 2), (KT // 2) ** 2):
                j, q = n // (KT // 2), n % (KT // 2)
                if q == 0 and j >= 1:
                    pool.wait_ge(ada_summed, j)
                pool.wait_ge(ada_in[n % RING], 32 * (n // RING + 1))
                add_odd_rows(ada_ring[:, n % RING, 1, :, :].rearrange("p s n -> p (s n)"),
                             cols[:, V_C + 2 * q + 1:V_C + 2 * q + 2], q == 0, ada_used_pool, n + 1 - POOL_FROM * (KT // 2))
            inverse_root(R_CKV, ckv_sq, 1, RANK)

            def head_root(h):
                k = R_HEAD + h
                pool.wait_ge(head_sq, h + 1)
                nc.gpsimd.tensor_scalar(in_range[:, :], sumsq[:, k, :], SQ_LIMIT, SQ_SCALE, ALU.is_lt, ALU.mult)
                nc.gpsimd.tensor_scalar(variance[:, k, :], sumsq[:, k, :], 1.0 / P, EPS * SQ_SCALE ** 2,
                                        ALU.mult, ALU.add).then_inc(var_ready, 1)
                pool.wait_ge(var_ready, k + 1)
                nc.gpsimd.tensor_tensor(variance[:, k, :], variance[:, k, :], power[:, :], ALU.pow).then_inc(root_ready, 1)
                pool.wait_ge(root_ready, h + 1)
                nc.gpsimd.tensor_tensor(rstd[:, k, :], variance[:, k, :], in_range[:, :], ALU.mult).then_inc(rstd_ready, 1)
                pool.wait_ge(rstd_ready, k + 1)

            def odd_gate_rows(k):
                n, i = k // (KT // 2), k % (KT // 2)
                pool.wait_ge(gate_in[k % 2], 16 * (k // 2 + 1))
                if i == 0 and n >= 1:
                    pool.wait_ge(gate_summed, n)
                add_odd_rows(gate_ring[:, k % 2, CH:2 * CH], cols[:, V_C + 2 * i + 1:V_C + 2 * i + 2],
                             i == 0, gate_used_pool, k + 1)

            work = [(place, 0, lambda k=parts[0]: odd_gate_rows(k)) for place, parts in gate_parts_at.items()]
            work += [(diff_at[h][2] + 4, 1, lambda h=h: head_root(h)) for h in range(HEADS)]
            for place, _, run in sorted(work, key=lambda w: w[:2]):
                run()
            for t in range(TOK):
                pool.wait_ge(y_sums, t + 1)
                nc.gpsimd.tensor_scalar(variance[:, R_Y, t:t + 1], sumsq[:, R_Y, t:t + 1], 1.0 / D, EPS,
                                        ALU.mult, ALU.add).then_inc(var_ready, 1)
                pool.wait_ge(var_ready, R_Y + t + 1)
                nc.gpsimd.tensor_tensor(rstd[:, R_Y, t:t + 1], variance[:, R_Y, t:t + 1], power[:, 0:1],
                                        ALU.pow).then_inc(y_root, 1)

        act = nc.scalar

        def act_copy_group(g, dst):
            def run(eng):
                eng.wait_ge(tr_made, g + 1)
                act.copy(dst, ps[:, group_bank(g), 0:dst_size(dst)]).then_inc(tr_copied, 1)
            return run

        def dst_size(ap):
            n = 1
            for s in ap.shape[1:]:
                n *= s
            return n

        def act_read(a, body):
            def run(eng):
                eng.wait_ge(piece_used, end[a] + 1)
                body(eng, banks(a)).then_inc(acc_read_act, 1)
            return run

        def read_q(n):
            def body(eng, b):
                for t in range(TOK):
                    ins = act.copy(q_tok[:, t, n * CH:(n + 1) * CH], ps[:, b + t, :])
                return ins
            return body

        def square_ckv(eng):
            eng.wait_ge(early_read, CKV_DONE)
            eng.wait_ge(h_hi_ready, KT // 2)
            for t in range(TOK):
                ins = act.activation(act_junk[:, t, :], stage[:, t, :], ACT.Square, accum_out=sumsq[:, R_CKV, t:t + 1])
            ins.then_inc(ckv_sq, 1)

        def read_kr(eng, b):
            return act.copy(kr_raw[0:ROPE, :], ps[0:ROPE, b, 0:SEQ])

        def copy_kr(eng):
            eng.wait_ge(kr_turned, 1)
            act.copy(kr_tok[:, :, :], ps[:, 7, 0:TOK * ROPE].rearrange("p (t n) -> p t n", t=TOK)).then_inc(kr_ready, 1)

        def act_silu(n):
            def run(eng):
                if n == 0:
                    eng.wait_ge(early_read, len(VISITS))
                    eng.wait_ge(ada_used, (KT // 2) ** 2)
                    eng.wait_ge(ada_used_pool, pool_parts(KT // 2 - 1))
                else:
                    eng.wait_ge(acc_read_dve, dve_reads("gate", n))
                act.activation(silu_gate[:, n // 2, :, n % 2 * CH:(n % 2 + 1) * CH], gate_part_sum[:, n, :, :],
                               ACT.Silu).then_inc(silu_ready, 1)
            return run

        def part_sum(job):
            kind, n = job
            return {"gate": gate_part_sum[:, n, :, :], "vd": vd_part[:, n % 2, :, :], "ckv": ckv_part[:, :, :]}[kind]

        def act_early(v):
            def run(eng):
                eng.wait_ge(piece_used, visit_end[v] + 1)
                act.copy(part_sum(VISITS[v][1]), ps[:, 6:8, :]).then_inc(early_read, 1)
            return run

        def read_ukv(n):
            def body(eng, b):
                if n >= 2:
                    eng.wait_ge(tr_made, G_KN + n - 1)
                else:
                    eng.wait_ge(tr_made, G_CKV + 2)
                for t in range(TOK):
                    both = ps[:, b + t, :].rearrange("p (h w d) -> p h w d", h=2, w=2)
                    act.copy(stage[:, t, (n % 2) * 256:(n % 2) * 256 + 256].rearrange("p (h d) -> p h d", h=2),
                             both[:, :, 0, :])
                    ins = act.copy(v_mla[:, t, 2 * n:2 * n + 2, :], both[:, :, 1, :])
                return ins
            return body

        def read_qk(k):
            def body(eng, b):
                eng.wait_ge(tr_made, G_D + 2 * k)
                for t in range(TOK):
                    ins = act.copy(stage[:, t, :], ps[:, b + t, :])
                return ins
            return body

        def read_sigmoid(k):
            def body(eng, b):
                if k == 0:
                    eng.wait_ge(tr_made, N_GROUPS)
                else:
                    eng.wait_ge(acc_read_dve, dve_reads("wom", k - 1) if k <= 4 else dve_reads("wod", k - 5))
                for t in range(TOK):
                    ins = act.activation(stage[:, t, :], ps[:, b + t, :], ACT.Sigmoid)
                return ins
            return body

        def act_ckv_hi(eng):
            for g in range(2):
                eng.wait_ge(tr_made, G_CKV + g + 1)
                for b in range(2):
                    k = 2 * g + b
                    ins = act.activation(ckvT_hi[:, k, :], ps[:, 4 + (G_CKV + g) % 4, b * SEQ:(b + 1) * SEQ],
                                         ACT.Copy, scale=cols[:, V_GKV + k:V_GKV + k + 1])
                ins.then_inc(ckv_hi, 1)
            eng.wait_ge(ckv_lo, 2)
            act.copy(ckv_signal[:, 0:1], cols[:, 0:1]).then_inc(tr_copied, 2)

        ckv_signal = sb("ckv_signal", [P, 1], F32)

        def act_exps(m):
            def run(eng):
                eng.wait_ge(max_ready, m + 1)
                if m < HEADS:
                    if m >= 2:
                        eng.wait_ge(pT_made, m - 1)
                    for b, (lo, hi) in enumerate(((0, P), (P, KEYS))):
                        ins = act.activation(probs[:, m % 2, 0, lo:hi], ps[:, 4, lo:hi], ACT.Exp,
                                             bias=neg_max[:, m % 2, b:b + 1], scale=MLA_SCALE,
                                             accum_out=sums[:, m % 2, b:b + 1])
                else:
                    for b, (lo, hi) in enumerate(((0, P), (P, KEYS))):
                        for w in range(2):
                            s = 2 * b + w
                            ins = act.activation(probs[:, m % 2, w, lo:hi], probs[:, m % 2, w, lo:hi], ACT.Exp,
                                                 bias=neg_max[:, m % 2, s:s + 1], scale=DIFF_SCALE,
                                                 accum_out=sums[:, m % 2, s:s + 1])
                ins.then_inc(exps_done, 1)
            return run

        def act_copy_probs(m):
            def run(eng):
                eng.wait_ge(pT_made, m + 1)
                if m >= 1:
                    eng.wait_ge(pv_done, m)
                act.copy(probsT[:, :], ps[:, 6, 0:KEYS]).then_inc(pT_copied, 1)
            return run

        def act_o_hi(m):
            def run(eng):
                eng.wait_ge(oT_made, m + 1)
                scale = 1.0 if m < HEADS else cols[:, NVEC:NVEC + 1]
                act.activation(o_hi[:, m, :], ps[:, 7, SEQ:2 * SEQ], ACT.Copy, scale=scale).then_inc(o_hi_ready, 1)
            return run

        def act_m_hi(n):
            def run(eng):
                eng.wait_ge(mT_made, n + 1)
                act.copy(m_hi[:, 4 * n:4 * n + 4, :], ps[:, 4:6, :]).then_inc(m_hi_ready, 1)
            return run

        def read_y(n):
            def body(eng):
                b = banks(acc_of["wout", n])
                for t in range(TOK):
                    if t == 0:
                        eng.wait_ge(y_made, n + 1)
                    else:
                        eng.wait_ge(piece_used, end[acc_of["wout", n]] + 1)
                    eng.wait_ge(y_squared[t], n)
                    act.activation(act_junk[:, t, :], ps[:, b + t, :], ACT.Square,
                                   accum_out=y_sq[:, t, n:n + 1]).then_inc(y_squared[t], 1)
            return body

        act_junk = sb("act_junk", [P, TOK, CH], F32, r_o_hi)

        for n in range(3):
            act_after[PH1 + n].append(act_read(n, read_q(n)))
        act_after[PH1 + 2].append(act_read(acc_of["kr", 0], read_kr))
        act_after[PH1 + 5].append(copy_kr)
        CKV_DONE = max(v for v, visit in enumerate(VISITS) if visit[1] == ("ckv", 0)) + 1
        act_after[visit_end[CKV_DONE - 1] + 4].append(square_ckv)
        seen = set()
        for v, visit in enumerate(VISITS):
            if visit[1] not in seen:
                seen.add(visit[1])
                act_after[visit_end[v] + 2].append(act_early(v))
        act_after[PH1 + 3].append(act_silu(0))
        for n in (1, 2, 3):
            act_after[last_piece("gate", n) + 4].append(act_silu(n))
        for n in range(4):
            act_after[last_piece("ukv", n) + 3].append(act_read(acc_of["ukv", n], read_ukv(n)))
        for k, (kind, n) in enumerate((("qd", 0), ("qd", 1), ("kd", 0), ("kd", 1))):
            act_after[last_piece(kind, n) + 3].append(act_read(acc_of[kind, n], read_qk(k)))
        for n in range(4):
            act_after[last_piece("mm", n) + 3].append(act_read(acc_of["mm", n], read_sigmoid(n)))
            act_after[last_piece("md", n) + 3].append(act_read(acc_of["md", n], read_sigmoid(4 + n)))
            act_after[min(last_piece("wout", n) + 3, NP - 1)].append(read_y(n))

        q_end = PH1
        group_at = {}
        for g in range(4):
            group_at[G_QN + g] = (q_end + 4 + g // 2, q_end + 8 + g // 2)
        for g in range(2):
            group_at[G_CKV + g] = (q_end + 6, q_end + 9)
            group_at[G_QR + g] = (q_end + 9, q_end + 13)
        group_at[G_KR] = (q_end + 11, q_end + 14)
        for n in range(4):
            group_at[G_KN + n] = (last_piece("ukv", n) + 2, last_piece("ukv", n) + 6)
        for k, (kind, n) in enumerate((("qd", 0), ("qd", 1), ("kd", 0), ("kd", 1))):
            for g in range(2):
                group_at[G_D + 2 * k + g] = (last_piece(kind, n) + 2 + 2 * g, last_piece(kind, n) + 5 + 2 * g)
        for g in range(N_GROUPS):
            at_pe, at_act = group_at[g]
            if g < G_CKV:
                dst = qnT[:, 2 * g:2 * g + 2, :]
            elif G_QR <= g < G_KR:
                dst = qrT[:, 2 * (g - G_QR):2 * (g - G_QR) + 2, :]
            elif g < G_QR:
                if g == G_CKV:
                    act_after[at_act].append(act_ckv_hi)
                continue
            elif g == G_KR:
                dst = krT[:, :]
            elif g < G_D:
                dst = knT[:, 2 * (g - G_KN):2 * (g - G_KN) + 2, :]
            else:
                k = g - G_D
                dst = (qdT if k < 4 else kdT)[:, 2 * (k % 4):2 * (k % 4) + 2, :]
            act_after[at_act].append(act_copy_group(g, dst))
        for h in range(HEADS):
            s, t, v, g = mla_at[h]
            act_after[s + 5].append(act_exps(h))
            act_after[t + 4].append(act_copy_probs(h))
            act_after[g + 4].append(act_o_hi(h))
            s, t, v, g = diff_at[h]
            act_after[s + 6].append(act_exps(HEADS + h))
            act_after[t + 4].append(act_copy_probs(HEADS + h))
            act_after[g + 4].append(act_o_hi(HEADS + h))
        merge_at = [last_piece("wod", n) + 5 for n in range(4)]
        for n in range(4):
            act_after[merge_at[n] + 4].append(act_m_hi(n))

        @block.scalar
        def _(eng):
            eng.wait_ge(x_in[0], 16)
            act.activation(xnT[:, 0:KT // 2, :].rearrange("p k s -> p (k s)"), x_tok[:, 0, :], ACT.Square,
                           accum_out=sumsq[:, R_X, 0:1]).then_inc(x_sq, 1)
            eng.wait_ge(x_sq, TOK)
            eng.wait_ge(cols_T, 1)
            act.copy(cols[:, 0:NVEC], ps[:, 7, 0:NVEC]).then_inc(cols_ready, 1)
            for g in range(KT // 2):
                eng.wait_ge(xT_made, g + 1)
                act.copy(xnT[:, 2 * g:2 * g + 2, :], ps[:, 6 + g % 2, :]).then_inc(xT_copied, 1)

            def make_h_hi(j):
                eng.wait_ge(mod_ready, j + 1)
                for b in range(2):
                    k = 2 * j + b
                    ins = act.activation(h_hi[:, k, :], xnT[:, k, :], ACT.Identity,
                                         bias=mod_shift[:, k:k + 1], scale=mod_gain[:, k:k + 1])
                ins.then_inc(h_hi_ready, 1)

            eng.wait_ge(xT_copied, KT // 2)
            for p, (a, kind, n, i, first, last) in enumerate(pieces):
                eng.wait_ge(raw_in[p % RING], 16 * (p // RING + 1))
                if p >= RING:
                    eng.wait_ge(piece_used, p - RING + 1)
                act.copy(w_hi[:, p % RING, :], w_raw[:, p % RING, :]).then_inc(hi_done, 1)
                if p == first_part[3][5]:
                    eng.wait_ge(angles_ready, 1)
                    act.activation(sin[:, :, :].rearrange("p t i -> p (t i)"), angle[:, 3, :], ACT.Sin)
                    act.activation(cos[:, :, :].rearrange("p t i -> p (t i)"), angle[:, 4, :], ACT.Sin).then_inc(cossin_ready, 1)
                    eng.wait_ge(lam_dots, 1)
                    act.activation(lam_exp[:, :], lam_dot[:, :], ACT.Exp).then_inc(lam_exps, 1)
                for work in act_after[p]:
                    work(eng)
                if p in h_after:
                    make_h_hi(h_after[p])

        dve = nc.vector
        steps = [0]

        def link(eng, ins):
            steps[0] += 1
            ins.then_inc(dve_step, 1)
            eng.wait_ge(dve_step, steps[0])

        def dve_rope(t, src, dst, heads):
            def run(eng):
                c_ = cos[:, t:t + 1, :].to_broadcast([P, heads, HALF])
                s_ = sin[:, t:t + 1, :].to_broadcast([P, heads, HALF])
                a, b = rot_a[:, 0:heads, :], rot_b[:, 0:heads, :]
                x1, x2 = src[:, :, 0:HALF], src[:, :, HALF:ROPE]
                dve.tensor_tensor(a, x1, c_, ALU.mult)
                link(eng, dve.tensor_tensor(b, x2, s_, ALU.mult))
                link(eng, dve.tensor_tensor(dst[:, :, 0:HALF], a, b, ALU.subtract))
                dve.tensor_tensor(a, x2, c_, ALU.mult)
                link(eng, dve.tensor_tensor(b, x1, s_, ALU.mult))
                link(eng, dve.tensor_tensor(dst[:, :, HALF:ROPE], a, b, ALU.add))
            return run

        def q_rope(t):
            def run(eng):
                if t == 0:
                    eng.wait_ge(acc_read_act, 3)
                    eng.wait_ge(cossin_ready, 1)
                src = q_tok[:, t, :].rearrange("p (h d) -> p h d", d=QH)[:, :, NOPE:QH]
                dve_rope(t, src, qr_tok[:, t, :, :], HEADS)(eng)
            return run

        def kr_rope(eng):
            eng.wait_ge(kr_ready, 1)
            a, b = rot_a[:, 0:TOK, :], rot_b[:, 0:TOK, :]
            x1, x2 = kr_tok[:, :, 0:HALF], kr_tok[:, :, HALF:ROPE]
            twice = kr_dup[:, :, :].rearrange("p t (c n) -> p t c n", c=2)
            wide = lambda ap: ap.unsqueeze(2).to_broadcast([P, TOK, 2, HALF])
            dve.tensor_tensor(a, x1, cos[:, :, :], ALU.mult)
            link(eng, dve.tensor_tensor(b, x2, sin[:, :, :], ALU.mult))
            link(eng, dve.tensor_tensor(twice[:, :, :, 0:HALF], wide(a), wide(b), ALU.subtract))
            dve.tensor_tensor(a, x2, cos[:, :, :], ALU.mult)
            link(eng, dve.tensor_tensor(b, x1, sin[:, :, :], ALU.mult))
            link(eng, dve.tensor_tensor(twice[:, :, :, HALF:ROPE], wide(a), wide(b), ALU.add))

        def scale_ckv(eng):
            eng.wait_ge(rstd_ready, R_CKV + 1)
            for t in range(TOK):
                ins = dve.tensor_scalar(stage[:, t, :], stage[:, t, :], rstd[:, R_CKV, t:t + 1], None, ALU.mult)
            ins.then_inc(ckv_scaled, 1)

        def dve_ckv_lo(eng):
            for g in range(2):
                eng.wait_ge(ckv_hi, g + 1)
                for b in range(2):
                    k = 2 * g + b
                    link(eng, dve.tensor_scalar(tmp[:, b * SEQ:(b + 1) * SEQ],
                                                ps[:, 4 + (G_CKV + g) % 4, b * SEQ:(b + 1) * SEQ],
                                                cols[:, V_GKV + k:V_GKV + k + 1], None, ALU.mult))
                link(eng, dve.tensor_tensor(ckvT_lo[:, 2 * g:2 * g + 2, :].rearrange("p k s -> p (k s)"), tmp[:, :],
                                            ckvT_hi[:, 2 * g:2 * g + 2, :].rearrange("p k s -> p (k s)").bitcast(F32),
                                            ALU.subtract))
            dve.memset(gain_tmp[:, 0:1], 0.0).then_inc(ckv_lo, 2)

        def mla_max(h):
            def run(eng):
                eng.wait_ge(scores_ready, h + 1)
                dve.reduce_max(maxes[:, h % 2, 0:1], ps[:, 4, 0:P], AX_X)
                link(eng, dve.reduce_max(maxes[:, h % 2, 1:2], ps[:, 4, P:KEYS], AX_X))
                if h >= 2:
                    eng.wait_ge(exps_done, h - 1)
                dve.tensor_scalar(neg_max[:, h % 2, 0:2], maxes[:, h % 2, 0:2], -MLA_SCALE, None,
                                  ALU.mult).then_inc(max_ready, 1)
            return run

        def add_early(v):
            def run(eng):
                job = VISITS[v][1]
                before = max(w for w in range(v) if VISITS[w][1] == job)
                eng.wait_ge(piece_used, visit_end[v] + 1)
                eng.wait_ge(early_read, before + 1)
                if job[0] == "ckv":
                    eng.wait_ge(h_lo_ready, KT // 2)
                dst = stage[:, :, :] if job[0] == "ckv" else part_sum(job)
                dve.tensor_tensor(dst, part_sum(job), ps[:, 6:8, :], ALU.add).then_inc(early_read, 1)
            return run

        def add_late(job):
            def run(eng):
                a = acc_of[job]
                eng.wait_ge(piece_used, end[a] + 1)
                eng.wait_ge(early_read, len(VISITS))
                part = part_sum(job)
                dst = part if job[0] == "gate" else v_diff[:, :, job[1] * CH:(job[1] + 1) * CH]
                dve.tensor_tensor(dst, part, ps[:, banks(a):banks(a) + TOK, :], ALU.add).then_inc(acc_read_dve, 1)
            return run

        def mla_out(h):
            def run(eng):
                eng.wait_ge(pv_done, h + 1)
                link(eng, dve.reciprocal(recip[:, h % 2, 0:2], sums[:, h % 2, 0:2]))
                if h == 0:
                    eng.wait_ge(silu_ready, 4)
                if h >= 1:
                    eng.wait_ge(oT_made, h)
                for t in range(TOK):
                    ins = dve.scalar_tensor_tensor(
                        out=o_gated[:, t, :], in0=ps[:, 7, t * P:(t + 1) * P], scalar=recip[:, h % 2, t:t + 1],
                        in1=silu_gate[:, 0, t, h * P:(h + 1) * P], op0=ALU.mult, op1=ALU.mult)
                ins.then_inc(o_gated_ready, 1)
            return run

        def dve_o_lo(m):
            def run(eng):
                src = ps[:, 7, SEQ:2 * SEQ]
                eng.wait_ge(o_hi_ready, m + 1)
                if m >= HEADS:
                    link(eng, dve.tensor_scalar(tmp[:, 0:SEQ], src, cols[:, NVEC:NVEC + 1], None, ALU.mult))
                    src = tmp[:, 0:SEQ]
                link(eng, dve.tensor_tensor(o_lo[:, m, :], src, o_hi[:, m, :].bitcast(F32), ALU.subtract))
                dve.memset(gain_tmp[:, 0:1], 0.0).then_inc(o_lo_ready, 1)
            return run

        def diff_scores(h):
            m = HEADS + h
            def run(eng):
                if m % 2 == h % 2 and m >= 2:
                    eng.wait_ge(pT_made, m - 1)
                eng.wait_ge(scores_ready, m + 1)
                dst = probs[:, m % 2, :, :]
                link(eng, dve.scalar_tensor_tensor(
                    out=dst, in0=dist[:, :].unsqueeze(1).to_broadcast([P, 2, KEYS]),
                    scalar=-SLOPES[h] / DIFF_SCALE, in1=ps[:, 4:6, 0:KEYS], op0=ALU.mult, op1=ALU.add))
                dve.tensor_reduce(maxes[:, m % 2, 0:2], dst[:, :, 0:P], AX_X, ALU.max).then_inc(scores_read, 1)
                link(eng, dve.tensor_reduce(maxes[:, m % 2, 2:4], dst[:, :, P:KEYS], AX_X, ALU.max))
                dve.tensor_scalar(neg_max[:, m % 2, :], maxes[:, m % 2, :], -DIFF_SCALE, None,
                                  ALU.mult).then_inc(max_ready, 1)
            return run

        def diff_weights(h):
            m = HEADS + h
            def run(eng):
                eng.wait_ge(exps_done, m + 1)
                link(eng, dve.reciprocal(recip[:, m % 2, :], sums[:, m % 2, :]))
                second = recip[:, m % 2, :].rearrange("p (b w) -> p b w", w=2)[:, :, 1]
                link(eng, dve.tensor_scalar(second, second, lam[:, 0:1], None, ALU.mult))
                spans = ((0, P), (P, KEYS))
                for b, (lo, hi) in enumerate(spans):
                    ins = dve.tensor_scalar(probs[:, m % 2, 1, lo:hi], probs[:, m % 2, 1, lo:hi],
                                            recip[:, m % 2, 2 * b + 1:2 * b + 2], None, ALU.mult)
                link(eng, ins)
                for b, (lo, hi) in enumerate(spans):
                    ins = dve.scalar_tensor_tensor(
                        out=probs[:, m % 2, 0, lo:hi], in0=probs[:, m % 2, 0, lo:hi],
                        scalar=recip[:, m % 2, 2 * b:2 * b + 1], in1=probs[:, m % 2, 1, lo:hi],
                        op0=ALU.mult, op1=ALU.subtract)
                ins.then_inc(weights_ready, 1)
            return run

        def head_squares(h):
            def run(eng):
                eng.wait_ge(pv_done, HEADS + h + 1)
                link(eng, dve.tensor_scalar(tmp[:, 0:SEQ], ps[:, 7, 0:SEQ], SQ_SCALE, SQ_CLAMP, ALU.mult, ALU.min))
                for t in range(TOK):
                    part = tmp[:, t * P:(t + 1) * P]
                    ins = dve.scalar_tensor_tensor(out=tmp[:, SEQ + t * P:SEQ + (t + 1) * P], in0=part, scalar=-SQ_CLAMP,
                                                   in1=part, op0=ALU.max, op1=ALU.mult,
                                                   accum_out=sumsq[:, R_HEAD + h, t:t + 1])
                ins.then_inc(head_sq, 1)
            return run

        def diff_out(h):
            def run(eng):
                eng.wait_ge(rstd_ready, R_HEAD + h + 1)
                eng.wait_ge(oT_made, HEADS + h)
                for t in range(TOK):
                    ins = dve.scalar_tensor_tensor(
                        out=o_gated[:, t, :], in0=ps[:, 7, t * P:(t + 1) * P], scalar=rstd[:, R_HEAD + h, t:t + 1],
                        in1=silu_gate[:, 1, t, h * P:(h + 1) * P], op0=ALU.mult, op1=ALU.mult)
                ins.then_inc(o_gated_ready, 1)
            return run

        def merge_mla(n):
            def run(eng):
                a = acc_of["wom", n]
                eng.wait_ge(piece_used, end[a] + 1)
                eng.wait_ge(acc_read_act, by_act.index(acc_of["mm", n]) + 1)
                for t in range(TOK):
                    ins = dve.tensor_tensor(merged[:, t, n * CH:(n + 1) * CH], ps[:, banks(a) + t, :],
                                            stage[:, t, :], ALU.mult)
                ins.then_inc(acc_read_dve, 1)
            return run

        def merge_diff(n):
            def run(eng):
                a = acc_of["wod", n]
                eng.wait_ge(piece_used, end[a] + 1)
                eng.wait_ge(acc_read_act, by_act.index(acc_of["md", n]) + 1)
                for t in range(TOK):
                    link(eng, dve.tensor_tensor(stage[:, t, :], ps[:, banks(a) + t, :], stage[:, t, :], ALU.mult))
                    part = merged[:, t, n * CH:(n + 1) * CH]
                    link(eng, dve.tensor_tensor(part, part, stage[:, t, :], ALU.add))
                dve.memset(gain_tmp[:, 0:1], 0.0).then_inc(acc_read_dve, 1)
            return run

        def dve_m_lo(n):
            def run(eng):
                eng.wait_ge(m_hi_ready, n + 1)
                dve.tensor_tensor(m_lo[:, 4 * n:4 * n + 4, :].rearrange("p (b k) s -> p b (k s)", b=2), ps[:, 4:6, :],
                                  m_hi[:, 4 * n:4 * n + 4, :].rearrange("p (b k) s -> p b (k s)", b=2).bitcast(F32),
                                  ALU.subtract).then_inc(m_lo_ready, 1)
            return run

        def add_rows(eng, src, cc, t, fresh, last, signal):
            if fresh:
                ins = dve.tensor_scalar(ada_acc[:, t, :], src, cc, None, ALU.mult)
            else:
                eng.wait_ge(*last)
                ins = dve.scalar_tensor_tensor(out=ada_acc[:, t, :], in0=src, scalar=cc, in1=ada_acc[:, t, :],
                                               op0=ALU.mult, op1=ALU.add)
            ins.then_inc(signal, 1)

        def gate_part(k):
            def run(eng):
                n, i = k // (KT // 2), k % (KT // 2)
                eng.wait_ge(gate_in[k % 2], 16 * (k // 2 + 1))
                if i == 0 and n >= 1:
                    eng.wait_ge(gate_summed, n)
                add_rows(eng, gate_ring[:, k % 2, 0:CH], cols[:, V_C + 2 * i:V_C + 2 * i + 1], 0, i == 0,
                         (gate_used, k), gate_used)
            return run

        def join_gate(n):
            def run(eng):
                eng.wait_ge(gate_used, (n + 1) * (KT // 2))
                eng.wait_ge(gate_used_pool, (n + 1) * (KT // 2))
                dve.tensor_tensor(ada_acc[:, 0, :], ada_acc[:, 0, :], ada_acc[:, 1, :], ALU.add).then_inc(gate_joined, 1)
            return run

        def gate_finish(n):
            def run(eng):
                eng.wait_ge(gate_summed, n + 1)
                eng.wait_ge(bias_in, 32 * (n + 1))
                link(eng, dve.tensor_tensor(tmp[:, :], ps[:, 6, :], bias_gain[:, 0, :], ALU.add))
                dve.tensor_tensor(post_gain[:, n * CH:(n + 1) * CH], tmp[:, :], bias_gain[:, 1, :],
                                  ALU.mult).then_inc(gg_ready, 1)
                eng.wait_ge(gg_ready, n + 1)
            return run

        def y_gain(n, tiles):
            def run(eng):
                a = acc_of["wout", n]
                eng.wait_ge(gg_ready, n + 1)
                if n == 0:
                    eng.wait_ge(piece_used, last_piece("md", 3) + 1)
                for t in tiles:
                    eng.wait_ge(y_squared[t], n + 1)
                    ins = dve.tensor_tensor(yg[:, t, n * CH:(n + 1) * CH], ps[:, banks(a) + t, :],
                                            post_gain[:, n * CH:(n + 1) * CH], ALU.mult)
                    ins.then_inc(yg_ready, 1)
                    if n == 3:
                        dve.tensor_reduce(sumsq[:, R_Y, t:t + 1], y_sq[:, t, :], AX_X, ALU.add).then_inc(y_sums, 1)
            return run

        dve_after[PH1 + 4].append(q_rope(0))
        dve_after[PH1 + 5].append(q_rope(1))
        dve_after[PH1 + 4].append(scale_ckv)
        dve_after[PH1 + 6].append(kr_rope)
        seen = set()
        for v, visit in enumerate(VISITS):
            if visit[1] in seen:
                dve_after[visit_end[v] + 2].append(add_early(v))
            seen.add(visit[1])
        for a in by_dve:
            job = pieces[start[a]][1:3]
            if job[0] in ("vd", "gate"):
                dve_after[end[a] + 3].append(add_late(job))
        dve_after[group_at[G_CKV][1]].append(dve_ckv_lo)
        for h in range(HEADS):
            s, t, v, g = mla_at[h]
            dve_after[s + 4].append(mla_max(h))
            dve_after[v + 4].append(mla_out(h))
            dve_after[g + 4].append(dve_o_lo(h))
            s, t, v, g = diff_at[h]
            dve_after[s + 4].append(diff_scores(h))
            dve_after[s + 8].append(diff_weights(h))
            dve_after[v + 4].append(head_squares(h))
            dve_after[v + 5].append(diff_out(h))
            dve_after[g + 4].append(dve_o_lo(HEADS + h))
        for n in range(4):
            dve_after[last_piece("wom", n) + 3].append(merge_mla(n))
            dve_after[last_piece("wod", n) + 3].append(merge_diff(n))
            dve_after[merge_at[n] + 4].append(dve_m_lo(n))
            dve_after[gate_end[n] + 1].append(join_gate(n))
            dve_after[gate_sum_at[n] + 4].append(gate_finish(n))
        for n in range(3):
            dve_after[min(last_piece("wout", n) + 3, NP - 1)].append(y_gain(n, range(TOK)))

        for p, parts in gate_parts_at.items():
            for k in parts:
                dve_after[p].append(gate_part(k))

        @block.vector
        def _(eng):
            eng.wait_ge(x_in[1], 16)
            dve.scalar_tensor_tensor(out=xnT[:, KT // 2:KT, :].rearrange("p k s -> p (k s)"), in0=x_tok[:, 1, :],
                                     scalar=1.0, in1=x_tok[:, 1, :], op0=ALU.mult, op1=ALU.mult,
                                     accum_out=sumsq[:, R_X, 1:2]).then_inc(x_sq, 1)
            eng.wait_ge(cols_ready, 1)
            link(eng, dve.tensor_scalar(cols[:, NVEC:NVEC + 1], cols[:, V_GSUB:V_GSUB + 1], 1.0 - LAMBDA_INIT, None,
                                        ALU.mult))

            def ada_part(j, q):
                n = j * (KT // 2) + q
                if q == 0 and j >= 1:
                    eng.wait_ge(ada_summed, j)
                eng.wait_ge(ada_in[n % RING], 32 * (n // RING + 1))
                rows = [ada_ring[:, n % RING, t, :, :].rearrange("p s n -> p (s n)") for t in range(2)]
                cc = [cols[:, V_C + 2 * q + t:V_C + 2 * q + t + 1] for t in range(2)]
                if j < POOL_FROM:
                    add_rows(eng, rows[1], cc[1], 1, q == 0, (ada_odd, n), ada_odd)
                    add_rows(eng, rows[0], cc[0], 0, q == 0, (ada_used, n), ada_used)
                else:
                    add_rows(eng, rows[0], cc[0], 0, q == 0, (ada_used, n), ada_used)

            def modulation(j):
                eng.wait_ge(ada_summed, j + 1)
                k = 2 * j
                dve.tensor_tensor(mod_shift[:, k:k + 2], ps[:, 6, 0:2], cols[:, V_SHIFT + k:V_SHIFT + k + 2], ALU.add)
                link(eng, dve.scalar_tensor_tensor(out=gain_tmp[:, 0:2], in0=ps[:, 6, 2:4], scalar=1.0,
                                                   in1=cols[:, V_SCALE + k:V_SCALE + k + 2],
                                                   op0=ALU.add, op1=ALU.add))
                dve.tensor_tensor(mod_gain[:, k:k + 2], gain_tmp[:, 0:2], cols[:, V_GPRE + k:V_GPRE + k + 2],
                                  ALU.mult).then_inc(mod_ready, 1)

            def make_h_lo(j):
                eng.wait_ge(mod_ready, j + 1)
                eng.wait_ge(xT_copied, KT // 2)
                if j >= 1:
                    eng.wait_ge(h_lo_ready, j)
                for b in range(2):
                    k = 2 * j + b
                    ins = dve.tensor_scalar(stage[:, 0, b * SEQ:(b + 1) * SEQ], xnT[:, k, :], mod_gain[:, k:k + 1],
                                            mod_shift[:, k:k + 1], ALU.mult, ALU.add)
                link(eng, ins)
                eng.wait_ge(h_hi_ready, j + 1)
                dve.tensor_tensor(h_lo[:, 2 * j:2 * j + 2, :].rearrange("p k s -> p (k s)"), stage[:, 0, :],
                                  h_hi[:, 2 * j:2 * j + 2, :].rearrange("p k s -> p (k s)").bitcast(F32),
                                  ALU.subtract).then_inc(h_lo_ready, 1)

            def angles():
                eng.wait_ge(pos_in, 32)
                eng.wait_ge(consts, 3)
                link(eng, dve.tensor_copy(pos_qf[:, :], pos_q[:, :]))
                ang, k_, r_, s_, c_ = (angle[:, i, :] for i in range(5))
                for t in range(TOK):
                    link(eng, dve.tensor_scalar(ang[:, t * HALF:(t + 1) * HALF], freq[:, :], pos_qf[:, t:t + 1], None,
                                                ALU.mult))

                def turns(dst, src, turn):
                    link(eng, dve.tensor_scalar(dst, src, 1.0 / turn, ROUND_MAGIC, ALU.mult, ALU.add))
                    link(eng, dve.tensor_scalar(dst, dst, ROUND_MAGIC, None, ALU.subtract))

                def less(dst, k, part, src):
                    link(eng, dve.scalar_tensor_tensor(out=dst, in0=k, scalar=-part, in1=src, op0=ALU.mult, op1=ALU.add))

                turns(k_, ang, BIG_TURN)
                less(ang, k_, BIG_PARTS[0], ang)
                less(ang, k_, BIG_PARTS[1], ang)
                link(eng, dve.tensor_scalar(r_, k_, -BIG_PARTS[2], None, ALU.mult))
                link(eng, dve.tensor_tensor(s_, ang, r_, ALU.add))
                turns(k_, s_, 2.0 * math.pi)
                less(ang, k_, TURN_PARTS[0], ang)
                less(ang, k_, TURN_PARTS[1], ang)
                link(eng, dve.tensor_tensor(ang, ang, r_, ALU.add))
                less(ang, k_, TURN_PARTS[2], ang)
                link(eng, dve.tensor_scalar(s_, ang, 3.1415925, -3.1415925, ALU.min, ALU.max))
                link(eng, dve.tensor_scalar(c_, s_, -1.0, None, ALU.mult))
                link(eng, dve.tensor_tensor(c_, c_, s_, ALU.max))
                link(eng, dve.tensor_scalar(c_, c_, -1.0, math.pi / 2, ALU.mult, ALU.add))
                dve.memset(gain_tmp[:, 0:1], 0.0).then_inc(angles_ready, 1)
                eng.wait_ge(lam_ld, 64)
                link(eng, dve.tensor_tensor(lam_prod[:, 0, :], lam_in[:, 0, :], lam_in[:, 1, :], ALU.mult))
                link(eng, dve.tensor_tensor(lam_prod[:, 1, :], lam_in[:, 2, :], lam_in[:, 3, :], ALU.mult))
                dve.tensor_reduce(lam_dot[:, :], lam_prod[:, :, :], AX_X, ALU.add).then_inc(lam_dots, 1)

            def distances():
                eng.wait_ge(consts, 6)
                link(eng, dve.tensor_copy(tmp[:, 0:SEQ], pos_row[:, :]))
                for lo, t, n in ((0, 0, P), (P, 1, SEQ)):
                    d_, n_ = dist[:, lo:lo + n], tmp[:, SEQ:SEQ + n]
                    link(eng, dve.tensor_scalar(d_, tmp[:, 0:n], pos_qf[:, t:t + 1], None, ALU.subtract))
                    link(eng, dve.tensor_scalar(n_, d_, -1.0, None, ALU.mult))
                    link(eng, dve.tensor_tensor(d_, d_, n_, ALU.max))
                for lo in (0, SEQ):
                    link(eng, dve.tensor_tensor(dist[:, lo:lo + P], dist[:, lo:lo + P], causal_far[:, :], ALU.add))
                eng.wait_ge(lam_exps, 1)
                link(eng, dve.scalar_tensor_tensor(out=lam[:, :], in0=lam_exp[:, 0:1], scalar=LAMBDA_INIT,
                                                   in1=lam_exp[:, 1:2], op0=ALU.add, op1=ALU.subtract))

            eng.wait_ge(rstd_ready, 1)
            for t in range(TOK):
                dve.tensor_scalar(x_diag[:, t, :], ident[:, :], rstd[:, R_X, t:t + 1], None, ALU.mult).then_inc(xn_ready, 1)
            for q in range(KT // 2):
                ada_part(0, q)
            for p, (a, kind, n, i, first, last) in enumerate(pieces):
                for j, q in ada_before.get(p, ()):
                    ada_part(j, q)
                eng.wait_ge(hi_done, p + 1)
                dve.tensor_tensor(w_lo[:, p % RING, :], w_raw[:, p % RING, :],
                                  w_hi[:, p % RING, :].bitcast(F32), ALU.subtract).then_inc(lo_done, 1)
                if p == first_part[3][1]:
                    angles()
                if p == first_part[4][1]:
                    distances()
                for work in dve_after[p]:
                    work(eng)
                if p in mod_after:
                    modulation(mod_after[p])
                if p in h_after:
                    make_h_lo(h_after[p])
            eng.wait_ge(x_again_in, 16 * TOK)
            for t in range(TOK):
                y_gain(3, [t])(eng)
                eng.wait_ge(yg_ready, 3 * TOK + t + 1)
                eng.wait_ge(y_root, t + 1)
                for tile, part in OUT_PARTS:
                    if tile == t:
                        dve.scalar_tensor_tensor(out=yg[:, t, part], in0=yg[:, t, part], scalar=rstd[:, R_Y, t:t + 1],
                                                 in1=x_again[:, t, part], op0=ALU.mult,
                                                 op1=ALU.add).then_inc(out_ready, 1)

        @block.tensor
        def _(pe):
            mm = nc.tensor.matmul
            tr = nc.tensor.transpose

            sum_before = {first_part[j][-1]: j + 1 for j in range(KT // 2 - 1)}

            def ada_sum(j):
                pe.wait_ge(ada_used, (j + 1) * (KT // 2))
                if pool_parts(j):
                    pe.wait_ge(ada_used_pool, pool_parts(j))
                if j == 0:
                    pe.wait_ge(xT_copied, KT // 2)
                else:
                    pe.wait_ge(mod_ready, j)
                visits = sum(visit[0] < j for visit in VISITS)
                if visits:
                    pe.wait_ge(early_read, visits)
                for b in range(4):
                    for t in range(2):
                        ins = mm(ps[:, 6, b:b + 1], lhsT=ada_acc[:, t, b * P:(b + 1) * P], rhs=ones[:, 0:1],
                                 start=t == 0, stop=t == 1)
                ins.then_inc(ada_summed, 1)

            def group(g):
                bank = group_bank(g)
                if g == G_QN:
                    pe.wait_ge(acc_read_act, 3)
                    pe.wait_ge(early_read, len(VISITS))
                if g == G_QN + 3:
                    pe.wait_ge(kr_ready, 1)
                if g == G_QR:
                    pe.wait_ge(lo_done, PH1 + 6 + 1)
                if g == G_CKV:
                    pe.wait_ge(ckv_scaled, 1)
                if g == G_KR:
                    pe.wait_ge(lo_done, PH1 + 7 + 1)
                if G_KN <= g < G_D:
                    pe.wait_ge(acc_read_act, by_act.index(acc_of["ukv", g - G_KN]) + 1)
                if g >= G_D:
                    kind, n = (("qd", 0), ("qd", 1), ("kd", 0), ("kd", 1))[(g - G_D) // 2]
                    pe.wait_ge(acc_read_act, by_act.index(acc_of[kind, n]) + 1)
                if g >= 4:
                    pe.wait_ge(tr_copied, g - 3 if g < G_KN else g)
                for b in range(2):
                    if g == G_KR and b:
                        break
                    for t in range(TOK):
                        if g < G_CKV:
                            src = q_tok[:, t, (2 * g + b) * QH:(2 * g + b) * QH + NOPE]
                        elif G_QR <= g < G_KR:
                            k = 2 * (2 * (g - G_QR) + b)
                            src = qr_tok[:, t, k:k + 2, :].rearrange("p h d -> p (h d)")
                        elif g < G_QR:
                            k = 2 * (g - G_CKV) + b
                            src = stage[:, t, k * P:(k + 1) * P]
                        elif g == G_KR:
                            src = kr_dup[:, t, :]
                        elif g < G_D:
                            col = (g - G_KN) % 2 * 256 + b * P
                            src = stage[:, t, col:col + P]
                        else:
                            k = 2 * ((g - G_D) % 2) + b
                            src = stage[:, t, k * P:(k + 1) * P]
                        ins = tr(ps[:, bank, b * SEQ + t * P:b * SEQ + (t + 1) * P], src, ident[:, :])
                ins.then_inc(tr_made, 1)

            def mla_scores(h):
                pe.wait_ge(tr_copied, G_KN + h // 2 + 1)
                if h >= 1:
                    pe.wait_ge(exps_done, h)
                r = ROPE * (h % 2)
                for t, (lo, keys) in enumerate(((0, P), (P, SEQ))):
                    q = slice(t * P, (t + 1) * P)
                    o = ps[:, 4, lo:lo + keys]
                    mm(o, lhsT=qnT[:, h, q], rhs=knT[:, h, 0:keys], start=True, stop=False)
                    mm(o, lhsT=qrT[r:r + ROPE, h // 2, q], rhs=krT[r:r + ROPE, 0:keys], start=False, stop=False)
                    ins = mm(ps[:, 4, lo + keys - P:lo + keys], lhsT=ident_b[:, :], rhs=causal_b[:, :],
                             start=False, stop=True)
                ins.then_inc(scores_ready, 1)

            def diff_scores_pe(h):
                if h == 0:
                    pe.wait_ge(tr_copied, N_GROUPS)
                else:
                    pe.wait_ge(scores_read, h)
                for w in range(2):
                    for t, (lo, keys) in enumerate(((0, P), (P, SEQ))):
                        ins = mm(ps[:, 4 + w, lo:lo + keys], lhsT=qdT[w * DQK:(w + 1) * DQK, h, t * P:(t + 1) * P],
                                 rhs=kdT[w * DQK:(w + 1) * DQK, h, 0:keys], start=True, stop=True)
                ins.then_inc(scores_ready, 1)

            def transpose_probs(m):
                if m < HEADS:
                    pe.wait_ge(exps_done, m + 1)
                else:
                    pe.wait_ge(weights_ready, m - HEADS + 1)
                if m >= 1:
                    pe.wait_ge(pT_copied, m)
                sums = sum(place < (mla_at + diff_at)[m][1] for place in gate_sum_at)
                if sums:
                    pe.wait_ge(gg_ready, sums)
                for k in range(3):
                    ins = tr(ps[:, 6, k * P:(k + 1) * P], probs[:, m % 2, 0, k * P:(k + 1) * P], ident[:, :])
                ins.then_inc(pT_made, 1)

            def values(m):
                pe.wait_ge(pT_copied, m + 1)
                if m >= 1:
                    pe.wait_ge(o_gated_ready, m)
                    pe.wait_ge(o_lo_ready, m)
                if m == HEADS:
                    pe.wait_ge(acc_read_dve, dve_reads("vd", 1))
                h = m % HEADS
                v = ((lambda t: v_mla[:, t, h, :]) if m < HEADS else (lambda t: v_diff[:, t, h * P:(h + 1) * P]))
                mm(ps[:, 7, 0:P], lhsT=probsT[:, 0:P], rhs=v(0), start=True, stop=True)
                mm(ps[:, 7, P:2 * P], lhsT=probsT[:, P:2 * P], rhs=v(0), start=True, stop=False)
                mm(ps[:, 7, P:2 * P], lhsT=probsT[:, 2 * P:3 * P], rhs=v(1), start=False, stop=True).then_inc(pv_done, 1)

            def transpose_out(m):
                pe.wait_ge(o_gated_ready, m + 1)
                if m >= 1:
                    pe.wait_ge(o_lo_ready, m)
                for t in range(TOK):
                    ins = tr(ps[:, 7, SEQ + t * P:SEQ + (t + 1) * P], o_gated[:, t, :], ident[:, :])
                ins.then_inc(oT_made, 1)

            def transpose_merged(n):
                pe.wait_ge(acc_read_dve, dve_reads("wod", n))
                if n >= 1:
                    pe.wait_ge(m_lo_ready, n)
                for b in range(4):
                    for t in range(TOK):
                        ins = tr(ps[:, 4 + b // 2, b % 2 * SEQ + t * P:b % 2 * SEQ + (t + 1) * P],
                                 merged[:, t, n * CH + b * P:n * CH + (b + 1) * P], ident[:, :])
                ins.then_inc(mT_made, 1)

            def gate_sum(n):
                pe.wait_ge(gate_joined, n + 1)
                if n >= 1:
                    pe.wait_ge(gg_ready, n)
                pe.wait_ge(pT_copied, HEADS + sum(gate_sum_at[n] > at[1] for at in diff_at))
                mm(ps[:, 6, :], lhsT=ones[:, :], rhs=ada_acc[:, 0, :], start=True, stop=True).then_inc(gate_summed, 1)

            def turn_kr():
                pe.wait_ge(acc_read_act, by_act.index(acc_of["kr", 0]) + 1)
                pe.wait_ge(early_read, len(VISITS))
                for t in range(TOK):
                    ins = tr(ps[:, 7, t * ROPE:(t + 1) * ROPE], kr_raw[0:ROPE, t * P:(t + 1) * P], ident[0:ROPE, 0:ROPE])
                ins.then_inc(kr_turned, 1)

            pe_after[PH1 + 2].append(turn_kr)
            for g in range(N_GROUPS):
                pe_after[group_at[g][0]].append(lambda g=g: group(g))
            for h in range(HEADS):
                for m, place, scores in ((h, mla_at[h], mla_scores), (HEADS + h, diff_at[h], diff_scores_pe)):
                    pe_after[place[0]].append(lambda h=h, f=scores: f(h))
                    pe_after[place[1]].append(lambda m=m: transpose_probs(m))
                    pe_after[place[2]].append(lambda m=m: values(m))
                    pe_after[place[3]].append(lambda m=m: transpose_out(m))
            for n in range(4):
                pe_after[merge_at[n]].append(lambda n=n: transpose_merged(n))
                pe_after[gate_sum_at[n]].append(lambda n=n: gate_sum(n))

            pe.wait_ge(consts, 2)
            pe.wait_ge(vec_in, 16 * 6)
            tr(ps[:, 7, 0:NVEC], vec_rows[0:NVEC, :], ident[0:NVEC, 0:NVEC]).then_inc(cols_T, 1)
            pe.wait_ge(xn_ready, TOK)
            for g in range(KT // 2):
                if g == 1:
                    pe.wait_ge(cols_ready, 1)
                if g >= 2:
                    pe.wait_ge(xT_copied, g - 1)
                for b in range(2):
                    for t in range(TOK):
                        k = 2 * g + b
                        ins = mm(ps[:, 6 + g % 2, b * SEQ + t * P:b * SEQ + (t + 1) * P],
                                 lhsT=x_tok[:, t, k * P:(k + 1) * P], rhs=x_diag[:, t, :], start=True, stop=True)
                ins.then_inc(xT_made, 1)
            ada_sum(0)
            for p, (a, kind, n, i, first, last) in enumerate(pieces[:NP - LAST_GROUP]):
                if p in sum_before:
                    ada_sum(sum_before[p])
                if kind == "q" and n == 0:
                    pe.wait_ge(h_lo_ready, i + 1)
                if kind == "early":
                    pe.wait_ge(h_lo_ready, i + 1)
                if kind == "early" and first:
                    pe.wait_ge(mod_ready, VISITS[n][0] + 1)
                    if n:
                        pe.wait_ge(early_read, n)
                if kind == "ukv" and n == 0 and first:
                    pe.wait_ge(ckv_lo, 2)
                if kind == "wom" and n == 0 and first:
                    pe.wait_ge(o_lo_ready, HEADS)
                if kind == "wod" and n == 0 and first:
                    pe.wait_ge(o_lo_ready, 2 * HEADS)
                if kind == "wout" and n == 0:
                    pe.wait_ge(m_lo_ready, i // 2 + 1)
                if first and a is not None and a >= 3:
                    wait_acc_read(pe, {3: 0, 4: 1}.get(a, a - 2))
                pe.wait_ge(lo_done, p + 1)
                b0 = banks(a)
                wide, tiles = CH, 2
                s_hi, s_lo = {"ukv": (ckvT_hi, ckvT_lo), "wom": (o_hi, o_lo), "wod": (o_hi, o_lo),
                              "wout": (m_hi, m_lo)}.get(kind, (h_hi, h_lo))
                if kind == "kr":
                    o = ps[0:ROPE, b0, 0:SEQ]
                    for k in range(KT):
                        hi, lo = (w[:, p % RING, k * ROPE:(k + 1) * ROPE] for w in (w_hi, w_lo))
                        mm(o, lhsT=hi, rhs=h_hi[:, k, :], start=k == 0, stop=False)
                        mm(o, lhsT=lo, rhs=h_hi[:, k, :], start=False, stop=False)
                        ins = mm(o, lhsT=hi, rhs=h_lo[:, k, :], start=False, stop=k == KT - 1)
                    tiles = 0
                order = [(r, t) for r in range(tiles) for t in range(TOK)]
                if kind == "wout" and last:
                    order.sort(key=lambda rt: rt[1])
                for r, t in order:
                    k = 2 * i + r + (HEADS if kind == "wod" else 0)
                    hi = w_hi[:, p % RING, r * wide:(r + 1) * wide]
                    lo = w_lo[:, p % RING, r * wide:(r + 1) * wide]
                    o = ps[:, b0 + t, 0:wide]
                    q = slice(t * P, (t + 1) * P)
                    mm(o, lhsT=s_hi[:, k, q], rhs=hi, start=first and r == 0, stop=False)
                    mm(o, lhsT=s_hi[:, k, q], rhs=lo, start=False, stop=False)
                    ins = mm(o, lhsT=s_lo[:, k, q], rhs=hi, start=False, stop=last and r == tiles - 1)
                    if kind == "wout" and last and (r, t) == (tiles - 1, 0):
                        ins.then_inc(y_made, 1)
                ins.then_inc(piece_used, 1)
                for work in pe_after[p]:
                    work()
            tail = list(range(NP - LAST_GROUP, NP))
            b0 = banks(pieces[-1][0])
            for t in range(TOK):
                q = slice(t * P, (t + 1) * P)
                for p in tail:
                    pe.wait_ge(lo_done, p + 1)
                    for r in range(2):
                        k = 2 * pieces[p][3] + r
                        hi, lo = (w[:, p % RING, r * CH:(r + 1) * CH] for w in (w_hi, w_lo))
                        mm(ps[:, b0 + t, :], lhsT=m_hi[:, k, q], rhs=hi, start=False, stop=False)
                        mm(ps[:, b0 + t, :], lhsT=m_hi[:, k, q], rhs=lo, start=False, stop=False)
                        ins = mm(ps[:, b0 + t, :], lhsT=m_lo[:, k, q], rhs=hi, start=False, stop=p == NP - 1 and r == 1)
                    if t == TOK - 1:
                        ins.then_inc(piece_used, 1)
                    elif p == NP - 1:
                        ins.then_inc(y_made, 1)


_INS = ["x", "c", "positions", "w_ada", "b_ada", "g_pre", "w_in", "g_kv", "w_ukv",
        "lambda_q1", "lambda_k1", "lambda_q2", "lambda_k2", "g_subln",
        "w_o_mla", "w_o_diff", "w_out", "g_post"]


def kernel(**inputs):
    import numpy as _np
    import concourse.bacc as _bacc
    from concourse import mybir as _mybir
    from concourse.bass_utils import run_bass_kernel_spmd as _run

    nc = _bacc.Bacc("TRN2", target_bir_lowering=False, num_devices=1)
    arrays, args = {}, []
    for name in _INS:
        a = _np.ascontiguousarray(inputs[name])
        arrays[f"in_{name}"] = a
        args.append(nc.dram_tensor(f"in_{name}", a.shape, _mybir.dt.from_np(a.dtype), kind="ExternalInput").ap())
    shape = (1, 256, 2048)
    args.append(nc.dram_tensor("out", shape, _mybir.dt.float32, kind="ExternalOutput").ap())
    hybrid_block(nc, *args)
    r = _run(nc, [arrays], core_ids=[0])
    return r.results[0]["out"]
```
